# Optimizing a Trainium2 kernel written in Bass

```python
import jax, jax.numpy as jnp
from jax import lax
import numpy as np

D_MODEL = 1024
BATCH = 1
SEQ = 256
DEPTH = 2

MEM_LEN = 256
EPS = 1e-6
GLA_HEADS = 4
GLA_KEY = D_MODEL // 2
GLA_VAL = D_MODEL
GLA_RANK = 16
GLA_GATE_NORM = 16.0
GLA_LOG_DECAY_MIN = -1.0
GLA_CHUNK = 64
M_HEADS = 4
M_KEY = D_MODEL // 2
M_VAL = D_MODEL
M_CHUNK = 64
CONV_W = 4
X_HEADS = 4
FFN_DIM = 64 * ((8 * D_MODEL // 3 + 63) // 64)
N_EXPERTS = 8
TOP_K = 2
EXPERT_DIM = 7 * D_MODEL // 2
N_DENSE = (DEPTH + 1) // 2
N_MOE = DEPTH // 2
IN_SPLITS = (GLA_KEY, GLA_KEY, GLA_VAL, GLA_RANK, GLA_VAL,
             M_KEY, M_KEY, M_VAL, M_HEADS, M_HEADS, M_VAL,
             D_MODEL, D_MODEL)
N_IN = sum(IN_SPLITS)

kernel_name = 'hybrid_gla_mlstm_xattn_moe_block'

def rms_norm(x, g):
    xf = x.astype(jnp.float32)
    y = xf * lax.rsqrt(jnp.mean(xf * xf, axis=-1, keepdims=True) + EPS)
    return (y * g.astype(jnp.float32)).astype(x.dtype)

def _heads(t, n_heads):
    return t.reshape(t.shape[0], t.shape[1], n_heads, -1)

def _head_rms_norm(o, g):
    y = o * lax.rsqrt(jnp.mean(o * o, axis=-1, keepdims=True) + EPS)
    return y.reshape(o.shape[0], o.shape[1], -1) * g.astype(jnp.float32)

def _causal_conv(t, w):
    k_w = w.shape[0]
    s = t.shape[1]
    tp = jnp.pad(t, ((0, 0), (k_w - 1, 0), (0, 0)))
    return sum(tp[:, j:j + s] * w[j] for j in range(k_w))

def gla_chunked(q, k, v, log_a):
    f32 = jnp.float32
    b_, s_, h_, dk = q.shape
    dv = v.shape[-1]
    c_ = GLA_CHUNK
    n_ = s_ // c_
    q = q.astype(f32).reshape(b_, n_, c_, h_, dk) * dk ** -0.5
    k = k.astype(f32).reshape(b_, n_, c_, h_, dk)
    v = v.astype(f32).reshape(b_, n_, c_, h_, dv)
    cum = jnp.cumsum(log_a.astype(f32).reshape(b_, n_, c_, h_, dk), axis=2)
    q_dec = q * jnp.exp(cum)
    scores = jnp.einsum('bnthd,bnshd->bnhts', q_dec, k * jnp.exp(-cum))
    causal = jnp.tril(jnp.ones((c_, c_), dtype=bool))
    scores = jnp.where(causal, scores, 0.0)
    o_intra = jnp.einsum('bnhts,bnshv->bnthv', scores, v)
    cum_last = cum[:, :, -1]
    k_end = k * jnp.exp(cum_last[:, :, None] - cum)
    d_state = jnp.einsum('bnshd,bnshv->nbhdv', k_end, v)
    decay = jnp.moveaxis(jnp.exp(cum_last), 1, 0)

    def step(state, inp):
        a, ds = inp
        return a[..., None] * state + ds, state

    _, s_prev = lax.scan(step, jnp.zeros((b_, h_, dk, dv), f32), (decay, d_state))
    o_inter = jnp.einsum('bnthd,nbhdv->bnthv', q_dec, s_prev)
    return (o_intra + o_inter).reshape(b_, s_, h_, dv)

def mlstm_chunked(q, k, v, log_i, log_f):
    f32 = jnp.float32
    b_, s_, h_, dk = q.shape
    dv = v.shape[-1]
    c_ = M_CHUNK
    n_ = s_ // c_
    q = q.astype(f32).reshape(b_, n_, c_, h_, dk) * dk ** -0.5
    k = k.astype(f32).reshape(b_, n_, c_, h_, dk)
    v = v.astype(f32).reshape(b_, n_, c_, h_, dv)
    li = log_i.reshape(b_, n_, c_, h_)
    g = jnp.cumsum(log_f.reshape(b_, n_, c_, h_), axis=2)
    causal = jnp.tril(jnp.ones((c_, c_), dtype=bool))
    dmat = g[:, :, :, None, :] - g[:, :, None, :, :] + li[:, :, None, :, :]
    dmat = jnp.where(causal[:, :, None], dmat, -jnp.inf)
    m_intra = jnp.max(dmat, axis=3)
    w_ts = jnp.exp(dmat - m_intra[:, :, :, None, :]) * jnp.einsum('bnthd,bnshd->bntsh', q, k)
    num_intra = jnp.einsum('bntsh,bnshv->bnthv', w_ts, v)
    den_intra = jnp.sum(w_ts, axis=3)
    g_last = g[:, :, -1]
    e = g_last[:, :, None] - g + li
    m_loc = jnp.max(e, axis=2)
    w_s = jnp.exp(e - m_loc[:, :, None])
    kw = k * w_s[..., None]
    d_c = jnp.einsum('bnshd,bnshv->nbhdv', kw, v)
    d_n = jnp.sum(kw, axis=2).transpose(1, 0, 2, 3)

    def step(carry, inp):
        c_st, n_st, m_st = carry
        gl, ml, dc, dn = inp
        m_new = jnp.maximum(gl + m_st, ml)
        a = jnp.exp(gl + m_st - m_new)
        bb = jnp.exp(ml - m_new)
        c_new = a[..., None, None] * c_st + bb[..., None, None] * dc
        n_new = a[..., None] * n_st + bb[..., None] * dn
        return (c_new, n_new, m_new), (c_st, n_st, m_st)

    init = (jnp.zeros((b_, h_, dk, dv), f32), jnp.zeros((b_, h_, dk), f32), jnp.zeros((b_, h_), f32))
    _, (c_prev, n_prev, m_prev) = lax.scan(
        step, init, (jnp.moveaxis(g_last, 1, 0), jnp.moveaxis(m_loc, 1, 0), d_c, d_n))
    m_inter = g + jnp.moveaxis(m_prev, 0, 1)[:, :, None]
    m_t = jnp.maximum(m_inter, m_intra)
    s_inter = jnp.exp(m_inter - m_t)
    s_intra = jnp.exp(m_intra - m_t)
    num = (s_intra[..., None] * num_intra
           + s_inter[..., None] * jnp.einsum('bnthd,nbhdv->bnthv', q, c_prev))
    den = s_intra * den_intra + s_inter * jnp.einsum('bnthd,nbhd->bnth', q, n_prev)
    h = num / jnp.maximum(jnp.abs(den), jnp.exp(-m_t))[..., None]
    return h.reshape(b_, s_, h_, dv)

def hybrid_mixer(h, w_in, gla_gk_up, gla_gk_bias, gla_norm, m_conv, m_gate_bias, m_norm,
                 gla_proj, m_proj, w_out):
    f32 = jnp.float32
    z = h @ w_in
    offsets = np.cumsum(IN_SPLITS)[:-1].tolist()
    (g_q, g_k, g_v, g_lr, g_g, m_q, m_k, m_v, m_i, m_f, m_o, a_gla, a_m) = jnp.split(z, offsets, axis=-1)
    log_a = jax.nn.log_sigmoid((g_lr @ gla_gk_up + gla_gk_bias).astype(f32)) / GLA_GATE_NORM
    log_a = jnp.maximum(log_a, GLA_LOG_DECAY_MIN)
    o_gla = gla_chunked(_heads(g_q, GLA_HEADS), _heads(g_k, GLA_HEADS),
                        _heads(g_v, GLA_HEADS), _heads(log_a, GLA_HEADS))
    o_gla = (_head_rms_norm(o_gla, gla_norm) * jax.nn.silu(g_g.astype(f32))).astype(h.dtype)
    qk = jax.nn.silu(_causal_conv(jnp.concatenate([m_q, m_k], axis=-1), m_conv))
    m_q, m_k = jnp.split(qk, 2, axis=-1)
    gates = (jnp.concatenate([m_i, m_f], axis=-1) + m_gate_bias).astype(f32)
    log_i = gates[..., :M_HEADS]
    log_f = jax.nn.log_sigmoid(gates[..., M_HEADS:])
    o_m = mlstm_chunked(_heads(m_q, M_HEADS), _heads(m_k, M_HEADS), _heads(m_v, M_HEADS), log_i, log_f)
    o_m = (_head_rms_norm(o_m, m_norm) * jax.nn.sigmoid(m_o.astype(f32))).astype(h.dtype)
    merged = jax.nn.sigmoid(a_gla) * (o_gla @ gla_proj) + jax.nn.sigmoid(a_m) * (o_m @ m_proj)
    return merged @ w_out

def cross_attention(h, mem_n, wq, wkv, wo):
    b_, s_, d_ = h.shape
    dh = d_ // X_HEADS
    q = _heads(h @ wq, X_HEADS)
    k, v = jnp.split(mem_n @ wkv, 2, axis=-1)
    k = _heads(k, X_HEADS)
    v = _heads(v, X_HEADS)
    scores = jnp.einsum('bshd,bmhd->bhsm', q, k).astype(jnp.float32) * dh ** -0.5
    p = jax.nn.softmax(scores, axis=-1).astype(v.dtype)
    o = jnp.einsum('bhsm,bmhd->bshd', p, v).reshape(b_, s_, d_)
    return o @ wo

def swiglu(h, w13, w2):
    gate, up = jnp.split(h @ w13, 2, axis=-1)
    return (jax.nn.silu(gate) * up) @ w2

def moe_swiglu(h, router, w13, w2):
    logits = (h @ router).astype(jnp.float32)
    top_val, top_idx = lax.top_k(logits, TOP_K)
    top_w = jax.nn.softmax(top_val, axis=-1)
    gate = jnp.sum(jax.nn.one_hot(top_idx, N_EXPERTS, dtype=jnp.float32) * top_w[..., None],
                   axis=-2).astype(h.dtype)
    out = jnp.zeros_like(h)
    for e in range(N_EXPERTS):
        out = out + gate[..., e:e + 1] * swiglu(h, w13[e], w2[e])
    return out

def setup_inputs(seed: int = 0) -> dict:
    key = jax.random.key(seed)
    ks = jax.random.split(key, 26)
    f32 = jnp.float32
    L = DEPTH

    def nrm(k, shape, fan_in):
        return jax.random.normal(k, shape, f32) * fan_in ** -0.5

    def gain(k, shape):
        return 1.0 + 0.02 * jax.random.normal(k, shape, f32)

    i_bias = 0.1 * jax.random.normal(ks[24], (L, M_HEADS), f32)
    f_bias = jnp.linspace(3.0, 6.0, M_HEADS, dtype=f32) + 0.1 * jax.random.normal(ks[25], (L, M_HEADS), f32)
    return {
        'x': jax.random.normal(ks[0], (BATCH, SEQ, D_MODEL), f32),
        'mem': jax.random.normal(ks[1], (BATCH, MEM_LEN, D_MODEL), f32),
        'norm_mix': gain(ks[2], (L, D_MODEL)),
        'w_in': nrm(ks[3], (L, D_MODEL, N_IN), D_MODEL),
        'gla_gk_up': nrm(ks[4], (L, GLA_RANK, GLA_KEY), GLA_RANK),
        'gla_gk_bias': 0.1 * jax.random.normal(ks[5], (L, GLA_KEY), f32),
        'gla_norm': gain(ks[6], (L, GLA_VAL)),
        'm_conv': nrm(ks[7], (L, CONV_W, 2 * M_KEY), CONV_W),
        'm_gate_bias': jnp.concatenate([i_bias, f_bias], axis=-1),
        'm_norm': gain(ks[8], (L, M_VAL)),
        'gla_proj': nrm(ks[9], (L, GLA_VAL, D_MODEL), GLA_VAL),
        'm_proj': nrm(ks[10], (L, M_VAL, D_MODEL), M_VAL),
        'w_out': nrm(ks[11], (L, D_MODEL, D_MODEL), D_MODEL),
        'norm_xattn': gain(ks[12], (L, D_MODEL)),
        'norm_mem': gain(ks[13], (L, D_MODEL)),
        'x_wq': nrm(ks[14], (L, D_MODEL, D_MODEL), D_MODEL),
        'x_wkv': nrm(ks[15], (L, D_MODEL, 2 * D_MODEL), D_MODEL),
        'x_wo': nrm(ks[16], (L, D_MODEL, D_MODEL), D_MODEL),
        'norm_ffn': gain(ks[17], (L, D_MODEL)),
        'ffn_w13': nrm(ks[18], (N_DENSE, D_MODEL, 2 * FFN_DIM), D_MODEL),
        'ffn_w2': nrm(ks[19], (N_DENSE, FFN_DIM, D_MODEL), FFN_DIM),
        'moe_router': nrm(ks[20], (N_MOE, D_MODEL, N_EXPERTS), D_MODEL),
        'moe_w13': nrm(ks[21], (N_MOE, N_EXPERTS, D_MODEL, 2 * EXPERT_DIM), D_MODEL),
        'moe_w2': nrm(ks[22], (N_MOE, N_EXPERTS, EXPERT_DIM, D_MODEL), EXPERT_DIM),
        'norm_final': gain(ks[23], (D_MODEL,)),
    }

def reference(x, mem, norm_mix, w_in, gla_gk_up, gla_gk_bias, gla_norm, m_conv, m_gate_bias, m_norm,
              gla_proj, m_proj, w_out, norm_xattn, norm_mem, x_wq, x_wkv, x_wo, norm_ffn,
              ffn_w13, ffn_w2, moe_router, moe_w13, moe_w2, norm_final):
    for l in range(DEPTH):
        h = rms_norm(x, norm_mix[l])
        x = x + hybrid_mixer(h, w_in[l], gla_gk_up[l], gla_gk_bias[l], gla_norm[l], m_conv[l],
                             m_gate_bias[l], m_norm[l], gla_proj[l], m_proj[l], w_out[l])
        h = rms_norm(x, norm_xattn[l])
        mem_n = rms_norm(mem, norm_mem[l])
        x = x + cross_attention(h, mem_n, x_wq[l], x_wkv[l], x_wo[l])
        h = rms_norm(x, norm_ffn[l])
        if l % 2 == 0:
            x = x + swiglu(h, ffn_w13[l // 2], ffn_w2[l // 2])
        else:
            x = x + moe_swiglu(h, moe_router[l // 2], moe_w13[l // 2], moe_w2[l // 2])
    return rms_norm(x, norm_final)


_drawn_inputs = setup_inputs


def setup_inputs(seed=0):
    import zlib

    import numpy as np

    out = dict(_drawn_inputs(seed))
    spreads = {}
    factors = {'norm_xattn': 5.99, 'norm_mem': 3.467, 'norm_final': 8.417, 'norm_ffn': 2.902}
    for name, (base, spread) in spreads.items():
        noise = np.random.default_rng([zlib.crc32(name.encode()), seed]).standard_normal(out[name].shape)
        drawn = base * np.exp(spread * noise) if base else spread * noise
        out[name] = __import__('jax').numpy.asarray(drawn.astype(out[name].dtype))
    for name, factor in factors.items():
        out[name] = (out[name] * factor).astype(out[name].dtype)
    return out
```

```python
import numpy as np
import concourse.bass as bass
from concourse import mybir
from concourse.alu_op_type import AluOpType as ALU
from contextlib import ExitStack

F32 = mybir.dt.float32
U32 = mybir.dt.uint32
I32 = mybir.dt.int32
ACT = mybir.ActivationFunctionType
AX = mybir.AxisListType

P = 128
S = 256
M = 256
D = 1024
TT = S // P
KC = D // P
DEPTH = 2
EPS = 1e-6
HEADS = 4
DK = 128
DV = 256
CH = 64
NCH = S // CH
RANK = 16
CONV_W = 4
FFN = 64 * ((8 * D // 3 + 63) // 64)
NE = 8
EXP = 7 * D // 2
HB = 512
DENSE_STEPS = (FFN + HB - 1) // HB
DENSE_TAIL = FFN - (DENSE_STEPS - 1) * HB
MOE_STEPS = EXP // HB
GATE_NORM = 16.0
LOG_DECAY_MIN = -1.0
QK_SCALE = DK ** -0.5
X_SCALE = (D // HEADS) ** -0.5
BIG = 1e30

OFF = {}
_at = 0
for _name, _w in (("g_q", 512), ("g_k", 512), ("g_v", D), ("g_lr", RANK), ("g_g", D), ("m_q", 512), ("m_k", 512),
                  ("m_v", D), ("m_i", HEADS), ("m_f", HEADS), ("m_o", D), ("a_gla", D), ("a_m", D)):
    OFF[_name] = _at
    _at += _w
N_IN = _at

BLOCKS = [(name, j) for name, n in (("g_q", 1), ("g_k", 1), ("g_v", 2), ("g_g", 2), ("m_q", 1), ("m_k", 1), ("m_v", 2),
                                    ("m_o", 2), ("a_gla", 2), ("a_m", 2), ("gla_proj", 2), ("m_proj", 2), ("w_out", 2),
                                    ("x_wq", 2), ("x_wk", 2), ("x_wv", 2), ("x_wo", 2)) for j in range(n)]
SLOTS = 3
assert len(BLOCKS) % SLOTS == 0
MIX_USES = len(BLOCKS) // SLOTS
DENSE_BASE = MIX_USES
LAYER_USES = MIX_USES + DENSE_STEPS
MOE_BASE = LAYER_USES + MIX_USES

GROUPS = {}


def _plan():
    def add(*name):
        GROUPS[name] = len(GROUPS)

    def turned(name):
        for j in range(4):
            add(name, j)

    add("vec", 0)
    turned("mix_t")
    add("small", 0)
    add("small", 1)
    for name, j in BLOCKS[:4]:
        add(name, j, 0)
        add(name, j, 1)
        if name == "g_k":
            add("decay", 0)
            add("decay", 1)
    for name, j in BLOCKS[4:16]:
        add(name, j, 0)
        add(name, j, 1)
    add("gate_cols", 0)
    turned("gla_t")
    for name, j in BLOCKS[16:18]:
        add(name, j, 0)
        add(name, j, 1)
    turned("m_t")
    for name, j in BLOCKS[18:20]:
        add(name, j, 0)
        add(name, j, 1)
    turned("merged_t")
    for name, j in BLOCKS[20:22]:
        add(name, j, 0)
        add(name, j, 1)
    turned("x_t")
    for name, j in BLOCKS[22:]:
        add(name, j, 0)
        add(name, j, 1)
    turned("ffn_t")


_plan()
LAST_OF_BLOCK = [GROUPS[(name, j, 1)] for name, j in BLOCKS]

VEC = {}
_at = 0
for _name, _w in (("norm_mix", 8), ("gla_gk_bias", 4), ("gla_norm", 8), ("m_conv", 32), ("m_norm", 8),
                  ("norm_xattn", 8), ("norm_mem", 8), ("norm_ffn", 8)):
    VEC[_name] = _at
    _at += _w
NVEC = _at


CONSTS = 23
VEC_DMAS = len(VEC) + 6
Q_STEPS = 3 * TT


class Steps:

    def __init__(self, eng, own):
        self.eng, self.own, self.n, self.last, self.base = eng, own, 0, None, 0

    def wait(self):
        if self.last is not None:
            self.eng.wait_ge(*self.last)

    def did(self, ins, sem=None, value=None):
        if sem is None:
            self.n += 1
            ins.then_inc(self.own, 1)
            self.last = (self.own, self.base + self.n)
        else:
            ins.then_inc(sem, 1)
            self.last = (sem, value)


def hybrid_decoder_kernel(nc, t, out):
    ctx = ExitStack()
    with ctx:
        def sb(name, shape, dt=F32):
            return ctx.enter_context(nc.sbuf_tensor("sb_" + name, shape, dt))

        def sem(name):
            return ctx.enter_context(nc.semaphore(name))

        bank = [ctx.enter_context(nc.psum_tensor(f"bank{i}", [P, 512], F32)) for i in range(8)]
        ring = sb("ring", [P, SLOTS, KC * 512])
        x = sb("x", [P, TT, D])
        xn = sb("xn", [P, TT, D])
        hT = sb("hT", [P, KC, S])
        memhT = sb("memhT", [P, KC, M])
        aT = sb("aT", [P, KC, S])
        bT = sb("bT", [P, KC, S])
        gqk = sb("gqk", [P, 2 * HEADS, S])
        gqT = gqk[:, 0:HEADS, :]
        gkT = gqk[:, HEADS:, :]
        gkeT = sb("gkeT", [P, HEADS, S])
        cum = sb("cum", [P, HEADS, S])
        e1 = sb("e1", [P, HEADS, S])
        gv = sb("gv", [P, TT, D])
        gg = sb("gg", [P, TT, D])
        cin = sb("cin", [P, KC, CONV_W - 1 + S])
        qk = sb("qk", [P, KC, S])
        mv = sb("mv", [P, TT, HEADS, DV + 1])
        mo = sb("mo", [P, TT, D])
        ag = sb("ag", [P, TT, D])
        am = sb("am", [P, TT, D])
        om = gqk[:, :, :].rearrange("p (a b) s -> p a (b s)", a=TT)
        junk = sb("junk", [P, D])
        ident = sb("ident", [P, P])
        tri = sb("tri", [P, P])
        ones = sb("ones", [P, P])
        slot_no = sb("slot_no", [P, P])
        expert_no = sb("expert_no", [P, NE])
        causal = sb("causal", [P, TT * P])
        hide = sb("hide", [P, TT * P])
        restart = sb("restart", [P, HEADS * S])
        pick = sb("pick", [HEADS, HEADS, P])
        zrow = sb("zrow", [HEADS, CH])
        zero1 = sb("zero1", [P, 1])
        lnscale = sb("lnscale", [P, 1])
        vrow = sb("vrow", [NVEC, P])
        vcol = sb("vcol", [P, NVEC])
        wsmall = sb("wsmall", [P, KC, RANK + 2 * HEADS])
        gkup = sb("gkup", [RANK, 512])
        gbias = sb("gbias", [HEADS, 2])
        lrT = sb("lrT", [RANK, S])
        sT = sb("sT", [P, TT * P])
        wT = aT[:, 0, :]
        kn = aT[:, 3, :].rearrange("p (a k) -> p a k", k=P)
        st = sb("st", [P, 3, DV + 1])
        qs = aT[:, 1, :]
        dexp = aT[:, 2, :]
        ssum = sb("ssum", [P, TT * HEADS])
        rstd = sb("rstd", [P, TT * HEADS])
        ssum2 = sb("ssum2", [P, TT])
        rstd2 = sb("rstd2", [P, TT])
        den = sb("den", [P, TT])
        rows = sb("rows", [P, S])
        mrow = sb("mrow", [HEADS, S + NCH])
        grow = bT[0:HEADS, 0:6, :]
        mst = sb("mst", [HEADS, NCH + 1])
        cols = sb("cols", [P, TT, P])
        sdec = sb("sdec", [P, HEADS, NCH])
        kT = gg[:, :, :].rearrange("p a (b c) -> p (a b) c", c=S)
        prob = e1[:, 0:TT, :]
        probT = e1[:, TT:2 * TT, :]
        mx = sb("mx", [P, TT])
        nmx = sb("nmx", [P, TT])
        rsum = sb("rsum", [P, TT])
        rinv = sb("rinv", [P, TT])
        sg = mo[:, :, 0:HB]
        hid = am[:, :, 0:HB]
        hidT = om[:, :, 0:HB].rearrange("p t (k c) -> p t k c", c=P)
        yacc = gv[:, 0, :]
        hgT = gv[:, 1, :].rearrange("p (k c) -> p k c", c=P)
        onehot = gg[:, 0, 0:TT * P].rearrange("p (t j) -> p t j", t=TT)
        gated = gg[:, 0, 256:256 + TT * P].rearrange("p (t j) -> p t j", t=TT)
        gatedT = gg[:, 0, 512:512 + S]
        gain = junk[:, :]
        rw = sb("rw", [P, KC, NE])
        logit = sb("logit", [P, TT, NE])
        top = sb("top", [P, TT, NE])
        topi = sb("topi", [P, TT, NE], U32)
        topf = sb("topf", [P, TT, NE])
        tw = sb("tw", [P, TT, 4])
        oh = sb("oh", [P, 2, NE])
        chosen = sb("chosen", [P, TT, NE])
        gates = sb("gates", [P, TT, NE])
        place = sb("place", [P, TT, NE])
        place_p = sb("place_p", [P, TT, NE])
        most = sb("most", [P, 2])
        npass_i = sb("npass_i", [P, 1], I32)

        def slot_a(s):
            return ring[:, s, :].rearrange("p (k n) -> p k n", k=KC)

        def slot_d(s):
            return ring[:, s, :].rearrange("p (k n) -> p k n", k=HB // P)

        layer_sems = []

        def lsem(name):
            layer_sems.append(sem(name))
            return layer_sems[-1]

        pe_group = lsem("pe_group")
        moved = [lsem(f"moved{b}") for b in range(4)]
        dve_own, act_own, pool_own = lsem("dve_own"), lsem("act_own"), lsem("pool_own")
        L = {n: lsem(n) for n in (
            "sq_done", "var_done", "root_done", "xn_ready", "decay_z", "decay_e", "cum_ready", "e_ready", "gla_in",
            "conv_out", "qk_ready", "row_abs", "row_ln", "row_dm", "row_exp", "rows_ready", "values_ready",
            "h_scores", "h_masked", "h_keys", "h_keys_sb", "h_dstate", "h_state", "h_out", "h_outsb",
            "h_bcast", "h_dexp_in", "h_dexp", "h_qs", "h_den", "h_sq",
            "norm_var", "norm_root", "gated_g", "gated_m", "gate_z",
            "mem_t", "x_score", "x_negmax", "x_exp", "x_prob", "x_pt", "x_pt_sb", "x_o", "x_o_sb",
            "gate_ps", "up_ps", "silu_done", "hid_ready", "hid_tr", "hidT_ready", "y_ps", "y_added",
            "logit_ps", "count_in", "top_e_in", "top_e", "count_ps", "npass_ready", "onehot_ready", "gather_ps", "gather_sb",
            "scatter_ps", "scattered", "gain_in")}
        vec_in = sem("vec_in")
        x_in = sem("x_in")
        mem_in = sem("mem_in")
        const_ready = sem("const_ready")
        last_in = sem("last_in")
        full = [sem(f"full{s}") for s in range(SLOTS)]
        layer_done = sem("layer_done")
        layer_go = sem("layer_go")
        layer_seen = sem("layer_seen")
        mem_ready = sem("mem_ready")
        mem_sq = sem("mem_sq")
        mem_var = sem("mem_var")
        mem_root = sem("mem_root")
        mem_n = sem("mem_n")
        mem_tp = sem("mem_tp")
        fin_sq, fin_var, fin_root, fin_out, out_done = sem("fin_sq"), sem("fin_var"), sem("fin_root"), sem("fin_out"), sem("out_done")
        ENGINES = 5
        dve_q, dve_p = lsem("dve_q"), lsem("dve_p")

        def group(*name):
            g = GROUPS[name]
            return bank[g % 4], moved[g % 4], g // 4 + 1

        def wait_group(eng, *name):
            eng.wait_ge(pe_group, GROUPS[name] + 1)

        def wait_moved(eng, *name):
            g = GROUPS[name]
            eng.wait_ge(moved[g % 4], g // 4 + 1)

        def source(l, name, j):
            if name in OFF:
                a = t["w_in"][l, :, OFF[name] + 512 * j:OFF[name] + 512 * (j + 1)]
            elif name == "x_wk":
                a = t["x_wkv"][l, :, 512 * j:512 * (j + 1)]
            elif name == "x_wv":
                a = t["x_wkv"][l, :, D + 512 * j:D + 512 * (j + 1)]
            else:
                a = t[name][l, :, 512 * j:512 * (j + 1)]
            return a.rearrange("(k p) n -> p k n", p=P)

        block = ctx.enter_context(nc.Block())

        def layer_end(eng, l, last=None):
            eng.drain().then_inc(layer_done, 1)
            eng.wait_ge(layer_go, 1)
            eng.sem_inc(layer_seen, 1)

        @block.sync
        def _(sp):
            sp.dma_start(x[:, :, :], t["x"][0].rearrange("(a p) d -> p a d", p=P)).then_inc(x_in, 16)

            def load(l, b):
                name, j = BLOCKS[b]
                sp.dma_start(slot_a(b % SLOTS), source(l, name, j)).then_inc(full[b % SLOTS], 16)

            for b in range(SLOTS):
                load(0, b)
            with sp.Fori(0, DEPTH) as l:
                for b in range(SLOTS, len(BLOCKS)):
                    sp.wait_ge(pe_group, LAST_OF_BLOCK[b - SLOTS] + 1)
                    load(l, b)
                n = len(BLOCKS)
                with sp.If(l == 0):
                    def dense_load(i, what):
                        w = HB if i < DENSE_STEPS - 1 else DENSE_TAIL
                        if what == "gate":
                            sp.dma_start(slot_a(0)[:, :, 0:w], t["ffn_w13"][0, :, HB * i:HB * i + w].rearrange(
                                "(k p) n -> p k n", p=P)).then_inc(full[0], 16)
                        elif what == "up":
                            sp.dma_start(slot_a(2)[:, :, 0:w], t["ffn_w13"][0, :, FFN + HB * i:FFN + HB * i + w].rearrange(
                                "(k p) n -> p k n", p=P)).then_inc(full[2], 16)
                        elif w == HB:
                            sp.dma_start(slot_d(1), t["ffn_w2"][0, HB * i:HB * i + w, :].rearrange(
                                "(k p) n -> p k n", p=P)).then_inc(full[1], 16)
                        else:
                            whole = w // P * P
                            sp.dma_start(slot_d(1)[:, 0:w // P, :], t["ffn_w2"][0, HB * i:HB * i + whole, :].rearrange(
                                "(k p) n -> p k n", p=P)).then_inc(full[1], 16)
                            sp.dma_start(slot_d(1)[0:w - whole, w // P, :],
                                         t["ffn_w2"][0, HB * i + whole:HB * i + w, :]).then_inc(full[1], 16)

                    sp.wait_ge(pe_group, LAST_OF_BLOCK[n - 3] + 1)
                    dense_load(0, "gate")
                    sp.wait_ge(pe_group, LAST_OF_BLOCK[n - 1] + 1)
                    dense_load(0, "up")
                    for i in range(1, DENSE_STEPS):
                        sp.wait_ge(L["gate_ps"], TT * i)
                        dense_load(i, "gate")
                        if i > 1:
                            sp.wait_ge(L["y_ps"], 2 * TT * (i - 1))
                        dense_load(i - 1, "down")
                        sp.wait_ge(L["up_ps"], TT * i)
                        dense_load(i, "up")
                    sp.wait_ge(L["y_ps"], 2 * TT * (DENSE_STEPS - 1))
                    dense_load(DENSE_STEPS - 1, "down")
                    sp.wait_ge(L["gate_ps"], TT * DENSE_STEPS)
                    load(1, 0)
                    sp.wait_ge(L["up_ps"], TT * DENSE_STEPS)
                    load(1, 2)
                    sp.wait_ge(L["y_ps"], 2 * TT * DENSE_STEPS)
                    load(1, 1)
                with sp.Else():
                    sp.wait_ge(L["npass_ready"], 1)
                    npass = sp.value_load(npass_i[0:1, 0:1], min_val=1, max_val=TT)
                    sp.wait_ge(pe_group, LAST_OF_BLOCK[n - 1] + 1)

                    def moe_load(e, i, what):
                        if what == "gate":
                            sp.dma_start(slot_a(0), t["moe_w13"][0, e, :, bass.ts(i, HB)].rearrange(
                                "(k p) n -> p k n", p=P)).then_inc(full[0], 16)
                        elif what == "up":
                            sp.dma_start(slot_a(2), t["moe_w13"][0, e, :, EXP:2 * EXP][:, bass.ts(i, HB)].rearrange(
                                "(k p) n -> p k n", p=P)).then_inc(full[2], 16)
                        else:
                            sp.dma_start(slot_d(1), t["moe_w2"][0, e, bass.ts(i, HB), :].rearrange(
                                "(k p) n -> p k n", p=P)).then_inc(full[1], 16)

                    with sp.Fori(0, npass) as ps:
                        with sp.Fori(0, NE) as e:
                            q = ps * NE + e
                            sp.wait_ge(L["gate_ps"], q * MOE_STEPS + 1)
                            moe_load(e, 0, "gate")
                            sp.wait_ge(L["up_ps"], q * MOE_STEPS + 1)
                            moe_load(e, 0, "up")
                            with sp.Fori(1, MOE_STEPS) as i:
                                k = q * MOE_STEPS + i
                                sp.wait_ge(L["gate_ps"], k + 1)
                                moe_load(e, i, "gate")
                                sp.wait_ge(L["y_ps"], 2 * (k - 1) + 1)
                                moe_load(e, i - 1, "down")
                                sp.wait_ge(L["up_ps"], k + 1)
                                moe_load(e, i, "up")
                            sp.wait_ge(L["y_ps"], 2 * (q * MOE_STEPS + MOE_STEPS - 1) + 1)
                            moe_load(e, MOE_STEPS - 1, "down")
                sp.nop()
                layer_end(sp, l)
            sp.wait_ge(fin_out, 2)
            sp.dma_start(out[0].rearrange("(a p) d -> p a d", p=P), xn[:, :, :]).then_inc(out_done, 16)
            sp.wait_ge(out_done, 16)

        @block.gpsimd
        def _(pool):
            n = [0]

            def did(ins):
                n[0] += 1
                ins.then_inc(const_ready, 1)

            def ordered():
                pool.wait_ge(const_ready, n[0])

            pool.dma_start(xn[:, :, :], t["mem"][0].rearrange("(a p) d -> p a d", p=P)).then_inc(mem_in, 16)
            did(pool.memset(ident[:, :], 0.0))
            did(pool.memset(tri[:, :], 1.0))
            did(pool.memset(ones[:, :], 1.0))
            did(pool.memset(causal[:, :], 1.0))
            did(pool.memset(restart[:, :], 1.0))
            did(pool.memset(pick[:, :, :], 0.0))
            did(pool.memset(zrow[:, :], 0.0))
            did(pool.memset(zero1[:, :], 0.0))
            did(pool.memset(lnscale[:, :], float(np.log(QK_SCALE))))
            did(pool.memset(rows[:, :], 0.0))
            did(pool.memset(sT[:, :], 0.0))
            did(pool.memset(cin[:, :, 0:CONV_W - 1], 0.0))
            did(pool.memset(mv[:, :, :, DV:DV + 1], 1.0))
            did(pool.memset(mst[:, 0:1], 0.0))
            did(pool.iota(slot_no[:, :], [[1, P]], base=0, channel_multiplier=0, allow_small_or_imprecise_dtypes=True))
            did(pool.iota(expert_no[:, :], [[1, NE]], base=0, channel_multiplier=0, allow_small_or_imprecise_dtypes=True))
            ordered()
            did(pool.affine_select(out=ident[:, :], in_=ident[:, :], compare_op=ALU.not_equal, fill=1.0, base=0,
                                   pattern=[[-1, P]], channel_multiplier=1))
            did(pool.affine_select(out=tri[:, :], in_=tri[:, :], compare_op=ALU.is_gt, fill=0.0, base=0,
                                   pattern=[[1, P]], channel_multiplier=-1))
            did(pool.affine_select(out=causal[:, :].rearrange("p (a t) -> p a t", a=TT),
                                   in_=causal[:, :].rearrange("p (a t) -> p a t", a=TT), compare_op=ALU.is_ge, fill=0.0,
                                   base=0, pattern=[[0, TT], [1, P]], channel_multiplier=-1))
            ordered()
            v = causal[:, :].rearrange("p (a c t) -> p a c t", a=TT, c=2)
            did(pool.affine_select(out=v, in_=v, compare_op=ALU.is_ge, fill=0.0, base=0,
                                   pattern=[[0, TT], [-CH, 2], [0, CH]], channel_multiplier=1))
            v = restart[:, :].rearrange("p (c t) -> p c t", t=CH)
            did(pool.affine_select(out=v, in_=v, compare_op=ALU.not_equal, fill=0.0, base=0,
                                   pattern=[[0, HEADS * NCH], [1, CH]], channel_multiplier=0))
            did(pool.affine_select(out=pick[:, :, :], in_=pick[:, :, :], compare_op=ALU.not_equal, fill=1.0, base=0,
                                   pattern=[[-1, HEADS], [0, P]], channel_multiplier=1))
            ordered()
            did(pool.tensor_scalar(hide[:, :], causal[:, :], -BIG, BIG, ALU.mult, ALU.add))
            ordered()
            assert n[0] == CONSTS, n[0]

            with pool.Fori(0, DEPTH) as l:
                for name in VEC:
                    rows_of = {"m_conv": CONV_W * KC, "gla_gk_bias": HEADS}.get(name, KC)
                    src = t[name][l]
                    src = src.rearrange("j (c p) -> (j c) p", p=P) if name == "m_conv" else src.rearrange("(c p) -> c p", p=P)
                    pool.dma_start(vrow[VEC[name]:VEC[name] + rows_of, :], src).then_inc(vec_in, 16)
                pool.dma_start(wsmall[:, :, 0:RANK], t["w_in"][l, :, OFF["g_lr"]:OFF["g_lr"] + RANK].rearrange(
                    "(k p) n -> p k n", p=P)).then_inc(vec_in, 16)
                pool.dma_start(wsmall[:, :, RANK:], t["w_in"][l, :, OFF["m_i"]:OFF["m_i"] + 2 * HEADS].rearrange(
                    "(k p) n -> p k n", p=P)).then_inc(vec_in, 16)
                pool.dma_start(gkup[:, :], t["gla_gk_up"][l]).then_inc(vec_in, 16)
                for c in range(2):
                    pool.dma_start(gbias[:, c:c + 1], t["m_gate_bias"][l, c * HEADS:(c + 1) * HEADS].rearrange(
                        "(h o) -> h o", o=1)).then_inc(vec_in, 16)
                pool.dma_start(rw[:, :, :], t["moe_router"][0].rearrange("(k p) e -> p k e", p=P)).then_inc(vec_in, 16)
                pool.wait_ge(layer_done, ENGINES - 1)
                for s_ in layer_sems:
                    pool.sem_clear(s_)
                pool.sem_clear(layer_done)
                pool.sem_inc(layer_go, 1)
                pool.wait_ge(layer_seen, ENGINES - 1)
                pool.sem_clear(layer_go)
                pool.sem_clear(layer_seen)

        @block.tensor
        def _(pe):
            pe.wait_ge(const_ready, CONSTS)

            def turn_mem():
                pe.wait_ge(mem_n, 2)
                for j in range(4):
                    for k in range(2):
                        for a in range(TT):
                            ins = pe.transpose(bank[j][:, (k * TT + a) * P:(k * TT + a + 1) * P],
                                               gg[:, a, (2 * j + k) * P:(2 * j + k + 1) * P], ident[:, :])
                    ins.then_inc(mem_tp, 1)
                pe.wait_ge(mem_ready, 4)

            turn_mem()

            with pe.Fori(0, DEPTH) as l:
                def begin(*name):
                    g = GROUPS[name]
                    if g >= 4:
                        pe.wait_ge(moved[g % 4], g // 4)
                    return bank[g % 4]

                def end(ins):
                    ins.then_inc(pe_group, 1)

                def turn(name, src):
                    for j in range(4):
                        b = begin(name, j)
                        for k in range(2):
                            for a in range(TT):
                                ins = pe.transpose(b[:, (k * TT + a) * P:(k * TT + a + 1) * P],
                                                   src[:, a, (2 * j + k) * P:(2 * j + k + 1) * P], ident[:, :])
                        end(ins)

                def turned(name):
                    for j in range(4):
                        wait_moved(pe, name, j)

                def weights(b):
                    extra = 16 * l if b % SLOTS == 1 else 0
                    pe.wait_ge(full[b % SLOTS], (l * LAYER_USES + (b // SLOTS + 1)) * 16 + extra)

                def rows_out(b, src):
                    name, j = BLOCKS[b]
                    weights(b)
                    for a in range(TT):
                        ps = begin(name, j, a)
                        for k in range(KC):
                            ins = pe.matmul(ps[:, :], src[:, k, a * P:(a + 1) * P], slot_a(b % SLOTS)[:, k, :],
                                            start=(k == 0), stop=(k == KC - 1))
                        end(ins)

                def channels_out(b, src):
                    name, j = BLOCKS[b]
                    weights(b)
                    for a in range(2):
                        ps = begin(name, j, a)
                        for c in range(2):
                            for k in range(KC):
                                ins = pe.matmul(ps[:, c * S:(c + 1) * S],
                                                slot_a(b % SLOTS)[:, k, (2 * a + c) * P:(2 * a + c + 1) * P], src[:, k, :],
                                                start=(k == 0), stop=(k == KC - 1))
                        end(ins)

                pe.wait_ge(vec_in, VEC_DMAS * 16 * (l + 1))
                end(pe.transpose(begin("vec", 0)[:, 0:NVEC], vrow[:, :], ident[0:NVEC, 0:NVEC]))
                pe.wait_ge(L["xn_ready"], 1)
                turn("mix_t", xn)
                turned("mix_t")
                ps = begin("small", 0)
                for k in range(KC):
                    pe.matmul(ps[0:RANK, 0:S], wsmall[:, k, 0:RANK], hT[:, k, :], start=(k == 0), stop=(k == KC - 1))
                for k in range(KC):
                    ins = pe.matmul(ps[0:HEADS, S:2 * S], wsmall[:, k, RANK:RANK + HEADS], hT[:, k, :],
                                    start=(k == 0), stop=(k == KC - 1))
                end(ins)
                ps = begin("small", 1)
                for k in range(KC):
                    ins = pe.matmul(ps[0:HEADS, 0:S], wsmall[:, k, RANK + HEADS:], hT[:, k, :],
                                    start=(k == 0), stop=(k == KC - 1))
                end(ins)
                channels_out(0, hT)
                channels_out(1, hT)
                wait_moved(pe, "small", 0)
                for a in range(2):
                    ps = begin("decay", a)
                    for c in range(2):
                        ins = pe.matmul(ps[:, c * S:(c + 1) * S], gkup[:, (2 * a + c) * P:(2 * a + c + 1) * P], lrT[:, :],
                                        start=True, stop=True)
                    end(ins)
                for b in range(2, 16):
                    if BLOCKS[b][0] in ("m_q", "m_k"):
                        channels_out(b, hT)
                    else:
                        rows_out(b, hT)
                pe.wait_ge(L["rows_ready"], 1)
                ps = begin("gate_cols", 0)
                for a in range(TT):
                    ins = pe.transpose(ps[:, a * P:(a + 1) * P], rows[:, a * P:(a + 1) * P], ident[:, :])
                end(ins)
                for b in range(4):
                    last = max(g for g in GROUPS.values() if g % 4 == b and g <= GROUPS[("gate_cols", 0)])
                    pe.wait_ge(moved[b], last // 4 + 1)

                pe.wait_ge(L["gla_in"], 1)
                for h in range(HEADS):
                    if h > 0:
                        pe.wait_ge(L["h_masked"], h)
                        pe.wait_ge(L["h_keys_sb"], h)
                    for a in range(TT):
                        ins = pe.matmul(bank[0][:, a * P:(a + 1) * P], gkT[:, h, a * P:(a + 1) * P],
                                        gqT[:, h, a * P:(a + 1) * P], start=True, stop=True)
                    for a in range(TT):
                        ins = pe.transpose(bank[5][:, a * P:(a + 1) * P], gkeT[:, h, a * P:(a + 1) * P], ident[:, :])
                    ins.then_inc(L["h_scores"], 1)
                    pe.wait_ge(L["h_keys_sb"], h + 1)
                    if h > 0:
                        pe.wait_ge(L["h_state"], 3 * h)
                    for c in range(NCH - 1):
                        r = slice((c % 2) * CH, (c % 2 + 1) * CH)
                        if c == 2:
                            pe.wait_ge(L["h_state"], 3 * h + 1)
                        ins = pe.matmul(bank[3 + c % 2][:, 0:DV], kn[r, c // 2, :], gv[r, c // 2, h * DV:(h + 1) * DV],
                                        start=True, stop=True)
                        ins.then_inc(L["h_dstate"], 1)
                    pe.wait_ge(L["h_masked"], h + 1)
                    if h > 0:
                        pe.wait_ge(L["h_outsb"], TT * h)
                    for a in range(TT):
                        for c in (2 * a, 2 * a + 1):
                            r = slice((c % 2) * CH, (c % 2 + 1) * CH)
                            ins = pe.matmul(bank[6 + a][r, 0:DV], sT[r, c * CH:(c + 1) * CH],
                                            gv[r, a, h * DV:(h + 1) * DV], start=True, stop=(c == 0))
                            if c > 0:
                                pe.wait_ge(L["h_state"], 3 * h + c)
                                ins = pe.matmul(bank[6 + a][r, 0:DV], gqT[:, h, c * CH:(c + 1) * CH], st[:, c - 1, 0:DV],
                                                start=False, stop=True)
                        ins.then_inc(L["h_out"], 1)

                pe.wait_ge(L["qk_ready"], 1)
                wait_moved(pe, "gate_cols", 0)
                for h in range(HEADS):
                    n = HEADS + h
                    pe.wait_ge(L["h_masked"], n)
                    pe.wait_ge(L["h_keys_sb"], n)
                    if h > 0:
                        pe.wait_ge(L["h_qs"], h)
                    pe.matmul(bank[1][:, 0:S + NCH], pick[:, h, :], mrow[:, :], start=True, stop=True)
                    ins = pe.matmul(bank[2][:, 0:S], pick[:, h, :], grow[:, 5, :], start=True, stop=True)
                    ins.then_inc(L["h_bcast"], 1)
                    for a in range(TT):
                        pe.matmul(bank[0][:, a * P:(a + 1) * P], qk[:, HEADS + h, a * P:(a + 1) * P],
                                  qk[:, h, a * P:(a + 1) * P], start=True, stop=True)
                    for a in range(TT):
                        ins = pe.transpose(bank[5][:, a * P:(a + 1) * P], qk[:, HEADS + h, a * P:(a + 1) * P], ident[:, :])
                    ins.then_inc(L["h_scores"], 1)
                    pe.wait_ge(L["h_keys_sb"], n + 1)
                    pe.wait_ge(L["h_state"], 3 * n)
                    for c in range(NCH - 1):
                        r = slice((c % 2) * CH, (c % 2 + 1) * CH)
                        if c == 2:
                            pe.wait_ge(L["h_state"], 3 * n + 1)
                        ins = pe.matmul(bank[3 + c % 2][:, 0:DV + 1], kn[r, c // 2, :], mv[r, c // 2, h, :], start=True, stop=True)
                        ins.then_inc(L["h_dstate"], 1)
                    pe.wait_ge(L["h_masked"], n + 1)
                    pe.wait_ge(L["h_qs"], h + 1)
                    pe.wait_ge(L["h_outsb"], TT * n)
                    for a in range(TT):
                        for c in (2 * a, 2 * a + 1):
                            r = slice((c % 2) * CH, (c % 2 + 1) * CH)
                            ins = pe.matmul(bank[6 + a][r, 0:DV + 1], wT[r, c * CH:(c + 1) * CH], mv[r, a, h, :],
                                            start=True, stop=(c == 0))
                            if c > 0:
                                pe.wait_ge(L["h_state"], 3 * n + c)
                                ins = pe.matmul(bank[6 + a][r, 0:DV + 1], qs[:, c * CH:(c + 1) * CH], st[:, c - 1, :],
                                                start=False, stop=True)
                        ins.then_inc(L["h_out"], 1)
                pe.wait_ge(L["h_masked"], 2 * HEADS)
                pe.wait_ge(L["h_keys_sb"], 2 * HEADS)
                pe.wait_ge(L["h_qs"], HEADS)
                pe.wait_ge(L["h_state"], 3 * 2 * HEADS)

                pe.wait_ge(L["gated_g"], TT * HEADS)
                turn("gla_t", xn)
                turned("gla_t")
                for b in (16, 17):
                    rows_out(b, aT)
                pe.wait_ge(L["gated_m"], TT * HEADS)
                turn("m_t", om)
                turned("m_t")
                for b in (18, 19):
                    rows_out(b, bT)
                for b in (18, 19):
                    for a in range(TT):
                        wait_moved(pe, *BLOCKS[b], a)
                turn("merged_t", ag)
                turned("merged_t")
                for b in (20, 21):
                    rows_out(b, hT)

                pe.wait_ge(L["xn_ready"], 2)
                turn("x_t", xn)
                turned("x_t")
                channels_out(22, hT)
                channels_out(23, hT)
                pe.wait_ge(L["mem_t"], 1)
                channels_out(24, aT)
                channels_out(25, aT)
                rows_out(26, aT)
                rows_out(27, aT)
                for b in range(22, 28):
                    for a in range(TT):
                        wait_moved(pe, *BLOCKS[b], a)

                def scores(h):
                    if h >= 2:
                        pe.wait_ge(L["x_exp"], TT * (h - 1))
                    for a in range(TT):
                        for c in range(2):
                            ins = pe.matmul(bank[4 + h % 2][:, a * M:(a + 1) * M], bT[:, 2 * h + c, a * P:(a + 1) * P],
                                            kT[:, 2 * h + c, :], start=(c == 0), stop=(c == 1))
                    ins.then_inc(L["x_score"], 1)

                def attend(h):
                    pe.wait_ge(L["x_prob"], h + 1)
                    if h > 0:
                        pe.wait_ge(L["x_pt_sb"], h)
                    for m in range(2):
                        for a in range(TT):
                            ins = pe.transpose(bank[6][:, (m * TT + a) * P:(m * TT + a + 1) * P],
                                               prob[:, a, m * P:(m + 1) * P], ident[:, :])
                    ins.then_inc(L["x_pt"], 1)
                    pe.wait_ge(L["x_pt_sb"], h + 1)
                    if h > 0:
                        pe.wait_ge(L["x_o_sb"], h)
                    for c in range(2):
                        for m in range(2):
                            ins = pe.matmul(bank[7][:, c * S:(c + 1) * S],
                                            gv[:, m, h * DV + c * P:h * DV + (c + 1) * P], probT[:, m, :],
                                            start=(m == 0), stop=(m == 1))
                    ins.then_inc(L["x_o"], 1)

                scores(0)
                scores(1)
                for h in range(HEADS):
                    attend(h)
                    if h + 2 < HEADS:
                        scores(h + 2)
                pe.wait_ge(L["x_o_sb"], HEADS)
                rows_out(28, aT)
                rows_out(29, aT)

                pe.wait_ge(L["xn_ready"], 3)
                turn("ffn_t", xn)
                turned("ffn_t")
                GATE, UP = (0, 5), (1, 6)

                def ff_gate(src, tiles, w, used, silu, mid=None):
                    pe.wait_ge(full[0], used)
                    for a in range(tiles):
                        if silu is not None:
                            pe.wait_ge(L["silu_done"], silu + a)
                        for k in range(KC):
                            ins = pe.matmul(bank[GATE[a]][:, 0:w], src[:, k, a * P:(a + 1) * P], slot_a(0)[:, k, 0:w],
                                            start=(k == 0), stop=(k == KC - 1))
                            if k == 3 and a == 0 and mid is not None:
                                mid()
                        ins.then_inc(L["gate_ps"], 1)

                def ff_up(src, tiles, w, used):
                    pe.wait_ge(full[2], used)
                    for a in range(tiles):
                        for k in range(KC):
                            ins = pe.matmul(bank[UP[a]][:, 0:w], src[:, k, a * P:(a + 1) * P], slot_a(2)[:, k, 0:w],
                                            start=(k == 0), stop=(k == KC - 1))
                        ins.then_inc(L["up_ps"], 1)

                def ff_turn(tiles, w, n):
                    for a in range(tiles):
                        pe.wait_ge(L["hid_ready"], n + a + 1)
                        for k in range((w + P - 1) // P):
                            m = min(P, w - k * P)
                            ins = pe.transpose(bank[(2, 7)[a]][0:m, k * P:(k + 1) * P], hid[:, a, k * P:k * P + m], ident[:, :])
                        ins.then_inc(L["hid_tr"], 1)

                def ff_down(tiles, w, n, used, free):
                    pe.wait_ge(full[1], used)
                    for a in range(tiles):
                        pe.wait_ge(L["hidT_ready"], n + a + 1)
                        for c in range(2):
                            if free(a, c) is not None:
                                pe.wait_ge(L["y_added"], free(a, c))
                            nk = (w + P - 1) // P
                            for k in range(nk):
                                m = min(P, w - k * P)
                                ins = pe.matmul(bank[3 + c][:, :], hidT[0:m, a, k, :], slot_d(1)[0:m, k, c * 512:(c + 1) * 512],
                                                start=(k == 0), stop=(k == nk - 1))
                            ins.then_inc(L["y_ps"], 1)

                with pe.If(l == 0):
                    def w_of(i):
                        return HB if i < DENSE_STEPS - 1 else DENSE_TAIL

                    def used(i, extra=0):
                        return 16 * (DENSE_BASE + i + 1) + extra

                    def free_of(i):
                        return lambda a, c: 2 * (TT * i + a) + c - 1 if TT * i + a > 0 else None

                    ff_gate(hT, TT, HB, used(0), None)
                    ff_up(hT, TT, HB, used(0))
                    for i in range(1, DENSE_STEPS):
                        ff_gate(hT, TT, w_of(i), used(i), TT * (i - 1) + 1,
                                mid=lambda: ff_turn(TT, w_of(i - 1), TT * (i - 1)))
                        ff_down(TT, w_of(i - 1), TT * (i - 1), used(i - 1), free_of(i - 1))
                        ff_up(hT, TT, w_of(i), used(i))
                    i = DENSE_STEPS
                    ff_turn(TT, w_of(i - 1), TT * (i - 1))
                    ff_down(TT, w_of(i - 1), TT * (i - 1), used(i - 1, 16), free_of(i - 1))
                    pe.wait_ge(L["y_added"], 2 * TT * DENSE_STEPS)
                with pe.Else():
                    pe.sem_inc(L["gate_ps"], 1)
                    pe.sem_inc(L["up_ps"], 1)
                    pe.sem_inc(L["y_ps"], 1)
                    for a in range(TT):
                        for k in range(KC):
                            ins = pe.matmul(bank[4][:, a * NE:(a + 1) * NE], hT[:, k, a * P:(a + 1) * P], rw[:, k, :],
                                            start=(k == 0), stop=(k == KC - 1))
                    ins.then_inc(L["logit_ps"], 1)
                    pe.wait_ge(L["count_in"], 1)
                    pe.matmul(bank[5][:, 0:NE], tri[:, :], chosen[:, 0, :], start=True, stop=True)
                    pe.matmul(bank[5][:, NE:2 * NE], tri[:, :], chosen[:, 1, :], start=True, stop=False)
                    pe.matmul(bank[5][:, NE:2 * NE], ones[:, :], chosen[:, 0, :], start=False, stop=True)
                    pe.matmul(bank[5][:, 2 * NE:3 * NE], ones[:, :], chosen[:, 0, :], start=True, stop=False)
                    pe.matmul(bank[5][:, 2 * NE:3 * NE], ones[:, :], chosen[:, 1, :], start=False, stop=True)\
                        .then_inc(L["count_ps"], 1)
                    pe.wait_ge(L["npass_ready"], 1)
                    npass = pe.value_load(npass_i[0:1, 0:1], min_val=1, max_val=TT)

                    def used(q, i):
                        return (MOE_BASE + i + 1 + q * MOE_STEPS) * 16

                    with pe.Fori(0, npass) as ps_:
                        with pe.Fori(0, NE) as e:
                            q = ps_ * NE + e
                            pe.wait_ge(L["onehot_ready"], q + 1)
                            for k in range(KC):
                                for a in range(TT):
                                    ins = pe.matmul(bank[5 + k // 4][:, (k % 4) * P:(k % 4 + 1) * P],
                                                    xn[:, a, k * P:(k + 1) * P], onehot[:, a, :], start=(a == 0), stop=(a == 1))
                            for a in range(TT):
                                ins = pe.transpose(bank[7][:, a * P:(a + 1) * P], gated[:, a, :], ident[:, :])
                            ins.then_inc(L["gather_ps"], 1)
                            pe.wait_ge(L["gather_sb"], q + 1)
                            ff_gate(hgT, 1, HB, used(q, 0), None)
                            ff_up(hgT, 1, HB, used(q, 0))
                            with pe.Fori(1, MOE_STEPS) as i:
                                k_ = q * MOE_STEPS + i
                                ff_gate(hgT, 1, HB, used(q, i), k_, mid=lambda: ff_turn(1, HB, k_ - 1))
                                ff_down(1, HB, k_ - 1, used(q, i - 1) + 16, lambda a, c: 2 * (k_ - 1) + 1)
                                ff_up(hgT, 1, HB, used(q, i))
                            k_ = q * MOE_STEPS + MOE_STEPS
                            ff_turn(1, HB, k_ - 1)
                            ff_down(1, HB, k_ - 1, used(q, MOE_STEPS - 1) + 16, lambda a, c: 2 * (k_ - 1) + 1)
                            pe.wait_ge(L["y_added"], 2 * k_ + 1)
                            for a in range(TT):
                                for c in range(2):
                                    ins = pe.matmul(bank[(5, 6, 7, 2)[2 * a + c]][:, :], gatedT[:, a * P:(a + 1) * P],
                                                    yacc[:, c * 512:(c + 1) * 512], start=True, stop=True)
                            ins.then_inc(L["scatter_ps"], 1)
                            pe.wait_ge(L["scattered"], q + 1)
                pe.nop()
                layer_end(pe, l)

        @block.scalar
        def _(act):
            step = Steps(act, act_own)
            act.wait_ge(const_ready, CONSTS)

            def chain(ins, sem=None, value=None):
                step.did(ins, sem, value)
                step.wait()

            act.wait_ge(mem_in, 16)
            for a in range(TT):
                act.activation(gv[:, a, :], xn[:, a, :], ACT.Square, accum_out=ssum2[:, a:a + 1]).then_inc(mem_sq, 1)
            act.wait_ge(mem_var, 1)
            act.activation(rstd2[:, :], ssum2[:, :], ACT.Sqrt).then_inc(mem_root, 1)
            act.wait_ge(mem_root, 1)
            act.wait_ge(x_in, 16)

            with act.Fori(0, DEPTH) as l:
                step.n, step.last = 0, None

                def squares(n):
                    for a in range(TT):
                        chain(act.activation(junk[:, :], x[:, a, :], ACT.Square, accum_out=ssum2[:, a:a + 1]),
                              L["sq_done"], TT * n + a + 1)
                    act.wait_ge(L["var_done"], n + 1)
                    chain(act.activation(rstd2[:, :], ssum2[:, :], ACT.Sqrt), L["root_done"], n + 1)

                def turn_even(name, dst, gain_name):
                    for j in (0, 2):
                        ps, mv_, v = group(name, j)
                        wait_group(act, name, j)
                        for k in range(2):
                            c = 2 * j + k
                            scale = vcol[:, VEC[gain_name] + c:VEC[gain_name] + c + 1] if gain_name else 1.0
                            ins = act.activation(dst[:, c, :], ps[:, k * S:(k + 1) * S], ACT.Copy, scale=scale)
                            chain(ins, mv_, v) if k else chain(ins)

                def read_out(name, dst, func, **kw):
                    wait_group(act, *name)
                    ps, mv_, v = group(*name)
                    chain(act.activation(dst, ps[:, :], func, **kw), mv_, v)

                squares(0)
                wait_moved(act, "vec", 0)
                turn_even("mix_t", hT, "norm_mix")
                ps, mv_, v = group("small", 0)
                wait_group(act, "small", 0)
                chain(act.activation(grow[:, 0, :], ps[0:HEADS, S:2 * S], ACT.Copy))
                chain(act.activation(lrT[:, :], ps[0:RANK, 0:S], ACT.Copy), mv_, v)
                for name, dst in (("g_q", gqT), ("g_k", gkT)):
                    for a in range(2):
                        read_out((name, 0, a), dst[:, 2 * a:2 * a + 2, :].rearrange("p a b -> p (a b)"), ACT.Copy)
                act.wait_ge(L["decay_z"], 1)
                chain(act.activation(e1[:, :, :], e1[:, :, :], ACT.Exp, scale=-1.0))
                chain(act.activation(e1[:, :, :], e1[:, :, :], ACT.Ln, bias=1.0), L["decay_e"], 1)
                act.wait_ge(L["gate_z"], 1)
                chain(act.activation(grow[:, 2, :], grow[:, 2, :], ACT.Exp, scale=-1.0))
                chain(act.activation(grow[:, 2, :], grow[:, 2, :], ACT.Ln, bias=1.0), L["row_ln"], 1)
                for j in range(2):
                    for a in range(TT):
                        read_out(("g_v", j, a), gv[:, a, j * 512:(j + 1) * 512], ACT.Copy)
                act.wait_ge(L["cum_ready"], 1)
                chain(act.activation(e1[:, :, :], gkeT[:, :, :], ACT.Exp))
                chain(act.activation(cum[:, :, :], gkeT[:, :, :], ACT.Exp, scale=-1.0), L["e_ready"], 1)
                act.wait_ge(L["row_dm"], 1)
                chain(act.activation(grow[:, 5, :], grow[:, 4, :], ACT.Exp, scale=-1.0, bias=lnscale[0:HEADS, :]))
                chain(act.activation(mrow[:, S:], grow[:, 4, CH - 1:S:CH], ACT.Exp, scale=-1.0))
                chain(act.activation(rows[64:64 + HEADS, :], rows[64:64 + HEADS, :], ACT.Exp))
                chain(act.activation(rows[96:96 + HEADS, :], rows[96:96 + HEADS, :], ACT.Exp, scale=-1.0), L["rows_ready"], 1)
                act.wait_ge(L["e_ready"], 1)
                for j in range(2):
                    for a in range(TT):
                        read_out(("g_g", j, a), gg[:, a, j * 512:(j + 1) * 512], ACT.Silu)
                for n_, name in enumerate(("m_q", "m_k")):
                    for a in range(2):
                        ps, mv_, v = group(name, 0, a)
                        wait_group(act, name, 0, a)
                        chain(act.activation(cin[:, 4 * n_ + 2 * a:4 * n_ + 2 * a + 2, CONV_W - 1:],
                                             ps[:, :].rearrange("p (c s) -> p c s", c=2), ACT.Copy), mv_, v)
                for j in range(2):
                    for a in range(TT):
                        ps, mv_, v = group("m_v", j, a)
                        wait_group(act, "m_v", j, a)
                        chain(act.activation(mv[:, a, 2 * j:2 * j + 2, 0:DV], ps[:, :].rearrange("p (h v) -> p h v", h=2),
                                             ACT.Copy), mv_, v)
                for name, dst in (("m_o", mo), ("a_gla", ag), ("a_m", am)):
                    for j in range(2):
                        for a in range(TT):
                            read_out((name, j, a), dst[:, a, j * 512:(j + 1) * 512], ACT.Sigmoid)
                act.wait_ge(L["conv_out"], 1)
                chain(act.activation(qk[:, :, :], qk[:, :, :], ACT.Silu), L["qk_ready"], 1)

                for h in range(HEADS):
                    act.wait_ge(L["h_scores"], h + 1)
                    if h > 0:
                        act.wait_ge(L["h_dstate"], 3 * h)
                    chain(act.activation(aT[:, 3, :], bank[5][:, 0:2 * P], ACT.Copy),
                          L["h_keys_sb"], h + 1)
                    for a in range(TT):
                        act.wait_ge(L["h_out"], TT * h + a + 1)
                        chain(act.activation(xn[:, a, h * DV:(h + 1) * DV], bank[6 + a][:, 0:DV], ACT.Copy))
                        chain(act.activation(junk[:, 0:DV], bank[6 + a][:, 0:DV], ACT.Square,
                                             accum_out=ssum[:, a * HEADS + h:a * HEADS + h + 1]), L["h_outsb"], TT * h + a + 1)
                act.wait_ge(L["norm_var"], 1)
                chain(act.activation(rstd[:, :], ssum[:, :], ACT.Sqrt), L["norm_root"], 1)

                wait_moved(act, "gate_cols", 0)
                for h in range(HEADS):
                    n = HEADS + h
                    act.wait_ge(L["h_dexp_in"], h + 1)
                    if h > 0:
                        act.wait_ge(L["h_masked"], n)
                    chain(act.activation(dexp[:, :], dexp[:, :], ACT.Exp, scale=-1.0), L["h_dexp"], h + 1)
                    act.wait_ge(L["h_scores"], n + 1)
                    act.wait_ge(L["h_dstate"], 3 * n)
                    for a in range(TT):
                        ins = act.activation(kn[:, a, :], bank[5][:, a * P:(a + 1) * P], ACT.Copy,
                                             scale=cols[:, a, 64 + h:65 + h])
                        chain(ins, L["h_keys_sb"], n + 1) if a else chain(ins)
                    for a in range(TT):
                        act.wait_ge(L["h_den"], TT * h + a + 1)
                        sl = slice(a * HEADS + h, a * HEADS + h + 1)
                        chain(act.activation(om[:, a, h * DV:(h + 1) * DV], bank[6 + a][:, 0:DV], ACT.Copy,
                                             scale=den[:, a:a + 1]))
                        if h == 0 and a == 0:
                            act.wait_ge(L["gated_g"], TT * HEADS)
                        chain(act.activation(junk[:, 0:DV], om[:, a, h * DV:(h + 1) * DV], ACT.Square,
                                             accum_out=ssum[:, sl]), L["h_outsb"], TT * n + a + 1)
                act.wait_ge(L["norm_var"], 2)
                chain(act.activation(rstd[:, :], ssum[:, :], ACT.Sqrt), L["norm_root"], 2)

                turn_even("gla_t", aT, "gla_norm")
                turn_even("m_t", bT, "m_norm")
                turn_even("merged_t", hT, None)
                for j in range(2):
                    for a in range(TT):
                        wait_moved(act, "w_out", j, a)
                squares(1)
                turn_even("x_t", hT, "norm_xattn")
                for j in range(2):
                    for a in range(2):
                        c = 4 * j + 2 * a
                        read_out(("x_wq", j, a), bT[:, c:c + 2, :].rearrange("p c s -> p (c s)"), ACT.Copy)
                for j in range(2):
                    for a in range(2):
                        c = 4 * j + 2 * a
                        read_out(("x_wk", j, a), kT[:, c:c + 2, :].rearrange("p c s -> p (c s)"), ACT.Copy)
                for j in range(2):
                    for a in range(TT):
                        read_out(("x_wv", j, a), gv[:, a, j * 512:(j + 1) * 512], ACT.Copy)
                for h in range(HEADS):
                    act.wait_ge(L["x_negmax"], h + 1)
                    if h > 0:
                        act.wait_ge(L["x_pt"], h)
                    for a in range(TT):
                        chain(act.activation(prob[:, a, :], bank[4 + h % 2][:, a * M:(a + 1) * M], ACT.Exp, scale=X_SCALE,
                                             bias=nmx[:, a:a + 1], accum_out=rsum[:, a:a + 1]), L["x_exp"], TT * h + a + 1)
                    act.wait_ge(L["x_pt"], h + 1)
                    if h > 0:
                        act.wait_ge(L["x_o"], h)
                    chain(act.activation(probT[:, :, :].rearrange("p m s -> p (m s)"), bank[6][:, :], ACT.Copy),
                          L["x_pt_sb"], h + 1)
                for j in range(2):
                    for a in range(TT):
                        wait_moved(act, "x_wo", j, a)
                squares(2)
                turn_even("ffn_t", hT, "norm_ffn")

                def ff_silu(tiles, w, n, n_wait):
                    for a in range(tiles):
                        act.wait_ge(L["gate_ps"], n_wait + a + 1)
                        act.activation(sg[:, a, 0:w], bank[(0, 5)[a]][:, 0:w], ACT.Silu).then_inc(L["silu_done"], 1)

                def ff_copy(tiles, w, n):
                    nk = (w + P - 1) // P
                    for a in range(tiles):
                        act.wait_ge(L["hid_tr"], n + a + 1)
                        full_k = w // P
                        ins = act.activation(hidT[:, a, 0:full_k, :], bank[(2, 7)[a]][:, 0:full_k * P].rearrange(
                            "p (k c) -> p k c", c=P), ACT.Copy)
                        if nk > full_k:
                            ins.then_inc(act_own, 1)
                            step.n += 1
                            m = w - full_k * P
                            act.wait_ge(act_own, step.n)
                            ins = act.activation(hidT[0:m, a, full_k, :], bank[(2, 7)[a]][0:m, full_k * P:nk * P], ACT.Copy)
                        ins.then_inc(L["hidT_ready"], 1)

                with act.If(l == 0):
                    def w_of(i):
                        return HB if i < DENSE_STEPS - 1 else DENSE_TAIL

                    ff_silu(TT, HB, 0, 0)
                    for i in range(1, DENSE_STEPS):
                        ff_copy(TT, w_of(i - 1), TT * (i - 1))
                        ff_silu(TT, w_of(i), TT * i, TT * i)
                    ff_copy(TT, w_of(DENSE_STEPS - 1), TT * (DENSE_STEPS - 1))
                    act.wait_ge(L["y_added"], 2 * TT * DENSE_STEPS)
                with act.Else():
                    act.dma_start(gain, t["norm_ffn"][1].rearrange("(o d) -> o d", o=1).broadcast_to([P, D]))\
                        .then_inc(L["gain_in"], 16)
                    act.wait_ge(L["top_e_in"], 1)
                    act.activation(tw[:, :, 0:1], tw[:, :, 0:1], ACT.Exp).then_inc(L["top_e"], 1)
                    act.wait_ge(L["npass_ready"], 1)
                    npass = act.value_load(npass_i[0:1, 0:1], min_val=1, max_val=TT)
                    with act.Fori(0, npass) as ps_:
                        with act.Fori(0, NE) as e:
                            q = ps_ * NE + e
                            act.wait_ge(L["gather_ps"], q + 1)
                            for k in range(2):
                                act.activation(hgT[:, 4 * k:4 * k + 4, :].rearrange("p k c -> p (k c)"), bank[5 + k][:, :],
                                               ACT.Copy)
                            act.activation(gatedT, bank[7][:, 0:S], ACT.Copy).then_inc(L["gather_sb"], 1)
                            ff_silu(1, HB, None, q * MOE_STEPS + 1)
                            with act.Fori(1, MOE_STEPS) as i:
                                k_ = q * MOE_STEPS + i
                                ff_copy(1, HB, k_ - 1)
                                ff_silu(1, HB, None, k_ + 1)
                            ff_copy(1, HB, q * MOE_STEPS + MOE_STEPS - 1)
                act.nop()
                layer_end(act, l)
            for a in range(TT):
                act.activation(gv[:, a, :], x[:, a, :], ACT.Square, accum_out=ssum2[:, a:a + 1]).then_inc(fin_sq, 1)
            act.wait_ge(fin_var, 1)
            act.activation(rstd2[:, :], ssum2[:, :], ACT.Sqrt).then_inc(fin_root, 1)
            act.dma_start(junk[:, :], t["norm_final"].rearrange("(o d) -> o d", o=1).broadcast_to([P, D])).then_inc(last_in, 16)

        @block.vector
        def _(dve):
            step = Steps(dve, dve_own)
            dve.wait_ge(const_ready, CONSTS)

            def op(ins, sem=None, value=None):
                step.did(ins, sem, value)
                step.wait()

            dve.wait_ge(mem_sq, 2)
            dve.tensor_scalar(ssum2[:, :], ssum2[:, :], 1.0 / D, EPS, ALU.mult, ALU.add).then_inc(mem_var, 1)
            dve.wait_ge(mem_root, 1)
            dve.reciprocal(rstd2[:, :], rstd2[:, :]).then_inc(mem_var, 1)
            dve.wait_ge(mem_var, 2)
            for a in range(TT):
                dve.tensor_scalar(gg[:, a, :], xn[:, a, :], rstd2[:, a:a + 1], None, ALU.mult).then_inc(mem_n, 1)
            for j in range(4):
                dve.wait_ge(mem_tp, j + 1)
                dve.tensor_copy(memhT[:, 2 * j:2 * j + 2, :].rearrange("p k s -> p (k s)"), bank[j][:, :]).then_inc(mem_ready, 1)
            dve.wait_ge(mem_ready, 4)
            dve.wait_ge(x_in, 16)

            with dve.Fori(0, DEPTH) as l:
                step.n, step.last = 0, None

                def norm(n):
                    dve.wait_ge(L["sq_done"], TT * (n + 1))
                    op(dve.tensor_scalar(ssum2[:, :], ssum2[:, :], 1.0 / D, EPS, ALU.mult, ALU.add), L["var_done"], n + 1)
                    dve.wait_ge(L["root_done"], n + 1)
                    op(dve.reciprocal(rstd2[:, :], rstd2[:, :]))
                    op(dve.tensor_scalar(xn[:, 0, :], x[:, 0, :], rstd2[:, 0:1], None, ALU.mult))
                    op(dve.tensor_scalar(xn[:, 1, :], x[:, 1, :], rstd2[:, 1:2], None, ALU.mult), L["xn_ready"], n + 1)

                def turn_odd(name, dst, gain_name):
                    for j in (1, 3):
                        ps, mv_, v = group(name, j)
                        wait_group(dve, name, j)
                        for k in range(2):
                            c = 2 * j + k
                            if gain_name:
                                ins = dve.tensor_scalar(dst[:, c, :], ps[:, k * S:(k + 1) * S],
                                                        vcol[:, VEC[gain_name] + c:VEC[gain_name] + c + 1], None, ALU.mult)
                            else:
                                ins = dve.tensor_copy(dst[:, c, :], ps[:, k * S:(k + 1) * S])
                            op(ins, mv_, v) if k else op(ins)

                wait_group(dve, "vec", 0)
                op(dve.tensor_copy(vcol[:, :], bank[GROUPS[("vec", 0)] % 4][:, 0:NVEC]), moved[0], 1)
                norm(0)
                turn_odd("mix_t", hT, "norm_mix")
                ps, mv_, v = group("small", 1)
                wait_group(dve, "small", 1)
                op(dve.tensor_scalar(grow[:, 1, :], ps[0:HEADS, 0:S], gbias[:, 1:2], None, ALU.add), mv_, v)
                op(dve.scalar_tensor_tensor(grow[:, 2, :], grow[:, 1, :], -1.0, grow[:, 1, :], ALU.mult, ALU.max), L["gate_z"], 1)
                for a in range(2):
                    ps, mv_, v = group("decay", a)
                    wait_group(dve, "decay", a)
                    for c in range(2):
                        h = 2 * a + c
                        ins = dve.tensor_scalar(cum[:, h, :], ps[:, c * S:(c + 1) * S],
                                                vcol[:, VEC["gla_gk_bias"] + h:VEC["gla_gk_bias"] + h + 1], None, ALU.add)
                        op(ins, mv_, v) if c else op(ins)
                op(dve.scalar_tensor_tensor(e1[:, :, :].rearrange("p h s -> p (h s)"), cum[:, :, :].rearrange("p h s -> p (h s)"), -1.0,
                                            cum[:, :, :].rearrange("p h s -> p (h s)"), ALU.mult, ALU.max), L["decay_z"], 1)
                dve.wait_ge(L["decay_e"], 1)
                op(dve.scalar_tensor_tensor(cum[:, :, :].rearrange("p h s -> p (h s)"), cum[:, :, :].rearrange("p h s -> p (h s)"),
                                            0.0, e1[:, :, :].rearrange("p h s -> p (h s)"), ALU.min, ALU.subtract))
                op(dve.tensor_scalar(cum[:, :, :], cum[:, :, :], 1.0 / GATE_NORM, LOG_DECAY_MIN, ALU.mult, ALU.max))
                op(dve.tensor_tensor_scan(gkeT[:, :, :].rearrange("p h s -> p (h s)"), restart[:, :],
                                          cum[:, :, :].rearrange("p h s -> p (h s)"), 0.0, ALU.mult, ALU.add),
                   L["cum_ready"], 1)
                dve.wait_ge(L["row_ln"], 1)
                op(dve.scalar_tensor_tensor(grow[:, 1, :], grow[:, 1, :], 0.0, grow[:, 2, :], ALU.min, ALU.subtract))
                op(dve.tensor_tensor_scan(grow[:, 3, :], restart[0:HEADS, 0:S], grow[:, 1, :], 0.0, ALU.mult, ALU.add))
                wait_moved(dve, "small", 0)
                op(dve.scalar_tensor_tensor(grow[:, 1, :], grow[:, 0, :], gbias[:, 0:1], grow[:, 3, :], ALU.add, ALU.subtract))
                op(dve.tensor_copy(rows[0:HEADS, :], grow[:, 1, :]))
                for c in range(NCH):
                    s_ = slice(c * CH, (c + 1) * CH)
                    e_ = slice((c + 1) * CH - 1, (c + 1) * CH)
                    op(dve.tensor_tensor_scan(mrow[:, s_], zrow[:, :], grow[:, 1, s_], mst[:, c:c + 1], ALU.add, ALU.max))
                    op(dve.tensor_scalar(grow[:, 4, s_], mrow[:, s_], mst[:, c:c + 1], None, ALU.subtract))
                    op(dve.tensor_scalar(rows[64:64 + HEADS, s_], grow[:, 1, s_], mrow[:, e_], None, ALU.subtract))
                    op(dve.tensor_tensor(mst[:, c + 1:c + 2], grow[:, 3, e_], mrow[:, e_], ALU.add))
                op(dve.tensor_tensor(rows[96:96 + HEADS, :], grow[:, 3, :], mrow[:, 0:S], ALU.add), L["row_dm"], 1)
                dve.wait_ge(L["e_ready"], 1)
                flat = "p h s -> p (h s)"
                for a in range(2):
                    wait_moved(dve, "g_q", 0, a)
                    wait_moved(dve, "g_k", 0, a)
                op(dve.scalar_tensor_tensor(gqT[:, :, :].rearrange(flat), gqT[:, :, :].rearrange(flat), QK_SCALE,
                                            e1[:, :, :].rearrange(flat), ALU.mult, ALU.mult))
                op(dve.tensor_tensor(gkT[:, :, :], gkT[:, :, :], cum[:, :, :], ALU.mult))
                ends = e1[:, :, CH - 1:S:CH].unsqueeze(3).broadcast_to([P, HEADS, NCH, CH])
                for h in range(HEADS):
                    ins = dve.tensor_tensor(gkeT[:, h, :].rearrange("p (c s) -> p c s", s=CH),
                                            gkT[:, h, :].rearrange("p (c s) -> p c s", s=CH), ends[:, h], ALU.mult)
                    op(ins, L["gla_in"], 1) if h == HEADS - 1 else op(ins)
                for n_, name in enumerate(("m_q", "m_k")):
                    for a in range(2):
                        wait_moved(dve, name, 0, a)
                        for c in (4 * n_ + 2 * a, 4 * n_ + 2 * a + 1):
                            def tap(j):
                                at = VEC["m_conv"] + j * KC + c
                                return vcol[:, at:at + 1]
                            op(dve.tensor_scalar(qk[:, c, :], cin[:, c, 0:S], tap(0), None, ALU.mult))
                            for j in range(1, CONV_W):
                                ins = dve.scalar_tensor_tensor(qk[:, c, :], cin[:, c, j:j + S], tap(j), qk[:, c, :],
                                                               ALU.mult, ALU.add)
                                last = c == KC - 1 and j == CONV_W - 1
                                op(ins, L["conv_out"], 1) if last else op(ins)
                ps, mv_, v = group("gate_cols", 0)
                wait_group(dve, "gate_cols", 0)
                op(dve.tensor_copy(cols[:, :, :].rearrange("p a c -> p (a c)"), ps[:, 0:TT * P]), mv_, v)

                for h in range(HEADS):
                    dve.wait_ge(L["h_scores"], h + 1)
                    if h > 0:
                        dve.wait_ge(L["h_out"], TT * h)
                    op(dve.copy_predicated(sT[:, :], causal[:, :].bitcast(U32), bank[0][:, 0:TT * P]), L["h_masked"], h + 1)
                    for c in range(NCH - 1):
                        dve.wait_ge(L["h_dstate"], 3 * h + c + 1)
                        if c == 0:
                            ins = dve.tensor_copy(st[:, 0, 0:DV], bank[3][:, 0:DV])
                        else:
                            ins = dve.scalar_tensor_tensor(st[:, c, 0:DV], st[:, c - 1, 0:DV],
                                                           e1[:, h, (c + 1) * CH - 1:(c + 1) * CH], bank[3 + c % 2][:, 0:DV],
                                                           ALU.mult, ALU.add)
                        op(ins, L["h_state"], 3 * h + c + 1)

                def head_norm(n, o, gate, done):
                    op(dve.tensor_scalar(ssum[:, :], ssum[:, :], 1.0 / DV, EPS, ALU.mult, ALU.add), L["norm_var"], n)
                    dve.wait_ge(L["norm_root"], n)
                    op(dve.reciprocal(rstd[:, :], rstd[:, :]))
                    for a in range(TT):
                        for h in range(HEADS):
                            i = a * HEADS + h
                            op(dve.scalar_tensor_tensor(o[:, a, h * DV:(h + 1) * DV], o[:, a, h * DV:(h + 1) * DV],
                                                        rstd[:, i:i + 1], gate[:, a, h * DV:(h + 1) * DV], ALU.mult, ALU.mult),
                               L[done], i + 1)

                dve.wait_ge(L["h_outsb"], TT * HEADS)
                for j in range(2):
                    for a in range(TT):
                        wait_moved(dve, "g_g", j, a)
                head_norm(1, xn, gg, "gated_g")

                for h in range(HEADS):
                    n = HEADS + h
                    dve.wait_ge(L["h_bcast"], h + 1)
                    if h > 0:
                        dve.wait_ge(L["h_dexp"], h)
                    for a in range(TT):
                        ins = dve.scalar_tensor_tensor(dexp[:, a * P:(a + 1) * P], bank[1][:, a * P:(a + 1) * P],
                                                       cols[:, a, h:h + 1], hide[:, a * P:(a + 1) * P], ALU.subtract, ALU.max)
                        op(ins, L["h_dexp_in"], h + 1) if a else op(ins)
                    op(dve.tensor_copy(sdec[:, h, :], bank[1][:, S:S + NCH]))
                    if h == 0:
                        dve.wait_ge(L["qk_ready"], 1)
                    dve.wait_ge(L["h_out"], TT * n)
                    op(dve.tensor_tensor(qs[:, :], qk[:, h, :], bank[2][:, 0:S], ALU.mult), L["h_qs"], h + 1)
                    dve.wait_ge(L["h_dexp"], h + 1)
                    dve.wait_ge(L["h_scores"], n + 1)
                    op(dve.scalar_tensor_tensor(wT[:, :], bank[0][:, 0:TT * P], QK_SCALE, dexp[:, :], ALU.mult, ALU.mult),
                       L["h_masked"], n + 1)
                    for c in range(NCH - 1):
                        dve.wait_ge(L["h_dstate"], 3 * n + c + 1)
                        if c == 0:
                            ins = dve.tensor_copy(st[:, 0, :], bank[3][:, 0:DV + 1])
                        else:
                            ins = dve.scalar_tensor_tensor(st[:, c, :], st[:, c - 1, :], sdec[:, h, c:c + 1],
                                                           bank[3 + c % 2][:, 0:DV + 1], ALU.mult, ALU.add)
                        op(ins, L["h_state"], 3 * n + c + 1)
                    for a in range(TT):
                        dve.wait_ge(L["h_out"], TT * n + a + 1)
                        if h > 0:
                            dve.wait_ge(L["h_outsb"], TT * (n - 1) + a + 1)
                        op(dve.scalar_tensor_tensor(den[:, a:a + 1], bank[6 + a][:, DV:DV + 1], -1.0,
                                                    cols[:, a, 96 + h:97 + h], ALU.mult, ALU.max))
                        op(dve.tensor_tensor(den[:, a:a + 1], den[:, a:a + 1], bank[6 + a][:, DV:DV + 1], ALU.max))
                        op(dve.reciprocal(den[:, a:a + 1], den[:, a:a + 1]), L["h_den"], TT * h + a + 1)
                dve.wait_ge(L["h_outsb"], TT * 2 * HEADS)
                for j in range(2):
                    for a in range(TT):
                        wait_moved(dve, "m_o", j, a)
                head_norm(2, om, mo, "gated_m")

                turn_odd("gla_t", aT, "gla_norm")
                for j in range(2):
                    for a in range(TT):
                        c = slice(j * 512, (j + 1) * 512)
                        ps, mv_, v = group("gla_proj", j, a)
                        wait_group(dve, "gla_proj", j, a)
                        op(dve.tensor_tensor(ag[:, a, c], ag[:, a, c], ps[:, :], ALU.mult), mv_, v)
                turn_odd("m_t", bT, "m_norm")
                for j in range(2):
                    for a in range(TT):
                        c = slice(j * 512, (j + 1) * 512)
                        ps, mv_, v = group("m_proj", j, a)
                        wait_group(dve, "m_proj", j, a)
                        op(dve.tensor_tensor(am[:, a, c], am[:, a, c], ps[:, :], ALU.mult))
                        op(dve.tensor_tensor(ag[:, a, c], ag[:, a, c], am[:, a, c], ALU.add), mv_, v)
                turn_odd("merged_t", hT, None)

                def add_to_x(name):
                    for j in range(2):
                        for a in range(TT):
                            c = slice(j * 512, (j + 1) * 512)
                            ps, mv_, v = group(name, j, a)
                            wait_group(dve, name, j, a)
                            op(dve.tensor_tensor(x[:, a, c], x[:, a, c], ps[:, :], ALU.add), mv_, v)

                for j in range(2):
                    for a in range(TT):
                        wait_group(dve, "gla_proj", j, a)
                for k in range(KC):
                    at = VEC["norm_mem"] + k
                    ins = dve.tensor_scalar(aT[:, k, :], memhT[:, k, :], vcol[:, at:at + 1], None, ALU.mult)
                    op(ins, L["mem_t"], 1) if k == KC - 1 else op(ins)
                add_to_x("w_out")
                norm(1)
                turn_odd("x_t", hT, "norm_xattn")
                for h in range(HEADS):
                    dve.wait_ge(L["x_score"], h + 1)
                    op(dve.tensor_reduce(mx[:, :], bank[4 + h % 2][:, :].rearrange("p (a m) -> p a m", a=TT), axis=AX.X, op=ALU.max))
                    op(dve.tensor_scalar(nmx[:, :], mx[:, :], -X_SCALE, None, ALU.mult), L["x_negmax"], h + 1)
                    dve.wait_ge(L["x_exp"], TT * (h + 1))
                    op(dve.reciprocal(rinv[:, :], rsum[:, :]))
                    for a in range(TT):
                        ins = dve.tensor_scalar(prob[:, a, :], prob[:, a, :], rinv[:, a:a + 1], None, ALU.mult)
                        op(ins, L["x_prob"], h + 1) if a else op(ins)
                    dve.wait_ge(L["x_o"], h + 1)
                    op(dve.tensor_copy(aT[:, 2 * h:2 * h + 2, :].rearrange("p c s -> p (c s)"), bank[7][:, :]), L["x_o_sb"], h + 1)
                add_to_x("x_wo")
                norm(2)
                turn_odd("ffn_t", hT, "norm_ffn")

                def ff_hid(tiles, w, n, n_up):
                    for a in range(tiles):
                        dve.wait_ge(L["silu_done"], n + a + 1)
                        dve.wait_ge(L["up_ps"], n_up + a + 1)
                        dve.tensor_tensor(hid[:, a, 0:w], sg[:, a, 0:w], bank[(1, 6)[a]][:, 0:w], ALU.mult)\
                            .then_inc(L["hid_ready"], 1)

                def ff_add(tiles, n, n_y, dst):
                    for a in range(tiles):
                        for c in range(2):
                            dve.wait_ge(L["y_ps"], n_y + 2 * a + c + 1)
                            s_ = slice(c * 512, (c + 1) * 512)
                            dve.tensor_tensor(dst(a)[:, s_], dst(a)[:, s_], bank[3 + c][:, :], ALU.add).then_inc(L["y_added"], 1)

                with dve.If(l == 0):
                    def w_of(i):
                        return HB if i < DENSE_STEPS - 1 else DENSE_TAIL

                    ff_hid(TT, HB, 0, 0)
                    for i in range(1, DENSE_STEPS):
                        ff_add(TT, TT * (i - 1), 2 * TT * (i - 1), lambda a: x[:, a, :])
                        ff_hid(TT, w_of(i), TT * i, TT * i)
                    ff_add(TT, None, 2 * TT * (DENSE_STEPS - 1), lambda a: x[:, a, :])
                    dve.wait_ge(L["y_added"], 2 * TT * DENSE_STEPS)
                with dve.Else():
                    dve.wait_ge(L["logit_ps"], 1)
                    op(dve.tensor_copy(logit[:, :, :].rearrange("p a e -> p (a e)"), bank[4][:, 0:TT * NE]))
                    for a in range(TT):
                        op(dve.max(top[:, a, :], logit[:, a, :]))
                        op(dve.max_index(topi[:, a, :], top[:, a, :], logit[:, a, :]))
                        op(dve.tensor_copy(topf[:, a, :], topi[:, a, :]))
                    ins = dve.tensor_tensor(tw[:, :, 0:1], top[:, :, 1:2], top[:, :, 0:1], ALU.subtract)
                    op(ins, L["top_e_in"], 1)
                    dve.wait_ge(L["top_e"], 1)
                    op(dve.tensor_scalar(tw[:, :, 1:2], tw[:, :, 0:1], 1.0, None, ALU.add))
                    op(dve.reciprocal(tw[:, :, 2:3], tw[:, :, 1:2]))
                    op(dve.tensor_tensor(tw[:, :, 3:4], tw[:, :, 0:1], tw[:, :, 2:3], ALU.mult))
                    for a in range(TT):
                        for r in range(2):
                            op(dve.tensor_scalar(oh[:, r, :], expert_no[:, :], topf[:, a, r:r + 1], None, ALU.is_equal))
                        op(dve.tensor_tensor(chosen[:, a, :], oh[:, 0, :], oh[:, 1, :], ALU.add))
                        op(dve.tensor_scalar(oh[:, 0, :], oh[:, 0, :], tw[:, a, 2:3], None, ALU.mult))
                        ins = dve.scalar_tensor_tensor(gates[:, a, :], oh[:, 1, :], tw[:, a, 3:4], oh[:, 0, :], ALU.mult, ALU.add)
                        op(ins, L["count_in"], 1) if a == TT - 1 else op(ins)
                    dve.wait_ge(L["count_ps"], 1)
                    op(dve.tensor_copy(place[:, :, :].rearrange("p a e -> p (a e)"), bank[5][:, 0:TT * NE]))
                    op(dve.tensor_reduce(most[:, 0:1], bank[5][:, TT * NE:(TT + 1) * NE], axis=AX.X, op=ALU.max))
                    op(dve.tensor_scalar(npass_i[:, :], most[:, 0:1], float(P), 1.0, ALU.is_gt, ALU.add), L["npass_ready"], 1)
                    npass = dve.value_load(npass_i[0:1, 0:1], min_val=1, max_val=TT)
                    dve.wait_ge(L["gain_in"], 16)
                    for a in range(TT):
                        op(dve.tensor_tensor(xn[:, a, :], xn[:, a, :], gain, ALU.mult))
                    dve.sem_inc(L["y_added"], 1)
                    with dve.Fori(0, npass) as ps_:
                        with dve.Fori(0, NE) as e:
                            q = ps_ * NE + e
                            for a in range(TT):
                                col = bass.ds(e, 1)
                                dve.tensor_copy(place_p[:, a, 0:1], place[:, a, col])
                                dve.tensor_copy(place_p[:, a, 1:2], chosen[:, a, col])
                                dve.tensor_copy(place_p[:, a, 2:3], gates[:, a, col]).then_inc(dve_q, 1)
                            dve.wait_ge(dve_q, q * Q_STEPS + TT)
                            for a in range(TT):
                                dve.tensor_scalar(onehot[:, a, :], slot_no[:, :], place_p[:, a, 0:1], place_p[:, a, 1:2],
                                                  ALU.is_equal, ALU.mult).then_inc(dve_q, 1)
                            dve.wait_ge(dve_q, q * Q_STEPS + 2 * TT)
                            for a in range(TT):
                                dve.tensor_scalar(gated[:, a, :], onehot[:, a, :], place_p[:, a, 2:3], None, ALU.mult)\
                                    .then_inc(dve_q, 1)
                            dve.wait_ge(dve_q, q * Q_STEPS + 3 * TT)
                            dve.memset(yacc, 0.0).then_inc(L["onehot_ready"], 1)
                            dve.wait_ge(L["onehot_ready"], q + 1)
                            ff_hid(1, HB, q * MOE_STEPS, q * MOE_STEPS + 1)
                            with dve.Fori(1, MOE_STEPS) as i:
                                k_ = q * MOE_STEPS + i
                                ff_add(1, None, 2 * (k_ - 1) + 1, lambda a: yacc)
                                ff_hid(1, HB, k_, k_ + 1)
                            k_ = q * MOE_STEPS + MOE_STEPS
                            ff_add(1, None, 2 * (k_ - 1) + 1, lambda a: yacc)
                            dve.wait_ge(L["scatter_ps"], q + 1)
                            for a in range(TT):
                                for c in range(2):
                                    s_ = slice(c * 512, (c + 1) * 512)
                                    ins = dve.tensor_tensor(x[:, a, s_], x[:, a, s_], bank[(5, 6, 7, 2)[2 * a + c]][:, :], ALU.add)
                            ins.then_inc(L["scattered"], 1)
                            dve.wait_ge(L["scattered"], q + 1)
                        dve.tensor_scalar(place[:, :, :], place[:, :, :], -float(P), None, ALU.add).then_inc(dve_p, 1)
                        dve.wait_ge(dve_p, ps_ + 1)
                dve.nop()
                layer_end(dve, l)
            dve.wait_ge(fin_sq, 2)
            dve.tensor_scalar(ssum2[:, :], ssum2[:, :], 1.0 / D, EPS, ALU.mult, ALU.add).then_inc(fin_var, 1)
            dve.wait_ge(fin_root, 1)
            dve.reciprocal(rstd2[:, :], rstd2[:, :]).then_inc(fin_var, 1)
            dve.wait_ge(fin_var, 2)
            dve.wait_ge(last_in, 16)
            for a in range(TT):
                dve.scalar_tensor_tensor(xn[:, a, :], x[:, a, :], rstd2[:, a:a + 1], junk[:, :], ALU.mult, ALU.mult)\
                    .then_inc(fin_out, 1)


_INS = ["x", "mem", "norm_mix", "w_in", "gla_gk_up", "gla_gk_bias", "gla_norm", "m_conv", "m_gate_bias", "m_norm",
        "gla_proj", "m_proj", "w_out", "norm_xattn", "norm_mem", "x_wq", "x_wkv", "x_wo", "norm_ffn",
        "ffn_w13", "ffn_w2", "moe_router", "moe_w13", "moe_w2", "norm_final"]


def kernel(**inputs):
    import numpy as _np
    import concourse.bacc as _bacc
    from concourse import mybir as _mybir
    from concourse.bass_utils import run_bass_kernel_spmd as _run

    nc = _bacc.Bacc("TRN2", target_bir_lowering=False, num_devices=1)
    arrays, tensors = {}, {}
    for name in _INS:
        a = _np.ascontiguousarray(inputs[name])
        arrays[f"in_{name}_dram"] = a
        tensors[name] = nc.dram_tensor(f"in_{name}_dram", a.shape, _mybir.dt.from_np(a.dtype), kind="ExternalInput").ap()
    out = nc.dram_tensor("out_0_dram", (1, S, D), F32, kind="ExternalOutput").ap()
    hybrid_decoder_kernel(nc, tensors, out)
    r = _run(nc, [arrays], core_ids=[0])
    return r.results[0]["out_0_dram"]
```

```python
import numpy as np
import concourse.bass as bass
from concourse import mybir
from concourse.alu_op_type import AluOpType as ALU
from contextlib import ExitStack

F32 = mybir.dt.float32
F32R = mybir.dt.float32r
U32 = mybir.dt.uint32
I32 = mybir.dt.int32
ACT = mybir.ActivationFunctionType
AX = mybir.AxisListType

P = 128
S = 256
M = 256
D = 1024
TT = S // P
KC = D // P
DEPTH = 2
EPS = 1e-6
HEADS = 4
DK = 128
DV = 256
CH = 64
NCH = S // CH
RANK = 16
CONV_W = 4
FFN = 64 * ((8 * D // 3 + 63) // 64)
NE = 8
EXP = 7 * D // 2
HB = 512
DENSE_STEPS = (FFN + HB - 1) // HB
DENSE_TAIL = FFN - (DENSE_STEPS - 1) * HB
MOE_STEPS = EXP // HB
GATE_NORM = 16.0
LOG_DECAY_MIN = -1.0
QK_SCALE = DK ** -0.5
X_SCALE = (D // HEADS) ** -0.5
BIG = 1e30

OFF = {}
_at = 0
for _name, _w in (("g_q", 512), ("g_k", 512), ("g_v", D), ("g_lr", RANK), ("g_g", D), ("m_q", 512), ("m_k", 512),
                  ("m_v", D), ("m_i", HEADS), ("m_f", HEADS), ("m_o", D), ("a_gla", D), ("a_m", D)):
    OFF[_name] = _at
    _at += _w
N_IN = _at

BLOCKS = [(name, j) for name, n in (("g_q", 1), ("g_k", 1), ("m_q", 1), ("m_k", 1), ("g_v", 2), ("m_v", 2), ("g_g", 2),
                                    ("m_o", 2), ("a_gla", 2), ("a_m", 2), ("gla_proj", 2), ("m_proj", 2), ("w_out", 2),
                                    ("x_wk", 2), ("x_wv", 2), ("x_wq", 2), ("x_wo", 2)) for j in range(n)]
COLUMN_BLOCKS = ("g_q", "g_k", "m_q", "m_k", "x_wk", "x_wq")

PIECES = 4
HALF = KC * 512 // 2
PIECE = HALF // 2
RAW = 3
SPLIT = 3
MIX_BLOCKS = len(BLOCKS)
DENSE_BLOCKS = 3 * DENSE_STEPS
MOE_BLOCKS = 3 * MOE_STEPS
assert 2 * MIX_BLOCKS % RAW == 2 * DENSE_BLOCKS % RAW == 2 * MOE_BLOCKS % RAW == 0
assert DENSE_STEPS != MOE_STEPS
assert PIECES * MIX_BLOCKS % SPLIT == PIECES * DENSE_BLOCKS % SPLIT == PIECES * MOE_BLOCKS % SPLIT == 0
LAYER_LOADS = 2 * (MIX_BLOCKS + DENSE_BLOCKS) // RAW

TURNS = ("mix_t", "gla_t", "m_t", "merged_t", "x_t", "ffn_t")

GROUP_BANKS = 2
GROUPS = {}
GAP_BLOCKS = range(8, 16)


def _plan():
    def add(*name):
        GROUPS[name] = len(GROUPS)

    def turned(name):
        for j in range(4):
            add(name, j)

    add("vec", 0)
    turned("mix_t")
    add("small", 0)
    add("small", 1)
    def blocks(numbers):
        for name, j in [BLOCKS[b] for b in numbers]:
            add(name, j, 0)
            add(name, j, 1)

    blocks(range(0, 2))
    add("decay", 0)
    add("decay", 1)
    blocks(range(2, 8))
    add("gate_cols", 0)
    blocks(GAP_BLOCKS)
    turned("gla_t")
    turned("m_t")
    blocks(range(16, 20))
    turned("merged_t")
    blocks(range(20, 26))
    turned("x_t")
    blocks(range(26, 30))
    turned("ffn_t")


_plan()


def ends_group(k, p):
    name, j = BLOCKS[k]
    if name in COLUMN_BLOCKS:
        return (name, j, p // 2) if p % 2 else None
    return (name, j, 1) if p == PIECES - 1 else None


_loose = [(k, p) for k in range(MIX_BLOCKS) for p in range(PIECES) if ends_group(k, p) is None]
LOOSE = {kp: n + 1 for n, kp in enumerate(_loose)}
MIX_LOOSE = len(LOOSE)

VEC = {}
_at = 0
for _name, _w in (("norm_mix", 8), ("gla_gk_bias", 4), ("gla_norm", 8), ("m_conv", 32), ("m_norm", 8),
                  ("norm_xattn", 8), ("norm_mem", 8), ("norm_ffn", 8)):
    VEC[_name] = _at
    _at += _w
NVEC = _at


CONSTS = 22
VEC_DMAS = len(VEC) + 5
Q_STEPS = 3 * TT


class Steps:

    def __init__(self, eng, own):
        self.eng, self.own, self.n, self.last, self.base = eng, own, 0, None, 0

    def wait(self):
        if self.last is not None:
            self.eng.wait_ge(*self.last)

    def did(self, ins, sem=None, value=None):
        if sem is None:
            self.n += 1
            ins.then_inc(self.own, 1)
            self.last = (self.own, self.base + self.n)
        else:
            ins.then_inc(sem, 1)
            self.last = (sem, value)


def hybrid_decoder_kernel(nc, t, out):
    ctx = ExitStack()
    with ctx:
        def sb(name, shape, dt=F32):
            return ctx.enter_context(nc.sbuf_tensor("sb_" + name, shape, dt))

        def sem(name):
            return ctx.enter_context(nc.semaphore(name))

        bank = [ctx.enter_context(nc.psum_tensor(f"bank{i}", [P, 512], F32)) for i in range(8)]
        raw = sb("raw", [P, RAW, HALF])
        whi = sb("whi", [P, SPLIT, PIECE], F32R)
        wlo = sb("wlo", [P, SPLIT, PIECE], F32R)
        x = sb("x", [P, TT, D])
        xn = sb("xn", [P, TT, D])
        Hhi, Hlo = sb("Hhi", [P, KC, S], F32R), sb("Hlo", [P, KC, S], F32R)
        memhT = sb("memhT", [P, KC, M])
        heads_only = ExitStack()

        def hsb(name, shape):
            return heads_only.enter_context(nc.sbuf_tensor("sb_" + name, shape, F32))

        gkeT = hsb("gkeT", [P, HEADS, S])
        qk = hsb("qk", [P, KC, S])
        scratch = hsb("scratch", [P, 6, S])
        heads_only.close()
        Bhi, Blo = sb("Bhi", [P, KC, S], F32R), sb("Blo", [P, KC, S], F32R)
        sb("rest", [P, 2 * S])
        gqk = sb("gqk", [P, 2 * HEADS, S])
        gqT = gqk[:, 0:HEADS, :]
        gkT = gqk[:, HEADS:, :]
        cum = sb("cum", [P, HEADS, S])
        e1 = sb("e1", [P, HEADS, S])
        gv = sb("gv", [P, TT, D])
        gg = sb("gg", [P, TT, D])
        cin = sb("cin", [P, KC, CONV_W - 1 + S])
        mv = sb("mv", [P, TT, HEADS, DV + 1])
        mo = sb("mo", [P, TT, D])
        ag = sb("ag", [P, TT, D])
        am = sb("am", [P, TT, D])
        om = gqk[:, :, :].rearrange("p (a b) s -> p a (b s)", a=TT)
        junk = sb("junk", [P, D])
        ident = sb("ident", [P, P])
        tri = sb("tri", [P, P])
        ones = sb("ones", [P, P])
        slot_no = sb("slot_no", [P, P])
        expert_no = sb("expert_no", [P, NE])
        causal = sb("causal", [P, TT * P])
        hide = sb("hide", [P, TT * P])
        restart = sb("restart", [P, S])
        pick = sb("pick", [HEADS, HEADS, P])
        zrow = sb("zrow", [HEADS, CH])
        lnscale = sb("lnscale", [P, 1])
        vrow = sb("vrow", [NVEC, P])
        vcol = sb("vcol", [P, NVEC])
        wsmall = sb("wsmall", [P, KC, RANK + 2 * HEADS])
        wsmall_hi = sb("wsmall_hi", [P, KC, RANK + 2 * HEADS], F32R)
        wsmall_lo = sb("wsmall_lo", [P, KC, RANK + 2 * HEADS], F32R)
        gkup = sb("gkup", [RANK, 512])
        gbias = sb("gbias", [HEADS, 2])
        lrT = sb("lrT", [RANK, S])
        sT = sb("sT", [P, 2, TT * P])
        wT = scratch[:, 0:2, :]
        kn = scratch[:, 5, :].rearrange("p (a k) -> p a k", k=P)
        st = sb("st", [P, 3, DV + 1])
        qs = scratch[:, 2:4, :]
        dexp = scratch[:, 4, :]
        ssum = sb("ssum", [P, 2, TT * HEADS])
        rstd = sb("rstd", [P, 2, TT * HEADS])
        ssum2 = sb("ssum2", [P, TT])
        rstd2 = sb("rstd2", [P, TT])
        den = sb("den", [P, TT])
        rows = sb("rows", [P, S])
        mrow = sb("mrow", [HEADS, S + NCH])
        grow = am[0:HEADS, :, :].rearrange("p a (r s) -> p (a r) s", s=S)
        mst = sb("mst", [HEADS, NCH + 1])
        cols = sb("cols", [P, TT, P])
        sdec = sb("sdec", [P, HEADS, NCH])
        kT = gg[:, :, :].rearrange("p a (b c) -> p (a b) c", c=S)
        prob = e1[:, :, :].rearrange("p (r a) m -> p r a m", r=2)
        probT = cum[:, 0:TT, :]
        mx = sb("mx", [P, TT])
        nmx = sb("nmx", [P, 2, TT])
        rsum = sb("rsum", [P, 2, TT])
        rinv = sb("rinv", [P, TT])
        xqT = gqk
        sg = mo[:, :, 0:HB]
        hid = am[:, :, 0:HB]
        hidT = [f[:, 0:4, :].rearrange("p (t c) s -> p t (c s)", t=TT) for f in (Hhi, Hlo)]
        hg = [[f[:, :, r * P:(r + 1) * P] for f in (Bhi, Blo)] for r in range(2)]
        yacc = gv[:, 0, :]
        onehot = gg[:, 0, 0:TT * P].rearrange("p (t j) -> p t j", t=TT)
        gated = gg[:, 0, 256:256 + TT * P].rearrange("p (t j) -> p t j", t=TT)
        gatedT = gg[:, 0, 512:512 + S]
        gain = junk[:, :]
        rw = sb("rw", [P, KC, NE])
        logit = sb("logit", [P, TT, NE])
        top = sb("top", [P, TT, NE])
        topi = sb("topi", [P, TT, NE], U32)
        topf = sb("topf", [P, TT, NE])
        tw = sb("tw", [P, TT, 4])
        oh = sb("oh", [P, 2, NE])
        chosen = sb("chosen", [P, TT, NE + 1])
        gates = sb("gates", [P, TT, NE + 1])
        place = sb("place", [P, TT, NE + 1])
        place_p = sb("place_p", [P, TT, NE])
        most = sb("most", [P, 2])
        npass_i = sb("npass_i", [P, 1], I32)

        def is_columns(k):
            return k < MIX_BLOCKS and BLOCKS[k][0] in COLUMN_BLOCKS

        def raw_half(k, half, kind):
            cols = {"rows": 512, "columns": 256, "down": 1024}[kind]
            return raw[:, (2 * k + half) % RAW, :].rearrange("p (k n) -> p k n", n=cols)

        def raw_piece(k, p, kind, w=512):
            h = raw_half(k, p // 2, kind)
            if kind == "columns":
                return h[:, :, (p % 2) * P:(p % 2 + 1) * P]
            if kind == "rows":
                return h[:, 2 * (p % 2):2 * (p % 2) + 2, 0:w]
            return h[:, p % 2:p % 2 + 1, :]

        def split_piece(part, k, p, kind, w=512):
            cols = {"rows": 512, "columns": P, "down": 1024}[kind]
            v = part[:, (PIECES * k + p) % SPLIT, :].rearrange("p (k n) -> p k n", n=cols)
            return v[:, :, 0:w] if kind == "rows" else v

        def kind_of(k):
            if k < MIX_BLOCKS:
                return "columns" if is_columns(k) else "rows"
            f = k - MIX_BLOCKS
            return "down" if f >= 2 and (f % 3 == 0 or f == DENSE_BLOCKS - 1) else "rows"

        layer_sems = []

        def lsem(name):
            layer_sems.append(sem(name))
            return layer_sems[-1]

        pe_piece = lsem("pe_piece")
        hi_done, lo_done = lsem("hi_done"), lsem("lo_done")
        pe_group = lsem("pe_group")
        moved = [lsem(f"moved{b}") for b in range(GROUP_BANKS)]
        dve_own, act_own, pool_own = lsem("dve_own"), lsem("act_own"), lsem("pool_own")
        L = {n: lsem(n) for n in (
            "sq_done", "var_done", "root_done", "xn_ready", "decay_z", "decay_e", "cum_ready", "e_ready", "gla_in",
            "conv_out", "qk_ready", "row_abs", "row_ln", "row_dm", "row_exp", "rows_ready", "values_ready",
            "h_scores", "h_masked", "h_keys", "h_keys_sb", "h_dstate", "h_state", "h_out", "h_outsb",
            "h_bcast", "h_dexp_in", "h_dexp", "h_qs", "h_den", "h_sq",
            "norm_var", "norm_root", "gated_g", "gated_m", "gate_z",
            "turn_hi", "small_hi", "small_lo",
            "mem_hi", "mem_t", "x_score", "x_negmax", "x_exp", "x_prob", "x_pt", "x_pt_sb", "x_o", "x_o_hi", "x_o_sb",
            "gate_ps", "up_ps", "silu_done", "hid_ready", "hid_tr", "hidT_hi", "hidT_ready", "y_ps", "y_done",
            "logit_ps", "count_in", "top_e_in", "top_e", "count_ps", "npass_ready", "onehot_ready", "gather_ps", "gather_hi",
            "gather_sb", "gated_ps", "gated_sb", "y_left", "y_right", "scatter_ps", "scattered", "gain_in", "pool_in_layer")}
        vec_in = sem("vec_in")
        router_in = sem("router_in")
        x_in = sem("x_in")
        mem_in = sem("mem_in")
        const_ready = sem("const_ready")
        last_in = sem("last_in")
        full = [sem(f"full{s}") for s in range(RAW)]
        layer_done = sem("layer_done")
        layer_go = sem("layer_go")
        layer_seen = sem("layer_seen")
        mem_ready = sem("mem_ready")
        mem_sq = sem("mem_sq")
        mem_var = sem("mem_var")
        mem_root = sem("mem_root")
        mem_n = sem("mem_n")
        mem_tp = sem("mem_tp")
        fin_sq, fin_var, fin_root, fin_out, out_done = sem("fin_sq"), sem("fin_var"), sem("fin_root"), sem("fin_out"), sem("out_done")
        ENGINES = 5
        dve_q, dve_p = lsem("dve_q"), lsem("dve_p")

        def group(*name):
            g = GROUPS[name]
            return bank[g % GROUP_BANKS], moved[g % GROUP_BANKS], g // GROUP_BANKS + 1

        def wait_group(eng, *name):
            eng.wait_ge(pe_group, GROUPS[name] + 1)

        def wait_moved(eng, *name):
            g = GROUPS[name]
            eng.wait_ge(moved[g % GROUP_BANKS], g // GROUP_BANKS + 1)

        def wait_full(eng, l, k, p, steps=0):
            half = 2 * k + p // 2
            n = l * LAYER_LOADS + steps * (6 // RAW) + (half // RAW + 1)
            eng.wait_ge(full[half % RAW], n * 16)

        def wait_used(eng, k, p):
            g = ends_group(k, p)
            if g is None:
                eng.wait_ge(pe_piece, LOOSE[(k, p)])
            else:
                wait_group(eng, *g)

        def ahead(k, p):
            s = PIECES * k + p + SPLIT
            return s // PIECES, s % PIECES

        def step_of(f, steps):
            if f < 2:
                return ("gate", "up")[f], 0
            if f == 3 * steps - 1:
                return "down", steps - 1
            if steps == MOE_STEPS and f >= 3 * steps - 3:
                return ("up", steps - 1) if f == 3 * steps - 3 else ("down", steps - 2)
            return ("gate", "down", "up")[(f + 1) % 3], (f + 1) // 3 - ((f + 1) % 3 == 1)

        def wait_piece(eng, f, p, steps, before=0, before_steps=0):
            what, i = step_of(f, steps)
            last = dense_pieces(f) - 1 if steps == DENSE_STEPS else PIECES - 1
            if p < last:
                eng.wait_ge(pe_piece, (before + before_steps) * (3 * (PIECES - 1)) + (MIX_LOOSE + f * (PIECES - 1) + p + 1))
            else:
                done = L[{"gate": "gate_ps", "up": "up_ps", "down": "y_ps"}[what]]
                eng.wait_ge(done, before + before_steps + (i + 1))

        def dense_width(i):
            return HB if i < DENSE_STEPS - 1 else DENSE_TAIL

        def dense_pieces(f):
            return (DENSE_TAIL + P - 1) // P if f == DENSE_BLOCKS - 1 else PIECES

        def dense_ahead(f, p):
            f, p = ahead(f, p)
            if f >= DENSE_BLOCKS or p >= dense_pieces(f):
                return None
            what, i = step_of(f, DENSE_STEPS)
            if what != "down":
                return f, p, "rows", dense_width(i), P, p
            tail = i == DENSE_STEPS - 1
            return f, p, "down", None, min(P, DENSE_TAIL - p * P) if tail else P, 2 * p if tail else p

        def wait_lo(eng, f, p, more=0):
            eng.wait_ge(hi_done, more + (PIECES * (MIX_BLOCKS + f) + p + 1))

        def moe_kind(f):
            return "down" if step_of(f, MOE_STEPS)[0] == "down" and f < MOE_BLOCKS else "rows"

        block = ctx.enter_context(nc.Block())

        def layer_end(eng, l, last=None):
            eng.wait_ge(L["pool_in_layer"], 1)
            eng.drain().then_inc(layer_done, 1)
            eng.wait_ge(layer_go, 1)
            eng.sem_inc(layer_seen, 1)

        @block.sync
        def _(sp):
            sp.dma_start(x[:, :, :], t["x"][0].rearrange("(a p) d -> p a d", p=P)).then_inc(x_in, 16)

            def load(l, k, half):
                name, j = BLOCKS[k]
                if name in OFF:
                    src, col = t["w_in"][l], OFF[name] + 512 * j
                elif name == "x_wk":
                    src, col = t["x_wkv"][l], 512 * j
                elif name == "x_wv":
                    src, col = t["x_wkv"][l], D + 512 * j
                else:
                    src, col = t[name][l], 512 * j
                if is_columns(k):
                    a = src[:, col + 256 * half:col + 256 * (half + 1)]
                else:
                    a = src[512 * half:512 * (half + 1), col:col + 512]
                sp.dma_start(raw_half(k, half, kind_of(k)), a.rearrange("(k p) n -> p k n", p=P))\
                    .then_inc(full[(2 * k + half) % RAW], 16)

            def wait_free(k, half, expert=None):
                n = 2 * (2 * k + half - RAW) + 2
                if expert is not None:
                    n = n + expert * (PIECES * MOE_BLOCKS)
                sp.wait_ge(lo_done, n)

            for n in range(RAW):
                load(0, n // 2, n % 2)
            with sp.Fori(0, DEPTH) as l:
                for n in range(RAW, 2 * MIX_BLOCKS):
                    wait_free(n // 2, n % 2)
                    load(l, n // 2, n % 2)
                with sp.If(l == 0):
                    def dense_load(f, what, i):
                        k = MIX_BLOCKS + f
                        w = HB if i < DENSE_STEPS - 1 else DENSE_TAIL
                        for half in range(2):
                            wait_free(k, half)
                            slot = full[(2 * k + half) % RAW]
                            if what != "down":
                                col = HB * i + (FFN if what == "up" else 0)
                                sp.dma_start(raw_half(k, half, "rows")[:, :, 0:w],
                                             t["ffn_w13"][0, 512 * half:512 * (half + 1), col:col + w].rearrange(
                                                 "(k p) n -> p k n", p=P)).then_inc(slot, 16)
                            elif w == HB:
                                row = HB * i + 256 * half
                                sp.dma_start(raw_half(k, half, "down"), t["ffn_w2"][0, row:row + 256, :].rearrange(
                                    "(k p) n -> p k n", p=P)).then_inc(slot, 16)
                            else:
                                row = HB * i + P * half
                                m = min(P, w - P * half)
                                sp.dma_start(raw_half(k, 0, "down")[0:m, half, :], t["ffn_w2"][0, row:row + m, :])\
                                    .then_inc(slot, 16)

                    dense_load(0, "gate", 0)
                    dense_load(1, "up", 0)
                    for i in range(1, DENSE_STEPS):
                        dense_load(3 * i - 1, "gate", i)
                        dense_load(3 * i, "down", i - 1)
                        dense_load(3 * i + 1, "up", i)
                    dense_load(DENSE_BLOCKS - 1, "down", DENSE_STEPS - 1)
                    sp.wait_ge(lo_done, PIECES * (MIX_BLOCKS + DENSE_BLOCKS - 1) + 2)
                    for n in range(RAW):
                        load(1, n // 2, n % 2)
                with sp.Else():
                    def moe_load(q, e, f, what, i, base=None):
                        k = MIX_BLOCKS + f
                        for half in range(2):
                            n = q * (PIECES * MOE_BLOCKS) + 2 * (2 * k + half - RAW) + 2
                            if base is not None:
                                n = n + base * (3 * PIECES)
                            sp.wait_ge(lo_done, n)
                            slot = full[(2 * k + half) % RAW]
                            if what == "down":
                                src = t["moe_w2"][0, e, bass.ts(i, HB), :][256 * half:256 * (half + 1), :]
                            elif what == "up":
                                src = t["moe_w13"][0, e, :, EXP:2 * EXP][512 * half:512 * (half + 1), bass.ts(i, HB)]
                            else:
                                src = t["moe_w13"][0, e, 512 * half:512 * (half + 1), bass.ts(i, HB)]
                            sp.dma_start(raw_half(k, half, "down" if what == "down" else "rows"),
                                         src.rearrange("(k p) n -> p k n", p=P)).then_inc(slot, 16)

                    moe_load(0, 0, 0, "gate", 0)
                    sp.wait_ge(L["npass_ready"], 1)
                    npass = sp.value_load(npass_i[0:1, 0:1], min_val=1, max_val=TT)
                    with sp.Fori(0, npass) as ps:
                        def expert(q, e):
                            moe_load(q, e, 1, "up", 0)
                            with sp.Fori(1, MOE_STEPS - 1) as i:
                                moe_load(q, e, 2, "gate", i, i - 1)
                                moe_load(q, e, 3, "down", i - 1, i - 1)
                                moe_load(q, e, 4, "up", i, i - 1)
                            moe_load(q, e, MOE_BLOCKS - 4, "gate", MOE_STEPS - 1)
                            moe_load(q, e, MOE_BLOCKS - 3, "up", MOE_STEPS - 1)
                            moe_load(q, e, MOE_BLOCKS - 2, "down", MOE_STEPS - 2)
                            moe_load(q, e, MOE_BLOCKS - 1, "down", MOE_STEPS - 1)

                        with sp.Fori(0, NE - 1) as e:
                            q = ps * NE + e
                            expert(q, e)
                            moe_load(q + 1, e + 1, 0, "gate", 0)
                        expert(ps * NE + (NE - 1), NE - 1)
                        moe_load(ps * NE + NE, 0, 0, "gate", 0)
                sp.nop()
                layer_end(sp, l)
            sp.wait_ge(fin_out, 2)
            sp.dma_start(out[0].rearrange("(a p) d -> p a d", p=P), xn[:, :, :]).then_inc(out_done, 16)
            sp.wait_ge(out_done, 16)

        @block.gpsimd
        def _(pool):
            n = [0]

            def did(ins):
                n[0] += 1
                ins.then_inc(const_ready, 1)

            def ordered():
                pool.wait_ge(const_ready, n[0])

            pool.dma_start(xn[:, :, :], t["mem"][0].rearrange("(a p) d -> p a d", p=P)).then_inc(mem_in, 16)
            did(pool.memset(ident[:, :], 0.0))
            did(pool.memset(tri[:, :], 1.0))
            did(pool.memset(ones[:, :], 1.0))
            did(pool.memset(causal[:, :], 1.0))
            did(pool.memset(restart[:, :], 1.0))
            did(pool.memset(pick[:, :, :], 0.0))
            did(pool.memset(zrow[:, :], 0.0))
            did(pool.memset(lnscale[:, :], float(np.log(QK_SCALE))))
            did(pool.memset(rows[:, :], 0.0))
            did(pool.memset(sT[:, :, :], 0.0))
            did(pool.memset(cin[:, :, 0:CONV_W - 1], 0.0))
            did(pool.memset(mv[:, :, :, DV:DV + 1], 1.0))
            did(pool.memset(mst[:, 0:1], 0.0))
            did(pool.iota(slot_no[:, :], [[1, P]], base=0, channel_multiplier=0, allow_small_or_imprecise_dtypes=True))
            did(pool.iota(expert_no[:, :], [[1, NE]], base=0, channel_multiplier=0, allow_small_or_imprecise_dtypes=True))
            ordered()
            did(pool.affine_select(out=ident[:, :], in_=ident[:, :], compare_op=ALU.not_equal, fill=1.0, base=0,
                                   pattern=[[-1, P]], channel_multiplier=1))
            did(pool.affine_select(out=tri[:, :], in_=tri[:, :], compare_op=ALU.is_gt, fill=0.0, base=0,
                                   pattern=[[1, P]], channel_multiplier=-1))
            did(pool.affine_select(out=causal[:, :].rearrange("p (a t) -> p a t", a=TT),
                                   in_=causal[:, :].rearrange("p (a t) -> p a t", a=TT), compare_op=ALU.is_ge, fill=0.0,
                                   base=0, pattern=[[0, TT], [1, P]], channel_multiplier=-1))
            ordered()
            v = causal[:, :].rearrange("p (a c t) -> p a c t", a=TT, c=2)
            did(pool.affine_select(out=v, in_=v, compare_op=ALU.is_ge, fill=0.0, base=0,
                                   pattern=[[0, TT], [-CH, 2], [0, CH]], channel_multiplier=1))
            v = restart[:, :].rearrange("p (c t) -> p c t", t=CH)
            did(pool.affine_select(out=v, in_=v, compare_op=ALU.not_equal, fill=0.0, base=0,
                                   pattern=[[0, NCH], [1, CH]], channel_multiplier=0))
            did(pool.affine_select(out=pick[:, :, :], in_=pick[:, :, :], compare_op=ALU.not_equal, fill=1.0, base=0,
                                   pattern=[[-1, HEADS], [0, P]], channel_multiplier=1))
            ordered()
            did(pool.tensor_scalar(hide[:, :], causal[:, :], -BIG, BIG, ALU.mult, ALU.add))
            ordered()
            assert n[0] == CONSTS, n[0]

            def small_inputs(l):
                for name in VEC:
                    rows_of = {"m_conv": CONV_W * KC, "gla_gk_bias": HEADS}.get(name, KC)
                    src = t[name][l]
                    src = src.rearrange("j (c p) -> (j c) p", p=P) if name == "m_conv" else src.rearrange("(c p) -> c p", p=P)
                    pool.dma_start(vrow[VEC[name]:VEC[name] + rows_of, :], src).then_inc(vec_in, 16)
                pool.dma_start(wsmall[:, :, 0:RANK], t["w_in"][l, :, OFF["g_lr"]:OFF["g_lr"] + RANK].rearrange(
                    "(k p) n -> p k n", p=P)).then_inc(vec_in, 16)
                pool.dma_start(wsmall[:, :, RANK:], t["w_in"][l, :, OFF["m_i"]:OFF["m_i"] + 2 * HEADS].rearrange(
                    "(k p) n -> p k n", p=P)).then_inc(vec_in, 16)
                pool.dma_start(gkup[:, :], t["gla_gk_up"][l]).then_inc(vec_in, 16)
                for c in range(2):
                    pool.dma_start(gbias[:, c:c + 1], t["m_gate_bias"][l, c * HEADS:(c + 1) * HEADS].rearrange(
                        "(h o) -> h o", o=1)).then_inc(vec_in, 16)

            small_inputs(0)
            pool.dma_start(rw[:, :, :], t["moe_router"][0].rearrange("(k p) e -> p k e", p=P)).then_inc(router_in, 16)
            with pool.Fori(0, DEPTH) as l:
                pool.sem_inc(L["pool_in_layer"], 1)
                pool.wait_ge(pe_group, GROUPS[("decay", 1)] + 1)
                pool.wait_ge(L["row_dm"], 1)
                with pool.If(l == 0):
                    small_inputs(1)
                pool.wait_ge(layer_done, ENGINES - 1)
                for s_ in layer_sems:
                    pool.sem_clear(s_)
                pool.sem_clear(layer_done)
                pool.sem_inc(layer_go, 1)
                pool.wait_ge(layer_seen, ENGINES - 1)
                pool.sem_clear(layer_go)
                pool.sem_clear(layer_seen)

        @block.tensor
        def _(pe):
            pe.wait_ge(const_ready, CONSTS)

            def turn_mem():
                pe.wait_ge(mem_n, 2)
                for j in range(4):
                    for k in range(2):
                        for a in range(TT):
                            ins = pe.transpose(bank[j][:, (k * TT + a) * P:(k * TT + a + 1) * P],
                                               gg[:, a, (2 * j + k) * P:(2 * j + k + 1) * P], ident[:, :])
                    ins.then_inc(mem_tp, 1)
                pe.wait_ge(mem_ready, 4)

            turn_mem()

            with pe.Fori(0, DEPTH) as l:
                def begin(*name):
                    g = GROUPS[name]
                    if g >= GROUP_BANKS:
                        pe.wait_ge(moved[g % GROUP_BANKS], g // GROUP_BANKS)
                    return bank[g % GROUP_BANKS]

                def end(ins):
                    ins.then_inc(pe_group, 1)

                def turn(name, src):
                    for j in range(4):
                        b = begin(name, j)
                        for k in range(2):
                            for a in range(TT):
                                ins = pe.transpose(b[:, (k * TT + a) * P:(k * TT + a + 1) * P],
                                                   src[:, a, (2 * j + k) * P:(2 * j + k + 1) * P], ident[:, :])
                        end(ins)

                def turned(name):
                    for j in range(4):
                        wait_moved(pe, name, j)

                def product(ps, moving, stationary, start, stop):
                    pe.matmul(ps, stationary[0], moving[0], start=start, stop=False)
                    pe.matmul(ps, stationary[0], moving[1], start=False, stop=False)
                    return pe.matmul(ps, stationary[1], moving[0], start=False, stop=stop)

                def both(pair, *index):
                    return [f[index] for f in pair]

                ALL = slice(None)

                H, B = (Hhi, Hlo), (Bhi, Blo)

                def weights(k, p, kind, w=512):
                    return [split_piece(f, k, p, kind, w) for f in (whi, wlo)]

                def rows_out(k, src, turn_name=None, before=None, after=None):
                    name, j = BLOCKS[k]
                    for p in range(PIECES):
                        if before is not None:
                            before(p)
                        if turn_name is not None:
                            wait_moved(pe, turn_name, p)
                        pe.wait_ge(lo_done, PIECES * k + p + 1)
                        w = weights(k, p, "rows")
                        for a in range(TT):
                            ps = begin(name, j, a) if p == 0 else bank[GROUPS[(name, j, a)] % GROUP_BANKS]
                            for c in range(2):
                                ins = product(ps[:, :], both(w, ALL, c, ALL),
                                              both(src, ALL, 2 * p + c, slice(a * P, (a + 1) * P)),
                                              start=(p == 0 and c == 0), stop=(p == PIECES - 1 and c == 1))
                            if p == PIECES - 1:
                                end(ins)
                        if p < PIECES - 1:
                            ins.then_inc(pe_piece, 1)
                        if after is not None:
                            after(p)

                def channels_out(k, src):
                    name, j = BLOCKS[k]
                    for p in range(PIECES):
                        pe.wait_ge(lo_done, PIECES * k + p + 1)
                        w = weights(k, p, "columns")
                        ps = begin(name, j, p // 2) if p % 2 == 0 else bank[GROUPS[(name, j, p // 2)] % GROUP_BANKS]
                        for c in range(KC):
                            ins = product(ps[:, (p % 2) * S:(p % 2 + 1) * S], both(src, ALL, c, ALL), both(w, ALL, c, ALL),
                                          start=(c == 0), stop=(c == KC - 1))
                        if p % 2:
                            end(ins)
                        else:
                            ins.then_inc(pe_piece, 1)

                pe.wait_ge(vec_in, VEC_DMAS * 16 * (l + 1))
                end(pe.transpose(begin("vec", 0)[:, 0:NVEC], vrow[:, :], ident[0:NVEC, 0:NVEC]))
                pe.wait_ge(L["xn_ready"], 1)
                turn("mix_t", xn)
                turned("mix_t")
                pe.wait_ge(L["small_lo"], 1)
                small = (wsmall_hi, wsmall_lo)
                ps = begin("small", 0)
                for k in range(KC):
                    product(ps[0:RANK, 0:S], both(H, ALL, k, ALL), both(small, ALL, k, slice(0, RANK)),
                            start=(k == 0), stop=(k == KC - 1))
                for k in range(KC):
                    ins = product(ps[0:HEADS, S:2 * S], both(H, ALL, k, ALL), both(small, ALL, k, slice(RANK, RANK + HEADS)),
                                  start=(k == 0), stop=(k == KC - 1))
                end(ins)
                ps = begin("small", 1)
                for k in range(KC):
                    ins = product(ps[0:HEADS, 0:S], both(H, ALL, k, ALL),
                                  both(small, ALL, k, slice(RANK + HEADS, RANK + 2 * HEADS)),
                                  start=(k == 0), stop=(k == KC - 1))
                end(ins)
                channels_out(0, H)
                channels_out(1, H)
                wait_moved(pe, "small", 0)
                for a in range(2):
                    ps = begin("decay", a)
                    for c in range(2):
                        ins = pe.matmul(ps[:, c * S:(c + 1) * S], gkup[:, (2 * a + c) * P:(2 * a + c + 1) * P], lrT[:, :],
                                        start=True, stop=True)
                    end(ins)
                channels_out(2, H)
                channels_out(3, H)
                for k in range(4, 8):
                    rows_out(k, H)
                pe.wait_ge(L["rows_ready"], 1)
                ps = begin("gate_cols", 0)
                for a in range(TT):
                    ins = pe.transpose(ps[:, a * P:(a + 1) * P], rows[:, a * P:(a + 1) * P], ident[:, :])
                end(ins)

                def head_scores(n):
                    h = n % HEADS
                    if n == 0:
                        pe.wait_ge(L["gla_in"], 1)
                    if n == HEADS:
                        pe.wait_ge(L["qk_ready"], 1)
                    if n > 0:
                        pe.wait_ge(L["h_masked"], n)
                    q_, k_, turned_ = ((gqT[:, h, :], gkT[:, h, :], gkeT[:, h, :]) if n < HEADS else
                                       (qk[:, h, :], qk[:, HEADS + h, :], qk[:, HEADS + h, :]))
                    for a in range(TT):
                        pe.matmul(bank[2][:, a * P:(a + 1) * P], k_[:, a * P:(a + 1) * P], q_[:, a * P:(a + 1) * P],
                                  start=True, stop=True)
                    for a in range(TT):
                        ins = pe.transpose(bank[2][:, (TT + a) * P:(TT + a + 1) * P], turned_[:, a * P:(a + 1) * P],
                                           ident[:, :])
                    ins.then_inc(L["h_scores"], 1)
                    if n >= HEADS:
                        pe.wait_ge(L["h_state"], 3 * n - 1)
                        if n > HEADS:
                            pe.wait_ge(L["h_qs"], h)
                        pe.matmul(bank[3][:, 0:S + NCH], pick[:, h, :], mrow[:, :], start=True, stop=True)
                        pe.matmul(bank[4][:, 0:S], pick[:, h, :], grow[:, 5, :], start=True, stop=True)\
                            .then_inc(L["h_bcast"], 1)

                def head_values(n, r, a):
                    h = n % HEADS
                    return gv[r, a, h * DV:(h + 1) * DV] if n < HEADS else mv[r, a, h, :]

                def head_increments(n):
                    width = DV if n < HEADS else DV + 1
                    if n == 0:
                        for j in range(2):
                            for a in range(TT):
                                wait_moved(pe, "g_v", j, a)
                    if n == HEADS:
                        for j in range(2):
                            for a in range(TT):
                                wait_moved(pe, "m_v", j, a)
                    pe.wait_ge(L["h_keys_sb"], n + 1)
                    if n > 0:
                        pe.wait_ge(L["h_state"], 3 * n)
                    if n >= HEADS:
                        pe.wait_ge(L["h_qs"], n - HEADS + 1)
                    for c in range(NCH - 1):
                        r = slice((c % 2) * CH, (c % 2 + 1) * CH)
                        if c == 2:
                            pe.wait_ge(L["h_state"], 3 * n + 1)
                        pe.matmul(bank[(5, 3)[c % 2]][:, 0:width], kn[r, c // 2, :], head_values(n, r, c // 2),
                                  start=True, stop=True).then_inc(L["h_dstate"], 1)

                def head_outputs(n):
                    h = n % HEADS
                    width = DV if n < HEADS else DV + 1
                    weight = sT[:, n % 2, :] if n < HEADS else wT[:, n % 2, :]
                    query = gqT[:, h, :] if n < HEADS else qs[:, n % 2, :]
                    pe.wait_ge(L["h_masked"], n + 1)
                    if n > 0:
                        pe.wait_ge(L["h_outsb"], TT * n)
                    for a in range(TT):
                        for c in (2 * a, 2 * a + 1):
                            r = slice((c % 2) * CH, (c % 2 + 1) * CH)
                            ins = pe.matmul(bank[6 + a][r, 0:width], weight[r, c * CH:(c + 1) * CH], head_values(n, r, a),
                                            start=True, stop=(c == 0))
                            if c > 0:
                                pe.wait_ge(L["h_state"], 3 * n + c)
                                ins = pe.matmul(bank[6 + a][r, 0:width], query[:, c * CH:(c + 1) * CH], st[:, c - 1, 0:width],
                                                start=False, stop=True)
                        ins.then_inc(L["h_out"], 1)

                def gap(i):
                    if 0 <= i - 2 < 2 * HEADS:
                        head_outputs(i - 2)
                    if 0 <= i - 1 < 2 * HEADS:
                        head_increments(i - 1)
                    if i < 2 * HEADS:
                        head_scores(i)

                for k in GAP_BLOCKS:
                    rows_out(k, H, after=lambda p: gap(2 * (k - GAP_BLOCKS[0]) + p // 2) if p % 2 else None)

                pe.wait_ge(L["gated_g"], TT * HEADS)
                turn("gla_t", xn)
                pe.wait_ge(L["gated_m"], TT * HEADS)
                turn("m_t", om)
                for k in (16, 17):
                    rows_out(k, B, turn_name="gla_t")
                for k in (18, 19):
                    rows_out(k, H, turn_name="m_t")
                for a in range(TT):
                    wait_moved(pe, *BLOCKS[19], a)
                turn("merged_t", ag)
                for k in (20, 21):
                    rows_out(k, B, turn_name="merged_t")

                pe.wait_ge(L["mem_t"], KC)
                channels_out(22, H)
                channels_out(23, H)
                rows_out(24, H)
                rows_out(25, H)
                pe.wait_ge(L["xn_ready"], 2)
                turn("x_t", xn)
                turned("x_t")

                def scores(h):
                    for a in range(2):
                        wait_moved(pe, "x_wq", h // 2, a)
                    if h >= 2:
                        pe.wait_ge(L["x_exp"], TT * (h - 1))
                    for a in range(TT):
                        for c in range(2):
                            ins = pe.matmul(bank[4 + h % 2][:, a * M:(a + 1) * M], xqT[:, 2 * h + c, a * P:(a + 1) * P],
                                            kT[:, 2 * h + c, :], start=(c == 0), stop=(c == 1))
                    ins.then_inc(L["x_score"], 1)

                def turn_prob(h):
                    pe.wait_ge(L["x_prob"], h + 1)
                    if h > 0:
                        pe.wait_ge(L["x_pt_sb"], h)
                    for m in range(2):
                        for a in range(TT):
                            ins = pe.transpose(bank[6][:, (m * TT + a) * P:(m * TT + a + 1) * P],
                                               prob[:, h % 2, a, m * P:(m + 1) * P], ident[:, :])
                    ins.then_inc(L["x_pt"], 1)

                def attend(h):
                    pe.wait_ge(L["x_pt_sb"], h + 1)
                    if h > 0:
                        pe.wait_ge(L["x_o_sb"], h)
                    for c in range(2):
                        for m in range(2):
                            ins = pe.matmul(bank[7][:, c * S:(c + 1) * S],
                                            gv[:, m, h * DV + c * P:h * DV + (c + 1) * P], probT[:, m, :],
                                            start=(m == 0), stop=(m == 1))
                    ins.then_inc(L["x_o"], 1)

                channels_out(26, B)
                scores(0)
                scores(1)
                channels_out(27, B)
                turn_prob(0)
                scores(2)
                attend(0)
                turn_prob(1)
                scores(3)
                attend(1)

                def after_piece(p):
                    if p == 1:
                        attend(2)
                    if p == 2:
                        attend(3)
                    if p < 2:
                        turn_prob(p + 2)

                rows_out(28, H, before=lambda p: pe.wait_ge(L["x_o_sb"], p + 1), after=after_piece)
                rows_out(29, H)

                pe.wait_ge(L["xn_ready"], 3)
                turn("ffn_t", xn)
                turned("ffn_t")
                GATE, UP, Y = (0, 5), (1, 6), ((3, 4), (2, 7))

                def ff_wait(f, p, q):
                    n = PIECES * (MIX_BLOCKS + f) + p + 1
                    pe.wait_ge(lo_done, n if q is None else q + n)

                def ff_columns(f, src, banks, tiles, w, done, q=None, after=None):
                    for p in range(PIECES):
                        ff_wait(f, p, q)
                        wt = weights(MIX_BLOCKS + f, p, "rows", w)
                        for a in range(tiles):
                            for c in range(2):
                                ins = product(bank[banks[a]][:, 0:w], both(wt, ALL, c, ALL),
                                              both(src, ALL, 2 * p + c, slice(a * P, (a + 1) * P)),
                                              start=(p == 0 and c == 0), stop=(p == PIECES - 1 and c == 1))
                        ins.then_inc(pe_piece if p < PIECES - 1 else done, 1)
                        if after is not None:
                            after(p)

                def at_piece(n, work):
                    return lambda p: work() if p == n else None

                def ff_turn(tiles, w, n):
                    pe.wait_ge(L["hid_ready"], n + 1)
                    for a in range(tiles):
                        for k in range((w + P - 1) // P):
                            m = min(P, w - k * P)
                            ins = pe.transpose(bank[UP[a]][0:m, k * P:(k + 1) * P], hid[:, a, k * P:k * P + m], ident[:, :])
                    ins.then_inc(L["hid_tr"], 1)

                def ff_down(f, tiles, w, n, first, last, q=None, half=0, after=None):
                    pe.wait_ge(L["hidT_ready"], n + 1)
                    chunks = (w + P - 1) // P
                    for p in range(chunks):
                        ff_wait(f, p, q)
                        wt = weights(MIX_BLOCKS + f, p, "down")
                        m = min(P, w - p * P)
                        for a in range(tiles):
                            for c in range(2):
                                ins = product(bank[Y[a][c]][:, :], both(wt, slice(0, m), 0, slice(c * 512, (c + 1) * 512)),
                                              both(hidT, slice(0, m), a + half, slice(p * P, (p + 1) * P)),
                                              start=(first and p == 0), stop=(last and p == chunks - 1))
                        ins.then_inc(pe_piece if p < chunks - 1 else L["y_ps"], 1)
                        if after is not None:
                            after(p)

                with pe.If(l == 0):
                    def w_of(i):
                        return HB if i < DENSE_STEPS - 1 else DENSE_TAIL

                    ff_columns(0, B, GATE, TT, HB, L["gate_ps"])
                    ff_columns(1, B, UP, TT, HB, L["up_ps"])
                    for i in range(1, DENSE_STEPS):
                        pe.wait_ge(L["silu_done"], i)
                        ff_columns(3 * i - 1, B, GATE, TT, w_of(i), L["gate_ps"], after=at_piece(0, lambda: ff_turn(TT, HB, i - 1)))
                        ff_down(3 * i, TT, HB, i - 1, first=(i == 1), last=False)
                        ff_columns(3 * i + 1, B, UP, TT, w_of(i), L["up_ps"])
                    i = DENSE_STEPS
                    ff_turn(TT, DENSE_TAIL, i - 1)
                    ff_down(3 * i - 1, TT, DENSE_TAIL, i - 1, first=False, last=True)
                    pe.wait_ge(L["y_done"], 1)
                with pe.Else():
                    pe.wait_ge(router_in, 16)
                    for a in range(TT):
                        for k in range(KC):
                            for part in range(2):
                                ins = pe.matmul(bank[4][:, a * NE:(a + 1) * NE],
                                                B[part][:, k, a * P:(a + 1) * P].bitcast(F32), rw[:, k, :],
                                                start=(k == 0 and part == 0), stop=(k == KC - 1 and part == 1))
                    ins.then_inc(L["logit_ps"], 1)
                    pe.wait_ge(L["count_in"], 1)
                    pe.matmul(bank[5][:, 0:NE], tri[:, :], chosen[:, 0, 0:NE], start=True, stop=True)
                    pe.matmul(bank[5][:, NE:2 * NE], tri[:, :], chosen[:, 1, 0:NE], start=True, stop=False)
                    pe.matmul(bank[5][:, NE:2 * NE], ones[:, :], chosen[:, 0, 0:NE], start=False, stop=True)
                    pe.matmul(bank[5][:, 2 * NE:3 * NE], ones[:, :], chosen[:, 0, 0:NE], start=True, stop=False)
                    pe.matmul(bank[5][:, 2 * NE:3 * NE], ones[:, :], chosen[:, 1, 0:NE], start=False, stop=True)\
                        .then_inc(L["count_ps"], 1)
                    pe.wait_ge(L["npass_ready"], 1)
                    npass = pe.value_load(npass_i[0:1, 0:1], min_val=1, max_val=TT)

                    def gather(n):
                        pe.wait_ge(L["onehot_ready"], n + 1)
                        for k in range(KC):
                            for a in range(TT):
                                ins = pe.matmul(bank[5 + k // 4][:, (k % 4) * P:(k % 4 + 1) * P],
                                                xn[:, a, k * P:(k + 1) * P], onehot[:, a, :], start=(a == 0), stop=(a == 1))
                        ins.then_inc(L["gather_ps"], 1)

                    def scatter(n):
                        pe.wait_ge(L["gated_sb"], n + 1)
                        pe.wait_ge(L["y_left"], n + 1)
                        pe.wait_ge(L["y_right"], n + 1)
                        for a in range(TT):
                            for c in range(2):
                                ins = pe.matmul(bank[(5, 6, 7, 2)[2 * a + c]][:, :], gatedT[:, a * P:(a + 1) * P],
                                                yacc[:, c * 512:(c + 1) * 512], start=True, stop=True)
                        ins.then_inc(L["scatter_ps"], 1)

                    def expert(q, g, tokens):
                        at = q * (PIECES * MOE_BLOCKS)

                        def turn_gates():
                            pe.wait_ge(L["scattered"], q + 1)
                            for a in range(TT):
                                ins = pe.transpose(bank[7][:, a * P:(a + 1) * P], gated[:, a, :], ident[:, :])
                            ins.then_inc(L["gated_ps"], 1)

                        pe.wait_ge(L["gather_sb"], g + 1)
                        ff_columns(0, tokens, GATE, 1, HB, L["gate_ps"], at, at_piece(1, lambda: scatter(q)))
                        ff_columns(1, tokens, UP, 1, HB, L["up_ps"], at, at_piece(1, turn_gates))

                        def step(i, at, first):
                            n = q * MOE_STEPS + i
                            pe.wait_ge(L["silu_done"], n)
                            ff_columns(2, tokens, GATE, 1, HB, L["gate_ps"], at, at_piece(0, lambda: ff_turn(1, HB, n - 1)))
                            ff_down(3, 1, HB, n - 1, first, False, at)
                            ff_columns(4, tokens, UP, 1, HB, L["up_ps"], at)

                        step(1, at, True)
                        with pe.Fori(2, MOE_STEPS - 1) as i:
                            step(i, at + (i - 1) * (3 * PIECES), False)
                        n = q * MOE_STEPS + MOE_STEPS - 1
                        f = MOE_BLOCKS - 4
                        pe.wait_ge(L["silu_done"], n)
                        ff_columns(f, tokens, GATE, 1, HB, L["gate_ps"], at, at_piece(0, lambda: ff_turn(1, HB, n - 1)))
                        pe.wait_ge(L["hidT_ready"], n)
                        ff_columns(f + 1, tokens, UP, 1, HB, L["up_ps"], at, at_piece(1, lambda: gather(g + 1)))
                        ff_down(f + 2, 1, HB, n - 1, False, False, at, after=at_piece(0, lambda: ff_turn(1, HB, n)))
                        ff_down(f + 3, 1, HB, n, False, True, at, half=1)

                    with pe.Fori(0, npass) as ps_:
                        gather(ps_ * (NE + 1))
                        with pe.Fori(0, NE // 2) as pair:
                            for r in range(2):
                                e = 2 * pair + r
                                expert(ps_ * NE + e, ps_ * (NE + 1) + e, hg[r])
                        pe.wait_ge(L["gather_sb"], (ps_ + 1) * (NE + 1))
                    scatter(npass * NE)
                pe.nop()
                layer_end(pe, l)

        @block.scalar
        def _(act):
            step = Steps(act, act_own)
            act.wait_ge(const_ready, CONSTS)

            def chain(ins, sem=None, value=None):
                step.did(ins, sem, value)
                step.wait()

            act.wait_ge(mem_in, 16)
            for a in range(TT):
                act.activation(gv[:, a, :], xn[:, a, :], ACT.Square, accum_out=ssum2[:, a:a + 1]).then_inc(mem_sq, 1)
            act.wait_ge(mem_var, 1)
            act.activation(rstd2[:, :], ssum2[:, :], ACT.Sqrt).then_inc(mem_root, 1)
            act.wait_ge(mem_root, 1)
            act.wait_ge(x_in, 16)

            with act.Fori(0, DEPTH) as l:
                step.n, step.last = 0, None

                def squares(n):
                    for a in range(TT):
                        chain(act.activation(junk[:, :], x[:, a, :], ACT.Square, accum_out=ssum2[:, a:a + 1]),
                              L["sq_done"], TT * n + a + 1)
                    act.wait_ge(L["var_done"], n + 1)
                    chain(act.activation(rstd2[:, :], ssum2[:, :], ACT.Sqrt), L["root_done"], n + 1)

                def turn_hi(name, dst, gain_name):
                    for j in range(4):
                        ps, _, _ = group(name, j)
                        wait_group(act, name, j)
                        for k in range(2):
                            c = 2 * j + k
                            scale = vcol[:, VEC[gain_name] + c:VEC[gain_name] + c + 1] if gain_name else 1.0
                            ins = act.activation(dst[:, c, :], ps[:, k * S:(k + 1) * S], ACT.Copy, scale=scale)
                            chain(ins, L["turn_hi"], 4 * TURNS.index(name) + j + 1) if k else chain(ins)

                def split(k, p, kind, w=512, rows=P):
                    act.activation(split_piece(whi, k, p, kind, w)[0:rows], raw_piece(k, p, kind, w)[0:rows], ACT.Copy)\
                        .then_inc(hi_done, 1)

                def split_ahead(k, p):
                    wait_used(act, k, p)
                    k, p = ahead(k, p)
                    wait_full(act, l, k, p)
                    split(k, p, kind_of(k))

                def blocks(numbers, read, between=None):
                    for k in numbers:
                        name, j = BLOCKS[k]
                        for p in range(PIECES):
                            if read is not None and ends_group(k, p) is not None:
                                for a in ((p // 2,) if is_columns(k) else range(TT)):
                                    read(name, j, a)
                            split_ahead(k, p)
                            if between is not None:
                                between(k, p)

                def read_out(name, dst, func, **kw):
                    wait_group(act, *name)
                    ps, mv_, v = group(*name)
                    chain(act.activation(dst, ps[:, :], func, **kw), mv_, v)

                squares(0)
                act.wait_ge(vec_in, VEC_DMAS * 16 * (l + 1))
                act.activation(wsmall_hi[:, :, :], wsmall[:, :, :], ACT.Copy).then_inc(L["small_hi"], 1)
                for p in range(SPLIT):
                    wait_full(act, l, 0, p)
                    split(0, p, kind_of(0))
                wait_moved(act, "vec", 0)
                turn_hi("mix_t", Hhi, "norm_mix")
                ps, mv_, v = group("small", 0)
                wait_group(act, "small", 0)
                chain(act.activation(grow[:, 0, :], ps[0:HEADS, S:2 * S], ACT.Copy))
                chain(act.activation(lrT[:, :], ps[0:RANK, 0:S], ACT.Copy), mv_, v)
                def read_front(name, j, a):
                    ps, mv_, v = group(name, j, a)
                    wait_group(act, name, j, a)
                    rows_ = "p (c s) -> p c s"
                    if name in ("g_q", "g_k"):
                        dst = (gqT if name == "g_q" else gkT)[:, 2 * a:2 * a + 2, :]
                        src = ps[:, :].rearrange(rows_, c=2)
                    elif name in ("m_q", "m_k"):
                        c = (0 if name == "m_q" else 4) + 2 * a
                        dst = cin[:, c:c + 2, CONV_W - 1:]
                        src = ps[:, :].rearrange(rows_, c=2)
                    elif name == "g_v":
                        dst, src = gv[:, a, j * 512:(j + 1) * 512], ps[:, :]
                    else:
                        dst, src = mv[:, a, 2 * j:2 * j + 2, 0:DV], ps[:, :].rearrange("p (h v) -> p h v", h=2)
                    chain(act.activation(dst, src, ACT.Copy), mv_, v)

                def front(k, p):
                    if (k, p) == (1, 3):
                        act.wait_ge(L["decay_z"], 1)
                        chain(act.activation(e1[:, :, :], e1[:, :, :], ACT.Exp, scale=-1.0))
                        chain(act.activation(e1[:, :, :], e1[:, :, :], ACT.Ln, bias=1.0), L["decay_e"], 1)
                    if (k, p) == (2, 0):
                        act.wait_ge(L["gate_z"], 1)
                        chain(act.activation(grow[:, 2, :], grow[:, 2, :], ACT.Exp, scale=-1.0))
                        chain(act.activation(grow[:, 2, :], grow[:, 2, :], ACT.Ln, bias=1.0), L["row_ln"], 1)
                    if (k, p) == (2, 3):
                        act.wait_ge(L["cum_ready"], 1)
                        chain(act.activation(e1[:, :, :], gkeT[:, :, :], ACT.Exp))
                        chain(act.activation(cum[:, :, :], gkeT[:, :, :], ACT.Exp, scale=-1.0), L["e_ready"], 1)
                    if (k, p) == (5, 3):
                        act.wait_ge(L["row_dm"], 1)
                        chain(act.activation(grow[:, 5, :], grow[:, 4, :], ACT.Exp, scale=-1.0, bias=lnscale[0:HEADS, :]))
                        chain(act.activation(mrow[:, S:], grow[:, 4, CH - 1:S:CH], ACT.Exp, scale=-1.0))
                        chain(act.activation(rows[64:64 + HEADS, :], rows[64:64 + HEADS, :], ACT.Exp))
                        chain(act.activation(rows[96:96 + HEADS, :], rows[96:96 + HEADS, :], ACT.Exp, scale=-1.0),
                              L["rows_ready"], 1)
                    if (k, p) == (7, 1):
                        act.wait_ge(L["conv_out"], 1)
                        chain(act.activation(qk[:, :, :], qk[:, :, :], ACT.Silu), L["qk_ready"], 1)

                blocks(range(8), read_front, front)
                wait_moved(act, "gate_cols", 0)

                def head_outputs(n):
                    h = n % HEADS
                    for a in range(TT):
                        s_ = slice(a * HEADS + h, a * HEADS + h + 1)
                        if n < HEADS:
                            act.wait_ge(L["h_out"], TT * n + a + 1)
                            o = xn[:, a, h * DV:(h + 1) * DV]
                            chain(act.activation(o, bank[6 + a][:, 0:DV], ACT.Copy))
                        else:
                            act.wait_ge(L["h_den"], TT * h + a + 1)
                            o = om[:, a, h * DV:(h + 1) * DV]
                            chain(act.activation(o, bank[6 + a][:, 0:DV], ACT.Copy, scale=den[:, a:a + 1]))
                        chain(act.activation(junk[:, 0:DV], o, ACT.Square, accum_out=ssum[:, n // HEADS, s_]),
                              L["h_outsb"], TT * n + a + 1)

                def head_scores(n):
                    h = n % HEADS
                    act.wait_ge(L["h_scores"], n + 1)
                    if n > 0:
                        act.wait_ge(L["h_dstate"], 3 * n)
                    for a in range(TT):
                        scale = cols[:, a, 64 + h:65 + h] if n >= HEADS else 1.0
                        ins = act.activation(kn[:, a, :], bank[2][:, (TT + a) * P:(TT + a + 1) * P], ACT.Copy, scale=scale)
                        chain(ins, L["h_keys_sb"], n + 1) if a else chain(ins)
                    if n >= HEADS:
                        act.wait_ge(L["h_dexp_in"], h + 1)
                        chain(act.activation(dexp[:, :], dexp[:, :], ACT.Exp, scale=-1.0), L["h_dexp"], h + 1)

                def head_root(r):
                    act.wait_ge(L["norm_var"], r + 1)
                    chain(act.activation(rstd[:, r, :], ssum[:, r, :], ACT.Sqrt), L["norm_root"], r + 1)

                def read_gate(name, j, a):
                    dst, func = {"g_g": (gg, ACT.Silu), "m_o": (mo, ACT.Sigmoid), "a_gla": (ag, ACT.Sigmoid),
                                 "a_m": (am, ACT.Sigmoid)}[name]
                    read_out((name, j, a), dst[:, a, j * 512:(j + 1) * 512], func)

                def gap(k, p):
                    i = 2 * (k - GAP_BLOCKS[0]) + p // 2
                    if p % 2 == 0:
                        return
                    if 0 <= i - 2 < 2 * HEADS:
                        head_outputs(i - 2)
                    if i < 2 * HEADS:
                        head_scores(i)
                    if i - 2 in (HEADS - 1, 2 * HEADS - 1):
                        head_root((i - 2) // HEADS)

                blocks(GAP_BLOCKS, read_gate, gap)
                turn_hi("gla_t", Bhi, "gla_norm")
                turn_hi("m_t", Hhi, "m_norm")
                blocks(range(16, 20), None)
                turn_hi("merged_t", Bhi, None)

                def memory(k, p):
                    c = PIECES * (k - 20) + p
                    at = VEC["norm_mem"] + c
                    chain(act.activation(Hhi[:, c, :], memhT[:, c, :], ACT.Copy, scale=vcol[:, at:at + 1]), L["mem_hi"], c + 1)

                blocks(range(20, 22), None, memory)
                for j in range(2):
                    for a in range(TT):
                        wait_moved(act, "w_out", j, a)

                def sums(n):
                    for a in range(TT):
                        chain(act.activation(junk[:, :], x[:, a, :], ACT.Square, accum_out=ssum2[:, a:a + 1]),
                              L["sq_done"], TT * n + a + 1)

                def root(n):
                    act.wait_ge(L["var_done"], n + 1)
                    chain(act.activation(rstd2[:, :], ssum2[:, :], ACT.Sqrt), L["root_done"], n + 1)

                def read_memory(name, j, a):
                    c = 4 * j + 2 * a
                    if name == "x_wk":
                        read_out((name, j, a), kT[:, c:c + 2, :].rearrange("p c s -> p (c s)"), ACT.Copy)
                    else:
                        read_out((name, j, a), gv[:, a, j * 512:(j + 1) * 512], ACT.Copy)

                sums(1)
                blocks(range(22, 26), read_memory, lambda k, p: root(1) if (k, p) == (22, 0) else None)
                turn_hi("x_t", Bhi, "norm_xattn")

                def queries(name, j, a):
                    c = 4 * j + 2 * a
                    read_out((name, j, a), xqT[:, c:c + 2, :].rearrange("p c s -> p (c s)"), ACT.Copy)

                def exps(h):
                    act.wait_ge(L["x_negmax"], h + 1)
                    if h >= 2:
                        act.wait_ge(L["x_pt"], h - 1)
                    for a in range(TT):
                        chain(act.activation(prob[:, h % 2, a, :], bank[4 + h % 2][:, a * M:(a + 1) * M], ACT.Exp,
                                             scale=X_SCALE, bias=nmx[:, h % 2, a:a + 1], accum_out=rsum[:, h % 2, a:a + 1]),
                              L["x_exp"], TT * h + a + 1)

                def turned_prob(h):
                    act.wait_ge(L["x_pt"], h + 1)
                    if h > 0:
                        act.wait_ge(L["x_o"], h)
                    chain(act.activation(probT[:, :, :].rearrange("p m s -> p (m s)"), bank[6][:, :], ACT.Copy),
                          L["x_pt_sb"], h + 1)

                def attended(h):
                    act.wait_ge(L["x_o"], h + 1)
                    chain(act.activation(Hhi[:, 2 * h:2 * h + 2, :].rearrange("p c s -> p (c s)"), bank[7][:, :], ACT.Copy),
                          L["x_o_hi"], h + 1)

                blocks((26,), queries)
                exps(0)
                exps(1)
                blocks((27,), queries)
                turned_prob(0)
                exps(2)
                attended(0)
                turned_prob(1)
                exps(3)
                attended(1)

                def last_heads(k, p):
                    if p == 1:
                        attended(2)
                    if p == 2:
                        attended(3)
                    if p < 2:
                        turned_prob(p + 2)

                blocks((28,), None, last_heads)
                blocks((29,), None)
                for j in range(2):
                    for a in range(TT):
                        wait_moved(act, "x_wo", j, a)
                squares(2)
                turn_hi("ffn_t", Bhi, "norm_ffn")

                def ff_silu(tiles, w, n):
                    act.wait_ge(L["gate_ps"], n + 1)
                    for a in range(tiles):
                        ins = act.activation(sg[:, a, 0:w], bank[(0, 5)[a]][:, 0:w], ACT.Silu)
                    ins.then_inc(L["silu_done"], 1)

                def ff_hidT(tiles, w, n, half=0):
                    act.wait_ge(L["hid_tr"], n + 1)
                    whole = w // P * P
                    for a in range(tiles):
                        ins = act.activation(hidT[0][:, a + half, 0:whole], bank[(1, 6)[a]][:, 0:whole], ACT.Copy)
                        if w > whole:
                            ins = act.activation(hidT[0][0:w - whole, a, whole:whole + P],
                                                 bank[(1, 6)[a]][0:w - whole, whole:whole + P], ACT.Copy)
                    ins.then_inc(L["hidT_hi"], 1)

                with act.If(l == 0):
                    for f in range(DENSE_BLOCKS):
                        what, i = step_of(f, DENSE_STEPS)
                        w = dense_width(i)
                        for p in range(dense_pieces(f)):
                            wait_piece(act, f, p, DENSE_STEPS)
                            if dense_ahead(f, p) is not None:
                                f_, p_, kind, w_, rows_, arrived = dense_ahead(f, p)
                                wait_full(act, 0, MIX_BLOCKS + f_, arrived)
                                split(MIX_BLOCKS + f_, p_, kind, w_, rows_)
                            if what == "gate" and p == 0 and i > 0:
                                ff_hidT(TT, HB, i - 1)
                        if what == "gate":
                            ff_silu(TT, w, i)
                        if what == "up" and i == DENSE_STEPS - 1:
                            ff_hidT(TT, w, i)
                    act.wait_ge(L["y_done"], 1)
                with act.Else():
                    act.dma_start(gain, t["norm_ffn"][1].rearrange("(o d) -> o d", o=1).broadcast_to([P, D]))\
                        .then_inc(L["gain_in"], 16)
                    act.wait_ge(L["top_e_in"], 1)
                    act.activation(tw[:, :, 0:1], tw[:, :, 0:1], ACT.Exp).then_inc(L["top_e"], 1)
                    act.wait_ge(L["npass_ready"], 1)
                    npass = act.value_load(npass_i[0:1, 0:1], min_val=1, max_val=TT)

                    act.sem_inc(L["y_left"], 1)

                    def gathered(n, tokens):
                        act.wait_ge(L["gather_ps"], n + 1)
                        for k in range(2):
                            ins = act.activation(tokens[0][:, 4 * k:4 * k + 4, :],
                                                 bank[5 + k][:, :].rearrange("p (k c) -> p k c", k=4), ACT.Copy)
                        ins.then_inc(L["gather_hi"], 1)

                    def expert(q, g, next_tokens):
                        def pieces(f, steps=0, after=None):
                            for p in range(PIECES):
                                wait_piece(act, f, p, MOE_STEPS, q * MOE_STEPS, steps)
                                f_, p_ = ahead(f, p)
                                wait_full(act, 1, MIX_BLOCKS + f_, p_, q * MOE_STEPS + steps)
                                split(MIX_BLOCKS + f_, p_, moe_kind(f_))
                                if after is not None:
                                    after(p)

                        def at_piece(n, work):
                            return lambda p: work() if p == n else None

                        def gates_turned():
                            act.wait_ge(L["gated_ps"], q + 1)
                            act.activation(gatedT, bank[7][:, 0:S], ACT.Copy).then_inc(L["gated_sb"], 1)

                        pieces(0)
                        ff_silu(1, HB, q * MOE_STEPS)
                        pieces(1, after=at_piece(1, gates_turned))

                        def step(i, steps):
                            n = q * MOE_STEPS + i
                            pieces(2, steps, at_piece(0, lambda: ff_hidT(1, HB, n - 1)))
                            ff_silu(1, HB, n)
                            pieces(3, steps)
                            pieces(4, steps)

                        step(1, 0)
                        with act.Fori(2, MOE_STEPS - 1) as i:
                            step(i, i - 1)
                        n = q * MOE_STEPS + MOE_STEPS - 1
                        f = MOE_BLOCKS - 4
                        pieces(f, after=at_piece(0, lambda: ff_hidT(1, HB, n - 1)))
                        ff_silu(1, HB, n)
                        pieces(f + 1, after=at_piece(1, lambda: gathered(g + 1, next_tokens)))
                        pieces(f + 2, after=at_piece(0, lambda: ff_hidT(1, HB, n, half=1)))
                        pieces(f + 3)
                        act.wait_ge(L["y_ps"], (q + 1) * MOE_STEPS)
                        act.activation(yacc[:, 0:512], bank[3][:, :], ACT.Copy).then_inc(L["y_left"], 1)

                    with act.Fori(0, npass) as ps_:
                        gathered(ps_ * (NE + 1), hg[0])
                        with act.Fori(0, NE // 2) as pair:
                            for r in range(2):
                                e = 2 * pair + r
                                expert(ps_ * NE + e, ps_ * (NE + 1) + e, hg[1 - r])
                act.nop()
                layer_end(act, l)
            for a in range(TT):
                act.activation(gv[:, a, :], x[:, a, :], ACT.Square, accum_out=ssum2[:, a:a + 1]).then_inc(fin_sq, 1)
            act.wait_ge(fin_var, 1)
            act.activation(rstd2[:, :], ssum2[:, :], ACT.Sqrt).then_inc(fin_root, 1)
            act.dma_start(junk[:, :], t["norm_final"].rearrange("(o d) -> o d", o=1).broadcast_to([P, D])).then_inc(last_in, 16)

        @block.vector
        def _(dve):
            step = Steps(dve, dve_own)
            dve.wait_ge(const_ready, CONSTS)

            def op(ins, sem=None, value=None):
                step.did(ins, sem, value)
                step.wait()

            dve.wait_ge(mem_sq, 2)
            dve.tensor_scalar(ssum2[:, :], ssum2[:, :], 1.0 / D, EPS, ALU.mult, ALU.add).then_inc(mem_var, 1)
            dve.wait_ge(mem_root, 1)
            dve.reciprocal(rstd2[:, :], rstd2[:, :]).then_inc(mem_var, 1)
            dve.wait_ge(mem_var, 2)
            for a in range(TT):
                dve.tensor_scalar(gg[:, a, :], xn[:, a, :], rstd2[:, a:a + 1], None, ALU.mult).then_inc(mem_n, 1)
            for j in range(4):
                dve.wait_ge(mem_tp, j + 1)
                dve.tensor_copy(memhT[:, 2 * j:2 * j + 2, :].rearrange("p k s -> p (k s)"), bank[j][:, :]).then_inc(mem_ready, 1)
            dve.wait_ge(mem_ready, 4)
            dve.wait_ge(x_in, 16)

            with dve.Fori(0, DEPTH) as l:
                step.n, step.last = 0, None

                def norm_var(n):
                    dve.wait_ge(L["sq_done"], TT * (n + 1))
                    op(dve.tensor_scalar(ssum2[:, :], ssum2[:, :], 1.0 / D, EPS, ALU.mult, ALU.add), L["var_done"], n + 1)

                def norm_inverse(n):
                    dve.wait_ge(L["root_done"], n + 1)
                    op(dve.reciprocal(rstd2[:, :], rstd2[:, :]))

                def norm_tile(n, a):
                    ins = dve.tensor_scalar(xn[:, a, :], x[:, a, :], rstd2[:, a:a + 1], None, ALU.mult)
                    op(ins, L["xn_ready"], n + 1) if a == TT - 1 else op(ins)

                def norm(n):
                    norm_var(n)
                    norm_inverse(n)
                    for a in range(TT):
                        norm_tile(n, a)

                def turn_lo(name, pair, gain_name):
                    for j in range(4):
                        ps, mv_, v = group(name, j)
                        dve.wait_ge(L["turn_hi"], 4 * TURNS.index(name) + j + 1)
                        for k in range(2):
                            c = 2 * j + k
                            if gain_name:
                                ins = dve.scalar_tensor_tensor(pair[1][:, c, :], ps[:, k * S:(k + 1) * S],
                                                               vcol[:, VEC[gain_name] + c:VEC[gain_name] + c + 1],
                                                               pair[0][:, c, :].bitcast(F32), ALU.mult, ALU.subtract)
                            else:
                                ins = dve.tensor_tensor(pair[1][:, c, :], ps[:, k * S:(k + 1) * S],
                                                        pair[0][:, c, :].bitcast(F32), ALU.subtract)
                            op(ins, mv_, v) if k else op(ins)

                def split(k, p, kind, w=512, rows=P):
                    dve.tensor_tensor(split_piece(wlo, k, p, kind, w)[0:rows], raw_piece(k, p, kind, w)[0:rows],
                                      split_piece(whi, k, p, kind, w)[0:rows].bitcast(F32), ALU.subtract).then_inc(lo_done, 1)

                def split_ahead(k, p):
                    k, p = ahead(k, p)
                    dve.wait_ge(hi_done, PIECES * k + p + 1)
                    split(k, p, kind_of(k))

                def blocks(numbers, read=None, between=None):
                    for k in numbers:
                        name, j = BLOCKS[k]
                        for p in range(PIECES):
                            if read is not None and ends_group(k, p) is not None:
                                for a in ((p // 2,) if is_columns(k) else range(TT)):
                                    read(name, j, a)
                            split_ahead(k, p)
                            if between is not None:
                                between(k, p)

                H, B = (Hhi, Hlo), (Bhi, Blo)
                wait_group(dve, "vec", 0)
                op(dve.tensor_copy(vcol[:, :], bank[GROUPS[("vec", 0)] % GROUP_BANKS][:, 0:NVEC]), moved[0], 1)
                norm(0)
                dve.wait_ge(L["small_hi"], 1)
                dve.tensor_tensor(wsmall_lo[:, :, :], wsmall[:, :, :], wsmall_hi[:, :, :].bitcast(F32), ALU.subtract)\
                    .then_inc(L["small_lo"], 1)
                for p in range(SPLIT):
                    dve.wait_ge(hi_done, p + 1)
                    split(0, p, kind_of(0))
                turn_lo("mix_t", H, "norm_mix")
                ps, mv_, v = group("small", 1)
                wait_group(dve, "small", 1)
                op(dve.tensor_scalar(grow[:, 1, :], ps[0:HEADS, 0:S], gbias[:, 1:2], None, ALU.add), mv_, v)
                op(dve.scalar_tensor_tensor(grow[:, 2, :], grow[:, 1, :], -1.0, grow[:, 1, :], ALU.mult, ALU.max), L["gate_z"], 1)

                def decay_input():
                    for a in range(2):
                        ps, mv_, v = group("decay", a)
                        wait_group(dve, "decay", a)
                        for c in range(2):
                            h = 2 * a + c
                            ins = dve.tensor_scalar(cum[:, h, :], ps[:, c * S:(c + 1) * S],
                                                    vcol[:, VEC["gla_gk_bias"] + h:VEC["gla_gk_bias"] + h + 1], None, ALU.add)
                            op(ins, mv_, v) if c else op(ins)
                    op(dve.scalar_tensor_tensor(e1[:, :, :].rearrange(flat), cum[:, :, :].rearrange(flat), -1.0,
                                                cum[:, :, :].rearrange(flat), ALU.mult, ALU.max), L["decay_z"], 1)

                def row_chunk(c):
                    s_ = slice(c * CH, (c + 1) * CH)
                    e_ = slice((c + 1) * CH - 1, (c + 1) * CH)
                    op(dve.tensor_tensor_scan(mrow[:, s_], zrow[:, :], grow[:, 1, s_], mst[:, c:c + 1], ALU.add, ALU.max))
                    op(dve.tensor_scalar(grow[:, 4, s_], mrow[:, s_], mst[:, c:c + 1], None, ALU.subtract))
                    op(dve.tensor_scalar(rows[64:64 + HEADS, s_], grow[:, 1, s_], mrow[:, e_], None, ALU.subtract))
                    op(dve.tensor_tensor(mst[:, c + 1:c + 2], grow[:, 3, e_], mrow[:, e_], ALU.add))

                def convolve(c):
                    if c % 2 == 0:
                        wait_moved(dve, "m_q" if c < 4 else "m_k", 0, c % 4 // 2)

                    def tap(j):
                        at = VEC["m_conv"] + j * KC + c
                        return vcol[:, at:at + 1]

                    op(dve.tensor_scalar(qk[:, c, :], cin[:, c, 0:S], tap(0), None, ALU.mult))
                    for j in range(1, CONV_W):
                        ins = dve.scalar_tensor_tensor(qk[:, c, :], cin[:, c, j:j + S], tap(j), qk[:, c, :],
                                                       ALU.mult, ALU.add)
                        op(ins, L["conv_out"], 1) if c == KC - 1 and j == CONV_W - 1 else op(ins)

                flat = "p h s -> p (h s)"

                def front(k, p):
                    at = PIECES * k + p
                    if (k, p) == (1, 3):
                        decay_input()
                    if (k, p) == (2, 0):
                        dve.wait_ge(L["decay_e"], 1)
                        op(dve.scalar_tensor_tensor(cum[:, :, :].rearrange(flat), cum[:, :, :].rearrange(flat), 0.0,
                                                    e1[:, :, :].rearrange(flat), ALU.min, ALU.subtract))
                    if (k, p) == (2, 1):
                        op(dve.tensor_scalar(cum[:, :, :], cum[:, :, :], 1.0 / GATE_NORM, LOG_DECAY_MIN, ALU.mult, ALU.max))
                    if (k, p) == (2, 2):
                        for h in range(HEADS):
                            ins = dve.tensor_tensor_scan(gkeT[:, h, :], restart[:, :], cum[:, h, :], 0.0, ALU.mult, ALU.add)
                            op(ins, L["cum_ready"], 1) if h == HEADS - 1 else op(ins)
                    if (k, p) == (2, 3):
                        dve.wait_ge(L["row_ln"], 1)
                        op(dve.scalar_tensor_tensor(grow[:, 1, :], grow[:, 1, :], 0.0, grow[:, 2, :], ALU.min, ALU.subtract))
                        op(dve.tensor_tensor_scan(grow[:, 3, :], restart[0:HEADS, :], grow[:, 1, :], 0.0, ALU.mult, ALU.add))
                        wait_moved(dve, "small", 0)
                        op(dve.scalar_tensor_tensor(grow[:, 1, :], grow[:, 0, :], gbias[:, 0:1], grow[:, 3, :],
                                                    ALU.add, ALU.subtract))
                        op(dve.tensor_copy(rows[0:HEADS, :], grow[:, 1, :]))
                    if k == 3:
                        row_chunk(p)
                    if (k, p) == (3, 3):
                        op(dve.tensor_tensor(rows[96:96 + HEADS, :], grow[:, 3, :], mrow[:, 0:S], ALU.add), L["row_dm"], 1)
                    if (k, p) == (4, 0):
                        dve.wait_ge(L["e_ready"], 1)
                        for a in range(2):
                            wait_moved(dve, "g_q", 0, a)
                            wait_moved(dve, "g_k", 0, a)
                        op(dve.scalar_tensor_tensor(gqT[:, :, :].rearrange(flat), gqT[:, :, :].rearrange(flat), QK_SCALE,
                                                    e1[:, :, :].rearrange(flat), ALU.mult, ALU.mult))
                    if (k, p) == (4, 1):
                        op(dve.tensor_tensor(gkT[:, :, :], gkT[:, :, :], cum[:, :, :], ALU.mult))
                    if (k, p) == (4, 2):
                        ends = e1[:, :, CH - 1:S:CH].unsqueeze(3).broadcast_to([P, HEADS, NCH, CH])
                        for h in range(HEADS):
                            ins = dve.tensor_tensor(gkeT[:, h, :].rearrange("p (c s) -> p c s", s=CH),
                                                    gkT[:, h, :].rearrange("p (c s) -> p c s", s=CH), ends[:, h], ALU.mult)
                            op(ins, L["gla_in"], 1) if h == HEADS - 1 else op(ins)
                    first = PIECES * 4 + 3
                    if first <= at < first + KC:
                        convolve(at - first)

                blocks(range(8), between=front)
                ps, mv_, v = group("gate_cols", 0)
                wait_group(dve, "gate_cols", 0)
                op(dve.tensor_copy(cols[:, :, :].rearrange("p a c -> p (a c)"), ps[:, 0:TT * P]), mv_, v)

                def head_outputs(n):
                    h = n - HEADS
                    for a in range(TT):
                        dve.wait_ge(L["h_out"], TT * n + a + 1)
                        if h > 0:
                            dve.wait_ge(L["h_outsb"], TT * (n - 1) + a + 1)
                        op(dve.scalar_tensor_tensor(den[:, a:a + 1], bank[6 + a][:, DV:DV + 1], -1.0,
                                                    cols[:, a, 96 + h:97 + h], ALU.mult, ALU.max))
                        op(dve.tensor_tensor(den[:, a:a + 1], den[:, a:a + 1], bank[6 + a][:, DV:DV + 1], ALU.max))
                        op(dve.reciprocal(den[:, a:a + 1], den[:, a:a + 1]), L["h_den"], TT * h + a + 1)

                def head_states(n):
                    h = n % HEADS
                    width = DV if n < HEADS else DV + 1
                    if n > 0:
                        dve.wait_ge(L["h_out"], TT * n)
                    for c in range(NCH - 1):
                        dve.wait_ge(L["h_dstate"], 3 * n + c + 1)
                        decay = e1[:, h, (c + 1) * CH - 1:(c + 1) * CH] if n < HEADS else sdec[:, h, c:c + 1]
                        inc = bank[(5, 3)[c % 2]][:, 0:width]
                        if c == 0:
                            ins = dve.tensor_copy(st[:, 0, 0:width], inc)
                        else:
                            ins = dve.scalar_tensor_tensor(st[:, c, 0:width], st[:, c - 1, 0:width], decay, inc,
                                                           ALU.mult, ALU.add)
                        op(ins, L["h_state"], 3 * n + c + 1)

                def head_scores(n):
                    h = n % HEADS
                    if n > 1:
                        dve.wait_ge(L["h_out"], TT * (n - 1))
                    if n < HEADS:
                        dve.wait_ge(L["h_scores"], n + 1)
                        dve.wait_ge(L["h_keys_sb"], n + 1)
                        op(dve.copy_predicated(sT[:, n % 2, :], causal[:, :].bitcast(U32), bank[2][:, 0:TT * P]),
                           L["h_masked"], n + 1)
                        return
                    dve.wait_ge(L["h_bcast"], h + 1)
                    for a in range(TT):
                        ins = dve.scalar_tensor_tensor(dexp[:, a * P:(a + 1) * P], bank[3][:, a * P:(a + 1) * P],
                                                       cols[:, a, h:h + 1], hide[:, a * P:(a + 1) * P], ALU.subtract, ALU.max)
                        op(ins, L["h_dexp_in"], h + 1) if a else op(ins)
                    op(dve.tensor_copy(sdec[:, h, :], bank[3][:, S:S + NCH]))
                    if h == 0:
                        dve.wait_ge(L["qk_ready"], 1)
                    op(dve.tensor_tensor(qs[:, n % 2, :], qk[:, h, :], bank[4][:, 0:S], ALU.mult), L["h_qs"], h + 1)
                    dve.wait_ge(L["h_dexp"], h + 1)
                    dve.wait_ge(L["h_keys_sb"], n + 1)
                    op(dve.scalar_tensor_tensor(wT[:, n % 2, :], bank[2][:, 0:TT * P], QK_SCALE, dexp[:, :], ALU.mult, ALU.mult),
                       L["h_masked"], n + 1)

                def head_norm(r, o, gate, gate_name, done):
                    dve.wait_ge(L["h_outsb"], TT * HEADS * (r + 1))
                    op(dve.tensor_scalar(ssum[:, r, :], ssum[:, r, :], 1.0 / DV, EPS, ALU.mult, ALU.add), L["norm_var"], r + 1)
                    for j in range(2):
                        for a in range(TT):
                            wait_moved(dve, gate_name, j, a)
                    dve.wait_ge(L["norm_root"], r + 1)
                    op(dve.reciprocal(rstd[:, r, :], rstd[:, r, :]))
                    for a in range(TT):
                        for h in range(HEADS):
                            i = a * HEADS + h
                            op(dve.scalar_tensor_tensor(o[:, a, h * DV:(h + 1) * DV], o[:, a, h * DV:(h + 1) * DV],
                                                        rstd[:, r, i:i + 1], gate[:, a, h * DV:(h + 1) * DV], ALU.mult, ALU.mult),
                               L[done], i + 1)

                def gap(k, p):
                    i = 2 * (k - GAP_BLOCKS[0]) + p // 2
                    if p % 2 == 0:
                        return
                    if HEADS <= i - 2 < 2 * HEADS:
                        head_outputs(i - 2)
                    if 0 <= i - 1 < 2 * HEADS:
                        head_states(i - 1)
                    if i < 2 * HEADS:
                        head_scores(i)
                    if i - 2 == HEADS - 1:
                        head_norm(0, xn, gg, "g_g", "gated_g")
                    if i - 2 == 2 * HEADS - 1:
                        head_norm(1, om, mo, "m_o", "gated_m")

                blocks(GAP_BLOCKS, between=gap)

                turn_lo("gla_t", B, "gla_norm")
                turn_lo("m_t", H, "m_norm")

                def read_branch(name, j, a):
                    c = slice(j * 512, (j + 1) * 512)
                    ps, mv_, v = group(name, j, a)
                    wait_group(dve, name, j, a)
                    if name == "gla_proj":
                        op(dve.tensor_tensor(ag[:, a, c], ag[:, a, c], ps[:, :], ALU.mult), mv_, v)
                    else:
                        op(dve.tensor_tensor(am[:, a, c], am[:, a, c], ps[:, :], ALU.mult))
                        op(dve.tensor_tensor(ag[:, a, c], ag[:, a, c], am[:, a, c], ALU.add), mv_, v)

                blocks(range(16, 20), read_branch)
                turn_lo("merged_t", B, None)

                def add_to_x(name, j, a):
                    c = slice(j * 512, (j + 1) * 512)
                    ps, mv_, v = group(name, j, a)
                    wait_group(dve, name, j, a)
                    op(dve.tensor_tensor(x[:, a, c], x[:, a, c], ps[:, :], ALU.add), mv_, v)

                def memory(k, p):
                    c = PIECES * (k - 20) + p
                    at = VEC["norm_mem"] + c
                    dve.wait_ge(L["mem_hi"], c + 1)
                    op(dve.scalar_tensor_tensor(Hlo[:, c, :], memhT[:, c, :], vcol[:, at:at + 1], Hhi[:, c, :].bitcast(F32),
                                                ALU.mult, ALU.subtract), L["mem_t"], c + 1)

                blocks(range(20, 22), add_to_x, memory)

                def norm_between(k, p):
                    if (k, p) == (22, 0):
                        norm_var(1)
                    if (k, p) == (22, 1):
                        norm_inverse(1)
                        norm_tile(1, 0)
                    if (k, p) == (22, 2):
                        norm_tile(1, 1)

                blocks(range(22, 26), between=norm_between)
                turn_lo("x_t", B, "norm_xattn")

                def negated_max(h):
                    dve.wait_ge(L["x_score"], h + 1)
                    op(dve.tensor_reduce(mx[:, :], bank[4 + h % 2][:, :].rearrange("p (a m) -> p a m", a=TT), axis=AX.X, op=ALU.max))
                    op(dve.tensor_scalar(nmx[:, h % 2, :], mx[:, :], -X_SCALE, None, ALU.mult), L["x_negmax"], h + 1)

                def normalise(h):
                    dve.wait_ge(L["x_exp"], TT * (h + 1))
                    op(dve.reciprocal(rinv[:, :], rsum[:, h % 2, :]))
                    for a in range(TT):
                        ins = dve.tensor_scalar(prob[:, h % 2, a, :], prob[:, h % 2, a, :], rinv[:, a:a + 1], None, ALU.mult)
                        op(ins, L["x_prob"], h + 1) if a else op(ins)

                def attended(h):
                    dve.wait_ge(L["x_o"], h + 1)
                    dve.wait_ge(L["x_o_hi"], h + 1)
                    c = slice(2 * h, 2 * h + 2)
                    op(dve.tensor_tensor(Hlo[:, c, :].rearrange("p c s -> p (c s)"), bank[7][:, :],
                                         Hhi[:, c, :].rearrange("p c s -> p (c s)").bitcast(F32), ALU.subtract),
                       L["x_o_sb"], h + 1)

                def between_heads(k, p):
                    if (k, p) == (26, 3):
                        negated_max(0)
                        negated_max(1)
                    if k == 27 and p < 2:
                        normalise(p)

                blocks((26, 27), between=between_heads)
                negated_max(2)
                attended(0)
                negated_max(3)
                attended(1)
                normalise(2)
                normalise(3)
                blocks((28, 29), add_to_x, lambda k, p: attended(p + 1) if k == 28 and p in (1, 2) else None)
                norm(2)
                turn_lo("ffn_t", B, "norm_ffn")

                def ff_hid(tiles, w, n):
                    dve.wait_ge(L["silu_done"], n + 1)
                    dve.wait_ge(L["up_ps"], n + 1)
                    for a in range(tiles):
                        ins = dve.tensor_tensor(hid[:, a, 0:w], sg[:, a, 0:w], bank[(1, 6)[a]][:, 0:w], ALU.mult)
                    ins.then_inc(L["hid_ready"], 1)

                def ff_hidT(tiles, w, n, half=0):
                    dve.wait_ge(L["hidT_hi"], n + 1)
                    whole = w // P * P
                    for a in range(tiles):
                        ins = dve.tensor_tensor(hidT[1][:, a + half, 0:whole], bank[(1, 6)[a]][:, 0:whole],
                                                hidT[0][:, a + half, 0:whole].bitcast(F32), ALU.subtract)
                        if w > whole:
                            r = slice(0, w - whole)
                            ins = dve.tensor_tensor(hidT[1][r, a, whole:whole + P], bank[(1, 6)[a]][r, whole:whole + P],
                                                    hidT[0][r, a, whole:whole + P].bitcast(F32), ALU.subtract)
                    ins.then_inc(L["hidT_ready"], 1)

                with dve.If(l == 0):
                    for f in range(DENSE_BLOCKS):
                        what, i = step_of(f, DENSE_STEPS)
                        for p in range(dense_pieces(f)):
                            if what == "up" and p == PIECES - 1:
                                ff_hid(TT, dense_width(i), i)
                            if dense_ahead(f, p) is not None:
                                f_, p_, kind, w_, rows_, _ = dense_ahead(f, p)
                                wait_lo(dve, f_, p_)
                                split(MIX_BLOCKS + f_, p_, kind, w_, rows_)
                            if what == "gate" and p == 0 and i > 0:
                                ff_hidT(TT, HB, i - 1)
                        if what == "up" and i == DENSE_STEPS - 1:
                            ff_hidT(TT, dense_width(i), i)
                    dve.wait_ge(L["y_ps"], DENSE_STEPS)
                    for a in range(TT):
                        for c in range(2):
                            s_ = slice(c * 512, (c + 1) * 512)
                            ins = dve.tensor_tensor(x[:, a, s_], x[:, a, s_], bank[((3, 4), (2, 7))[a][c]][:, :], ALU.add)
                    ins.then_inc(L["y_done"], 1)
                    dve.wait_ge(L["y_done"], 1)
                with dve.Else():
                    for v in (place, chosen, gates):
                        op(dve.memset(v[:, :, NE:NE + 1], 0.0))
                    dve.wait_ge(L["logit_ps"], 1)
                    op(dve.tensor_copy(logit[:, :, :].rearrange("p a e -> p (a e)"), bank[4][:, 0:TT * NE]))
                    for a in range(TT):
                        op(dve.max(top[:, a, :], logit[:, a, :]))
                        op(dve.max_index(topi[:, a, :], top[:, a, :], logit[:, a, :]))
                        op(dve.tensor_copy(topf[:, a, :], topi[:, a, :]))
                    ins = dve.tensor_tensor(tw[:, :, 0:1], top[:, :, 1:2], top[:, :, 0:1], ALU.subtract)
                    op(ins, L["top_e_in"], 1)
                    dve.wait_ge(L["top_e"], 1)
                    op(dve.tensor_scalar(tw[:, :, 1:2], tw[:, :, 0:1], 1.0, None, ALU.add))
                    op(dve.reciprocal(tw[:, :, 2:3], tw[:, :, 1:2]))
                    op(dve.tensor_tensor(tw[:, :, 3:4], tw[:, :, 0:1], tw[:, :, 2:3], ALU.mult))
                    for a in range(TT):
                        for r in range(2):
                            op(dve.tensor_scalar(oh[:, r, :], expert_no[:, :], topf[:, a, r:r + 1], None, ALU.is_equal))
                        op(dve.tensor_tensor(chosen[:, a, 0:NE], oh[:, 0, :], oh[:, 1, :], ALU.add))
                        op(dve.tensor_scalar(oh[:, 0, :], oh[:, 0, :], tw[:, a, 2:3], None, ALU.mult))
                        ins = dve.scalar_tensor_tensor(gates[:, a, 0:NE], oh[:, 1, :], tw[:, a, 3:4], oh[:, 0, :], ALU.mult, ALU.add)
                        op(ins, L["count_in"], 1) if a == TT - 1 else op(ins)
                    dve.wait_ge(L["count_ps"], 1)
                    op(dve.tensor_copy(place[:, :, 0:NE], bank[5][:, 0:TT * NE].rearrange("p (a e) -> p a e", a=TT)))
                    op(dve.tensor_reduce(most[:, 0:1], bank[5][:, TT * NE:(TT + 1) * NE], axis=AX.X, op=ALU.max))
                    op(dve.tensor_scalar(npass_i[:, :], most[:, 0:1], float(P), 1.0, ALU.is_gt, ALU.add), L["npass_ready"], 1)
                    npass = dve.value_load(npass_i[0:1, 0:1], min_val=1, max_val=TT)
                    dve.wait_ge(L["gain_in"], 16)
                    for a in range(TT):
                        op(dve.tensor_tensor(xn[:, a, :], xn[:, a, :], gain, ALU.mult))
                    op(dve.memset(yacc, 0.0))
                    op(dve.memset(gatedT, 0.0))
                    dve.sem_inc(L["y_right"], 1)
                    dve.sem_inc(L["gated_sb"], 1)

                    def prepare(e, n):
                        for a in range(TT):
                            col = bass.ds(e, 1)
                            dve.tensor_copy(place_p[:, a, 0:1], place[:, a, col])
                            dve.tensor_copy(place_p[:, a, 1:2], chosen[:, a, col])
                            dve.tensor_copy(place_p[:, a, 2:3], gates[:, a, col]).then_inc(dve_q, 1)
                        dve.wait_ge(dve_q, n * Q_STEPS + TT)
                        for a in range(TT):
                            dve.tensor_scalar(onehot[:, a, :], slot_no[:, :], place_p[:, a, 0:1], place_p[:, a, 1:2],
                                              ALU.is_equal, ALU.mult).then_inc(dve_q, 1)
                        dve.wait_ge(dve_q, n * Q_STEPS + 2 * TT)
                        for a in range(TT):
                            dve.tensor_scalar(gated[:, a, :], onehot[:, a, :], place_p[:, a, 2:3], None, ALU.mult)\
                                .then_inc(dve_q, 1)
                        dve.wait_ge(dve_q, n * Q_STEPS + 3 * TT)
                        dve.sem_inc(L["onehot_ready"], 1)

                    def gathered(n, tokens):
                        dve.wait_ge(L["gather_hi"], n + 1)
                        for k in range(2):
                            c = slice(4 * k, 4 * k + 4)
                            ins = dve.tensor_tensor(tokens[1][:, c, :], bank[5 + k][:, :].rearrange("p (k c) -> p k c", k=4),
                                                    tokens[0][:, c, :].bitcast(F32), ALU.subtract)
                        ins.then_inc(L["gather_sb"], 1)

                    def scattered(n):
                        dve.wait_ge(L["scatter_ps"], n + 1)
                        for a in range(TT):
                            for c in range(2):
                                s_ = slice(c * 512, (c + 1) * 512)
                                ins = dve.tensor_tensor(x[:, a, s_], x[:, a, s_], bank[(5, 6, 7, 2)[2 * a + c]][:, :], ALU.add)
                        ins.then_inc(L["scattered"], 1)

                    def expert(q, g, e, next_tokens):
                        def pieces(f, steps=0, before=None, after=None):
                            for p in range(PIECES):
                                if p == PIECES - 1 and before is not None:
                                    before()
                                f_, p_ = ahead(f, p)
                                wait_lo(dve, f_, p_, (q * MOE_STEPS + steps) * (3 * PIECES))
                                split(MIX_BLOCKS + f_, p_, moe_kind(f_))
                                if after is not None:
                                    after(p)

                        def at_piece(n, work):
                            return lambda p: work() if p == n else None

                        def step(i, steps):
                            n = q * MOE_STEPS + i
                            pieces(2, steps, after=at_piece(0, lambda: ff_hidT(1, HB, n - 1)))
                            pieces(3, steps)
                            pieces(4, steps, before=lambda: ff_hid(1, HB, n))

                        pieces(0, after=at_piece(2, lambda: scattered(q)))
                        pieces(1, before=lambda: ff_hid(1, HB, q * MOE_STEPS))
                        step(1, 0)
                        dve.wait_ge(L["gather_ps"], g + 1)
                        dve.wait_ge(L["gated_ps"], q + 1)
                        prepare(e + 1, g + 1)
                        with dve.Fori(2, MOE_STEPS - 1) as i:
                            step(i, i - 1)
                        n = q * MOE_STEPS + MOE_STEPS - 1
                        f = MOE_BLOCKS - 4
                        dve.wait_ge(L["scattered"], q + 1)
                        pieces(f, after=at_piece(0, lambda: ff_hidT(1, HB, n - 1)))
                        pieces(f + 1, before=lambda: ff_hid(1, HB, n), after=at_piece(1, lambda: gathered(g + 1, next_tokens)))
                        pieces(f + 2, after=at_piece(0, lambda: ff_hidT(1, HB, n, half=1)))
                        pieces(f + 3)
                        dve.wait_ge(L["y_ps"], (q + 1) * MOE_STEPS)
                        dve.tensor_copy(yacc[:, 512:1024], bank[4][:, :]).then_inc(L["y_right"], 1)

                    with dve.Fori(0, npass) as ps_:
                        prepare(0, ps_ * (NE + 1))
                        gathered(ps_ * (NE + 1), hg[0])
                        with dve.Fori(0, NE // 2) as pair:
                            for r in range(2):
                                e = 2 * pair + r
                                expert(ps_ * NE + e, ps_ * (NE + 1) + e, e, hg[1 - r])
                        dve.wait_ge(L["gather_ps"], (ps_ + 1) * (NE + 1))
                        dve.tensor_scalar(place[:, :, :], place[:, :, :], -float(P), None, ALU.add).then_inc(dve_p, 1)
                        dve.wait_ge(dve_p, ps_ + 1)
                    scattered(npass * NE)
                dve.nop()
                layer_end(dve, l)
            dve.wait_ge(fin_sq, 2)
            dve.tensor_scalar(ssum2[:, :], ssum2[:, :], 1.0 / D, EPS, ALU.mult, ALU.add).then_inc(fin_var, 1)
            dve.wait_ge(fin_root, 1)
            dve.reciprocal(rstd2[:, :], rstd2[:, :]).then_inc(fin_var, 1)
            dve.wait_ge(fin_var, 2)
            dve.wait_ge(last_in, 16)
            for a in range(TT):
                dve.scalar_tensor_tensor(xn[:, a, :], x[:, a, :], rstd2[:, a:a + 1], junk[:, :], ALU.mult, ALU.mult)\
                    .then_inc(fin_out, 1)


_INS = ["x", "mem", "norm_mix", "w_in", "gla_gk_up", "gla_gk_bias", "gla_norm", "m_conv", "m_gate_bias", "m_norm",
        "gla_proj", "m_proj", "w_out", "norm_xattn", "norm_mem", "x_wq", "x_wkv", "x_wo", "norm_ffn",
        "ffn_w13", "ffn_w2", "moe_router", "moe_w13", "moe_w2", "norm_final"]


def kernel(**inputs):
    import numpy as _np
    import concourse.bacc as _bacc
    from concourse import mybir as _mybir
    from concourse.bass_utils import run_bass_kernel_spmd as _run

    nc = _bacc.Bacc("TRN2", target_bir_lowering=False, num_devices=1)
    arrays, tensors = {}, {}
    for name in _INS:
        a = _np.ascontiguousarray(inputs[name])
        arrays[f"in_{name}_dram"] = a
        tensors[name] = nc.dram_tensor(f"in_{name}_dram", a.shape, _mybir.dt.from_np(a.dtype), kind="ExternalInput").ap()
    out = nc.dram_tensor("out_0_dram", (1, S, D), F32, kind="ExternalOutput").ap()
    hybrid_decoder_kernel(nc, tensors, out)
    r = _run(nc, [arrays], core_ids=[0])
    return r.results[0]["out_0_dram"]
```

```python
import numpy as np
import concourse.bass as bass
from concourse import mybir
from concourse.alu_op_type import AluOpType as ALU
from contextlib import ExitStack

F32 = mybir.dt.float32
F32R = mybir.dt.float32r
U32 = mybir.dt.uint32
I32 = mybir.dt.int32
ACT = mybir.ActivationFunctionType
AX = mybir.AxisListType

P = 128
S = 256
M = 256
D = 1024
TT = S // P
KC = D // P
DEPTH = 2
EPS = 1e-6
HEADS = 4
DK = 128
DV = 256
CH = 64
NCH = S // CH
RANK = 16
CONV_W = 4
FFN = 64 * ((8 * D // 3 + 63) // 64)
NE = 8
EXP = 7 * D // 2
HB = 512
DENSE_STEPS = (FFN + HB - 1) // HB
DENSE_TAIL = FFN - (DENSE_STEPS - 1) * HB
MOE_STEPS = EXP // HB
GATE_NORM = 16.0
LOG_DECAY_MIN = -1.0
QK_SCALE = DK ** -0.5
X_SCALE = (D // HEADS) ** -0.5
BIG = 1e30

OFF = {}
_at = 0
for _name, _w in (("g_q", 512), ("g_k", 512), ("g_v", D), ("g_lr", RANK), ("g_g", D), ("m_q", 512), ("m_k", 512),
                  ("m_v", D), ("m_i", HEADS), ("m_f", HEADS), ("m_o", D), ("a_gla", D), ("a_m", D)):
    OFF[_name] = _at
    _at += _w
N_IN = _at

BLOCKS = [(name, j) for name, n in (("g_q", 1), ("g_k", 1), ("m_q", 1), ("m_k", 1), ("g_v", 2), ("m_v", 2), ("g_g", 2),
                                    ("m_o", 2), ("a_gla", 2), ("a_m", 2), ("gla_proj", 2), ("m_proj", 2), ("w_out", 2),
                                    ("x_wk", 2), ("x_wv", 2), ("x_wq", 2), ("x_wo", 2)) for j in range(n)]
COLUMN_BLOCKS = ("g_q", "g_k", "m_q", "m_k", "x_wk", "x_wq")

PIECES = 4
HALF = KC * 512 // 2
PIECE = HALF // 2
RAW = 3
SPLIT = 3
MIX_BLOCKS = len(BLOCKS)
DENSE_BLOCKS = 3 * DENSE_STEPS
MOE_BLOCKS = 3 * MOE_STEPS
assert 2 * MIX_BLOCKS % RAW == 2 * DENSE_BLOCKS % RAW == 2 * MOE_BLOCKS % RAW == 0
assert DENSE_STEPS != MOE_STEPS
assert PIECES * MIX_BLOCKS % SPLIT == PIECES * DENSE_BLOCKS % SPLIT == PIECES * MOE_BLOCKS % SPLIT == 0
LAYER_LOADS = 2 * (MIX_BLOCKS + DENSE_BLOCKS) // RAW

TURNS = ("mix_t", "gla_t", "m_t", "merged_t", "x_t", "ffn_t")

GROUP_BANKS = 2
GROUPS = {}
GAP_BLOCKS = range(8, 16)


def _plan():
    def add(*name):
        GROUPS[name] = len(GROUPS)

    add("vec", 0)
    add("small", 0)
    add("small", 1)
    def blocks(numbers):
        for name, j in [BLOCKS[b] for b in numbers]:
            add(name, j, 0)
            add(name, j, 1)

    blocks(range(0, 2))
    add("decay", 0)
    add("decay", 1)
    blocks(range(2, 8))
    add("gate_cols", 0)
    blocks(GAP_BLOCKS)
    blocks(range(16, 20))
    blocks(range(20, 26))
    blocks(range(26, 30))


_plan()


def ends_group(k, p):
    name, j = BLOCKS[k]
    if name in COLUMN_BLOCKS:
        return (name, j, p // 2) if p % 2 else None
    return (name, j, 1) if p == PIECES - 1 else None


_loose = [(k, p) for k in range(MIX_BLOCKS) for p in range(PIECES) if ends_group(k, p) is None]
LOOSE = {kp: n + 1 for n, kp in enumerate(_loose)}
MIX_LOOSE = len(LOOSE)

VEC = {}
_at = 0
for _name, _w in (("norm_mix", 8), ("gla_gk_bias", 4), ("gla_norm", 8), ("m_conv", 32), ("m_norm", 8),
                  ("norm_xattn", 8), ("norm_mem", 8), ("norm_ffn", 8)):
    VEC[_name] = _at
    _at += _w
NVEC = _at


CONSTS = 22
VEC_DMAS = len(VEC) + 5
Q_STEPS = 3 * TT


class Steps:

    def __init__(self, eng, own):
        self.eng, self.own, self.n, self.last, self.base = eng, own, 0, None, 0

    def wait(self):
        if self.last is not None:
            self.eng.wait_ge(*self.last)

    def did(self, ins, sem=None, value=None):
        if sem is None:
            self.n += 1
            ins.then_inc(self.own, 1)
            self.last = (self.own, self.base + self.n)
        else:
            ins.then_inc(sem, 1)
            self.last = (sem, value)


def hybrid_decoder_kernel(nc, t, out):
    ctx = ExitStack()
    with ctx:
        def sb(name, shape, dt=F32):
            return ctx.enter_context(nc.sbuf_tensor("sb_" + name, shape, dt))

        def sem(name):
            return ctx.enter_context(nc.semaphore(name))

        bank = [ctx.enter_context(nc.psum_tensor(f"bank{i}", [P, 512], F32)) for i in range(8)]
        raw = sb("raw", [P, RAW, HALF])
        whi = sb("whi", [P, SPLIT, PIECE], F32R)
        wlo = sb("wlo", [P, SPLIT, PIECE], F32R)
        x = sb("x", [P, TT, D])
        xn = sb("xn", [P, TT, D])
        Hhi, Hlo = sb("Hhi", [P, KC, S], F32R), sb("Hlo", [P, KC, S], F32R)
        memhT = sb("memhT", [P, KC, M])
        heads_only = ExitStack()

        def hsb(name, shape):
            return heads_only.enter_context(nc.sbuf_tensor("sb_" + name, shape, F32))

        gkeT = hsb("gkeT", [P, HEADS, S])
        qk = hsb("qk", [P, KC, S])
        scratch = hsb("scratch", [P, 6, S])
        heads_only.close()
        Bhi, Blo = sb("Bhi", [P, KC, S], F32R), sb("Blo", [P, KC, S], F32R)
        sb("rest_of_heads_only", [P, 2 * S])
        gqk = sb("gqk", [P, 2 * HEADS, S])
        gqT = gqk[:, 0:HEADS, :]
        gkT = gqk[:, HEADS:, :]
        cum = sb("cum", [P, HEADS, S])
        e1 = sb("e1", [P, HEADS, S])
        gv = sb("gv", [P, TT, D])
        gg = sb("gg", [P, TT, D])
        cin = sb("cin", [P, KC, CONV_W - 1 + S])
        mv = sb("mv", [P, TT, HEADS, DV + 1])
        mo = sb("mo", [P, TT, D])
        ag = sb("ag", [P, TT, D])
        am = sb("am", [P, TT, D])
        om = gqk[:, :, :].rearrange("p (a b) s -> p a (b s)", a=TT)
        junk = sb("junk", [P, D])
        ident = sb("ident", [P, P])
        tri = sb("tri", [P, P])
        ones = sb("ones", [P, P])
        slot_no = sb("slot_no", [P, P])
        expert_no = sb("expert_no", [P, NE])
        causal = sb("causal", [P, TT * P])
        hide = sb("hide", [P, TT * P])
        restart = sb("restart", [P, S])
        pick = sb("pick", [HEADS, HEADS, P])
        zrow = sb("zrow", [HEADS, CH])
        lnscale = sb("lnscale", [P, 1])
        vrow = sb("vrow", [NVEC, P])
        vcol = sb("vcol", [P, NVEC])
        wsmall = sb("wsmall", [P, KC, RANK + 2 * HEADS])
        wsmall_hi = sb("wsmall_hi", [P, KC, RANK + 2 * HEADS], F32R)
        wsmall_lo = sb("wsmall_lo", [P, KC, RANK + 2 * HEADS], F32R)
        gkup = sb("gkup", [RANK, 512])
        gbias = sb("gbias", [HEADS, 2])
        lrT = sb("lrT", [RANK, S])
        sT = sb("sT", [P, 2, TT * P])
        wT = scratch[:, 0:2, :]
        kn = scratch[:, 5, :].rearrange("p (a k) -> p a k", k=P)
        st = sb("st", [P, 3, DV + 1])
        qs = scratch[:, 2:4, :]
        dexp = scratch[:, 4, :]
        ssum = sb("ssum", [P, 2, TT * HEADS])
        rstd = sb("rstd", [P, 2, TT * HEADS])
        ssum2 = sb("ssum2", [P, TT])
        ssq = sb("ssq", [P, 2, TT])
        rstd2 = sb("rstd2", [P, TT])
        den = sb("den", [P, TT])
        rows = sb("rows", [P, S])
        mrow = sb("mrow", [HEADS, S + NCH])
        grow = am[0:HEADS, :, :].rearrange("p a (r s) -> p (a r) s", s=S)
        mst = sb("mst", [HEADS, NCH + 1])
        cols = sb("cols", [P, TT, P])
        sdec = sb("sdec", [P, HEADS, NCH])
        kT = gg[:, :, :].rearrange("p a (b c) -> p (a b) c", c=S)
        prob = e1[:, :, :].rearrange("p (r a) m -> p r a m", r=2)
        probT = cum[:, 0:TT, :]
        mx = sb("mx", [P, TT])
        nmx = sb("nmx", [P, 2, TT])
        rsum = sb("rsum", [P, 2, TT])
        rinv = sb("rinv", [P, TT])
        xqT = gqk
        sg = mo[:, :, 0:HB]
        hid = am[:, :, 0:HB]
        hidT = [f[:, 0:4, :].rearrange("p (t c) s -> p t (c s)", t=TT) for f in (Hhi, Hlo)]
        hg = [[f[:, :, r * P:(r + 1) * P] for f in (Bhi, Blo)] for r in range(2)]
        yacc = gv[:, 0, :]
        onehot = gg[:, 0, 0:TT * P].rearrange("p (t j) -> p t j", t=TT)
        gated = gg[:, 0, 256:256 + TT * P].rearrange("p (t j) -> p t j", t=TT)
        gatedT = gg[:, 0, 512:512 + S]
        gain = junk[:, :]
        rw = sb("rw", [P, KC, NE])
        rw_hi, rw_lo = sb("rw_hi", [P, KC, NE], F32R), sb("rw_lo", [P, KC, NE], F32R)
        logitT = sb("logitT", [NE, S])
        logit = sb("logit", [P, TT, NE])
        top = sb("top", [P, TT, NE])
        topi = sb("topi", [P, TT, NE], U32)
        topf = sb("topf", [P, TT, NE])
        tw = sb("tw", [P, TT, 4])
        oh = sb("oh", [P, TT, 2, NE])
        chosen = sb("chosen", [P, TT, NE + 1])
        gates = sb("gates", [P, TT, NE + 1])
        place = sb("place", [P, TT, NE + 1])
        place_p = sb("place_p", [P, TT, NE])
        most = sb("most", [P, 2])[:, 0:1]
        npass_i = sb("npass_i", [P, 1], I32)

        def is_columns(k):
            return k < MIX_BLOCKS and BLOCKS[k][0] in COLUMN_BLOCKS

        def raw_half(k, half, kind):
            cols = {"rows": 512, "columns": 256, "down": 1024}[kind]
            return raw[:, (2 * k + half) % RAW, :].rearrange("p (k n) -> p k n", n=cols)

        def raw_piece(k, p, kind, w=512):
            h = raw_half(k, p // 2, kind)
            if kind == "columns":
                return h[:, :, (p % 2) * P:(p % 2 + 1) * P]
            if kind == "rows":
                return h[:, 2 * (p % 2):2 * (p % 2) + 2, 0:w]
            return h[:, p % 2:p % 2 + 1, :]

        def split_piece(part, k, p, kind, w=512):
            cols = {"rows": 512, "columns": P, "down": 1024}[kind]
            v = part[:, (PIECES * k + p) % SPLIT, :].rearrange("p (k n) -> p k n", n=cols)
            return v[:, :, 0:w] if kind == "rows" else v

        def kind_of(k):
            if k < MIX_BLOCKS:
                return "columns" if is_columns(k) else "rows"
            f = k - MIX_BLOCKS
            return "down" if f >= 2 and (f % 3 == 0 or f == DENSE_BLOCKS - 1) else "rows"

        layer_sems = []

        def lsem(name):
            layer_sems.append(sem(name))
            return layer_sems[-1]

        pe_piece = lsem("pe_piece")
        hi_done, lo_done = lsem("hi_done"), lsem("lo_done")
        pe_group = lsem("pe_group")
        moved = [lsem(f"moved{b}") for b in range(GROUP_BANKS)]
        dve_own, act_own, pool_own = lsem("dve_own"), lsem("act_own"), lsem("pool_own")
        L = {n: lsem(n) for n in (
            "sq_done", "var_done", "root_done", "inverse_done", "xn_ready", "xn_second", "decay_z", "decay_e",
            "cum_ready", "e_ready", "gla_in",
            "conv_out", "qk_ready", "row_abs", "row_ln", "row_dm", "row_exp", "rows_ready", "values_ready",
            "h_scores", "h_masked", "h_keys", "h_keys_sb", "h_dstate", "h_state", "h_out", "h_outsb",
            "h_bcast", "h_dexp_in", "h_dexp", "h_qs", "h_den", "h_sq",
            "norm_var", "norm_root", "gated_g", "gated_m", "gate_z",
            "turn_ps", "turn_hi", "turn_lo", "small_hi", "small_lo",
            "mem_hi", "mem_t", "x_score", "x_negmax", "x_exp", "x_prob", "x_pt", "x_pt_sb", "x_o", "x_o_hi", "x_o_sb",
            "gate_ps", "up_ps", "silu_done", "hid_ready", "hid_tr", "hidT_hi", "hidT_ready", "y_ps", "y_done",
            "logit_ps", "logitT_sb", "count_in", "top_e_in", "top_e", "count_ps", "npass_ready", "onehot_ready", "gather_ps",
            "gather_hi",
            "gather_sb", "gated_ps", "gated_sb", "y_left", "y_right", "scatter_ps", "scattered", "gain_in", "pool_in_layer")}
        vec_in = sem("vec_in")
        router_in = sem("router_in")
        x_in = sem("x_in")
        mem_in = sem("mem_in")
        const_ready = sem("const_ready")
        last_in = sem("last_in")
        full = [sem(f"full{s}") for s in range(RAW)]
        layer_done = sem("layer_done")
        layer_go = sem("layer_go")
        layer_seen = sem("layer_seen")
        mem_ready = sem("mem_ready")
        mem_sq = sem("mem_sq")
        mem_var = sem("mem_var")
        mem_root = sem("mem_root")
        mem_n = sem("mem_n")
        mem_tp = sem("mem_tp")
        fin_sq, fin_var, fin_root, fin_out, out_done = sem("fin_sq"), sem("fin_var"), sem("fin_root"), sem("fin_out"), sem("out_done")
        ENGINES = 5
        dve_q, dve_p = lsem("dve_q"), lsem("dve_p")

        def group(*name):
            g = GROUPS[name]
            return bank[g % GROUP_BANKS], moved[g % GROUP_BANKS], g // GROUP_BANKS + 1

        def turn_no(name, j):
            n = 4 * TURNS.index(name) + j
            return n, bank[2 + n % 6]

        def wait_turned(eng, name, j):
            eng.wait_ge(L["turn_lo"], turn_no(name, j)[0] + 1)

        def wait_group(eng, *name):
            eng.wait_ge(pe_group, GROUPS[name] + 1)

        def wait_moved(eng, *name):
            g = GROUPS[name]
            eng.wait_ge(moved[g % GROUP_BANKS], g // GROUP_BANKS + 1)

        def wait_full(eng, l, k, p, steps=0):
            half = 2 * k + p // 2
            n = l * LAYER_LOADS + steps * (6 // RAW) + (half // RAW + 1)
            eng.wait_ge(full[half % RAW], n * 16)

        def wait_used(eng, k, p):
            g = ends_group(k, p)
            if g is None:
                eng.wait_ge(pe_piece, LOOSE[(k, p)])
            else:
                wait_group(eng, *g)

        def ahead(k, p):
            s = PIECES * k + p + SPLIT
            return s // PIECES, s % PIECES

        def step_of(f, steps):
            if f < 2:
                return ("gate", "up")[f], 0
            if f == 3 * steps - 1:
                return "down", steps - 1
            if steps == MOE_STEPS and f >= 3 * steps - 3:
                return ("up", steps - 1) if f == 3 * steps - 3 else ("down", steps - 2)
            return ("gate", "down", "up")[(f + 1) % 3], (f + 1) // 3 - ((f + 1) % 3 == 1)

        def wait_piece(eng, f, p, steps, before=0, before_steps=0):
            what, i = step_of(f, steps)
            last = dense_pieces(f) - 1 if steps == DENSE_STEPS else PIECES - 1
            if p < last:
                eng.wait_ge(pe_piece, (before + before_steps) * (3 * (PIECES - 1)) + (MIX_LOOSE + f * (PIECES - 1) + p + 1))
            else:
                done = L[{"gate": "gate_ps", "up": "up_ps", "down": "y_ps"}[what]]
                eng.wait_ge(done, before + before_steps + (i + 1))

        def dense_width(i):
            return HB if i < DENSE_STEPS - 1 else DENSE_TAIL

        def dense_pieces(f):
            return (DENSE_TAIL + P - 1) // P if f == DENSE_BLOCKS - 1 else PIECES

        def dense_ahead(f, p):
            f, p = ahead(f, p)
            if f >= DENSE_BLOCKS or p >= dense_pieces(f):
                return None
            what, i = step_of(f, DENSE_STEPS)
            if what != "down":
                return f, p, "rows", dense_width(i), P, p
            tail = i == DENSE_STEPS - 1
            return f, p, "down", None, min(P, DENSE_TAIL - p * P) if tail else P, 2 * p if tail else p

        def wait_lo(eng, f, p, more=0):
            eng.wait_ge(hi_done, more + (PIECES * (MIX_BLOCKS + f) + p + 1))

        def moe_kind(f):
            return "down" if step_of(f, MOE_STEPS)[0] == "down" and f < MOE_BLOCKS else "rows"

        block = ctx.enter_context(nc.Block())

        def layer_end(eng, l, last=None):
            eng.wait_ge(L["pool_in_layer"], 1)
            eng.drain().then_inc(layer_done, 1)
            eng.wait_ge(layer_go, 1)
            eng.sem_inc(layer_seen, 1)

        @block.sync
        def _(sp):
            sp.dma_start(x[:, :, :], t["x"][0].rearrange("(a p) d -> p a d", p=P)).then_inc(x_in, 16)

            def load(l, k, half):
                name, j = BLOCKS[k]
                if name in OFF:
                    src, col = t["w_in"][l], OFF[name] + 512 * j
                elif name == "x_wk":
                    src, col = t["x_wkv"][l], 512 * j
                elif name == "x_wv":
                    src, col = t["x_wkv"][l], D + 512 * j
                else:
                    src, col = t[name][l], 512 * j
                if is_columns(k):
                    a = src[:, col + 256 * half:col + 256 * (half + 1)]
                else:
                    a = src[512 * half:512 * (half + 1), col:col + 512]
                sp.dma_start(raw_half(k, half, kind_of(k)), a.rearrange("(k p) n -> p k n", p=P))\
                    .then_inc(full[(2 * k + half) % RAW], 16)

            def wait_free(k, half, expert=None):
                n = 2 * (2 * k + half - RAW) + 2
                if expert is not None:
                    n = n + expert * (PIECES * MOE_BLOCKS)
                sp.wait_ge(lo_done, n)

            for n in range(RAW):
                load(0, n // 2, n % 2)
            with sp.Fori(0, DEPTH) as l:
                for n in range(RAW, 2 * MIX_BLOCKS):
                    wait_free(n // 2, n % 2)
                    load(l, n // 2, n % 2)
                with sp.If(l == 0):
                    def dense_load(f, what, i):
                        k = MIX_BLOCKS + f
                        w = HB if i < DENSE_STEPS - 1 else DENSE_TAIL
                        for half in range(2):
                            wait_free(k, half)
                            slot = full[(2 * k + half) % RAW]
                            if what != "down":
                                col = HB * i + (FFN if what == "up" else 0)
                                sp.dma_start(raw_half(k, half, "rows")[:, :, 0:w],
                                             t["ffn_w13"][0, 512 * half:512 * (half + 1), col:col + w].rearrange(
                                                 "(k p) n -> p k n", p=P)).then_inc(slot, 16)
                            elif w == HB:
                                row = HB * i + 256 * half
                                sp.dma_start(raw_half(k, half, "down"), t["ffn_w2"][0, row:row + 256, :].rearrange(
                                    "(k p) n -> p k n", p=P)).then_inc(slot, 16)
                            else:
                                row = HB * i + P * half
                                m = min(P, w - P * half)
                                sp.dma_start(raw_half(k, 0, "down")[0:m, half, :], t["ffn_w2"][0, row:row + m, :])\
                                    .then_inc(slot, 16)

                    dense_load(0, "gate", 0)
                    dense_load(1, "up", 0)
                    for i in range(1, DENSE_STEPS):
                        dense_load(3 * i - 1, "gate", i)
                        dense_load(3 * i, "down", i - 1)
                        dense_load(3 * i + 1, "up", i)
                    dense_load(DENSE_BLOCKS - 1, "down", DENSE_STEPS - 1)
                    sp.wait_ge(lo_done, PIECES * (MIX_BLOCKS + DENSE_BLOCKS - 1) + 2)
                    for n in range(RAW):
                        load(1, n // 2, n % 2)
                with sp.Else():
                    def moe_load(q, e, f, what, i, base=None):
                        k = MIX_BLOCKS + f
                        for half in range(2):
                            n = q * (PIECES * MOE_BLOCKS) + 2 * (2 * k + half - RAW) + 2
                            if base is not None:
                                n = n + base * (3 * PIECES)
                            sp.wait_ge(lo_done, n)
                            slot = full[(2 * k + half) % RAW]
                            if what == "down":
                                src = t["moe_w2"][0, e, bass.ts(i, HB), :][256 * half:256 * (half + 1), :]
                            elif what == "up":
                                src = t["moe_w13"][0, e, :, EXP:2 * EXP][512 * half:512 * (half + 1), bass.ts(i, HB)]
                            else:
                                src = t["moe_w13"][0, e, 512 * half:512 * (half + 1), bass.ts(i, HB)]
                            sp.dma_start(raw_half(k, half, "down" if what == "down" else "rows"),
                                         src.rearrange("(k p) n -> p k n", p=P)).then_inc(slot, 16)

                    moe_load(0, 0, 0, "gate", 0)
                    sp.wait_ge(L["npass_ready"], 1)
                    npass = sp.value_load(npass_i[0:1, 0:1], min_val=1, max_val=TT)
                    with sp.Fori(0, npass) as ps:
                        def expert(q, e):
                            moe_load(q, e, 1, "up", 0)
                            with sp.Fori(1, MOE_STEPS - 1) as i:
                                moe_load(q, e, 2, "gate", i, i - 1)
                                moe_load(q, e, 3, "down", i - 1, i - 1)
                                moe_load(q, e, 4, "up", i, i - 1)
                            moe_load(q, e, MOE_BLOCKS - 4, "gate", MOE_STEPS - 1)
                            moe_load(q, e, MOE_BLOCKS - 3, "up", MOE_STEPS - 1)
                            moe_load(q, e, MOE_BLOCKS - 2, "down", MOE_STEPS - 2)
                            moe_load(q, e, MOE_BLOCKS - 1, "down", MOE_STEPS - 1)

                        with sp.Fori(0, NE - 1) as e:
                            q = ps * NE + e
                            expert(q, e)
                            moe_load(q + 1, e + 1, 0, "gate", 0)
                        expert(ps * NE + (NE - 1), NE - 1)
                        moe_load(ps * NE + NE, 0, 0, "gate", 0)
                sp.nop()
                layer_end(sp, l)
            sp.wait_ge(fin_out, 2)
            sp.dma_start(out[0].rearrange("(a p) d -> p a d", p=P), xn[:, :, :]).then_inc(out_done, 16)
            sp.wait_ge(out_done, 16)

        @block.gpsimd
        def _(pool):
            n = [0]

            def did(ins):
                n[0] += 1
                ins.then_inc(const_ready, 1)

            def ordered():
                pool.wait_ge(const_ready, n[0])

            pool.dma_start(xn[:, :, :], t["mem"][0].rearrange("(a p) d -> p a d", p=P)).then_inc(mem_in, 16)
            did(pool.memset(ident[:, :], 0.0))
            did(pool.memset(tri[:, :], 1.0))
            did(pool.memset(ones[:, :], 1.0))
            did(pool.memset(causal[:, :], 1.0))
            did(pool.memset(restart[:, :], 1.0))
            did(pool.memset(pick[:, :, :], 0.0))
            did(pool.memset(zrow[:, :], 0.0))
            did(pool.memset(lnscale[:, :], float(np.log(QK_SCALE))))
            did(pool.memset(rows[:, :], 0.0))
            did(pool.memset(sT[:, :, :], 0.0))
            did(pool.memset(cin[:, :, 0:CONV_W - 1], 0.0))
            did(pool.memset(mv[:, :, :, DV:DV + 1], 1.0))
            did(pool.memset(mst[:, 0:1], 0.0))
            did(pool.iota(slot_no[:, :], [[1, P]], base=0, channel_multiplier=0, allow_small_or_imprecise_dtypes=True))
            did(pool.iota(expert_no[:, :], [[1, NE]], base=0, channel_multiplier=0, allow_small_or_imprecise_dtypes=True))
            ordered()
            did(pool.affine_select(out=ident[:, :], in_=ident[:, :], compare_op=ALU.not_equal, fill=1.0, base=0,
                                   pattern=[[-1, P]], channel_multiplier=1))
            did(pool.affine_select(out=tri[:, :], in_=tri[:, :], compare_op=ALU.is_gt, fill=0.0, base=0,
                                   pattern=[[1, P]], channel_multiplier=-1))
            did(pool.affine_select(out=causal[:, :].rearrange("p (a t) -> p a t", a=TT),
                                   in_=causal[:, :].rearrange("p (a t) -> p a t", a=TT), compare_op=ALU.is_ge, fill=0.0,
                                   base=0, pattern=[[0, TT], [1, P]], channel_multiplier=-1))
            ordered()
            v = causal[:, :].rearrange("p (a c t) -> p a c t", a=TT, c=2)
            did(pool.affine_select(out=v, in_=v, compare_op=ALU.is_ge, fill=0.0, base=0,
                                   pattern=[[0, TT], [-CH, 2], [0, CH]], channel_multiplier=1))
            v = restart[:, :].rearrange("p (c t) -> p c t", t=CH)
            did(pool.affine_select(out=v, in_=v, compare_op=ALU.not_equal, fill=0.0, base=0,
                                   pattern=[[0, NCH], [1, CH]], channel_multiplier=0))
            did(pool.affine_select(out=pick[:, :, :], in_=pick[:, :, :], compare_op=ALU.not_equal, fill=1.0, base=0,
                                   pattern=[[-1, HEADS], [0, P]], channel_multiplier=1))
            ordered()
            did(pool.tensor_scalar(hide[:, :], causal[:, :], -BIG, BIG, ALU.mult, ALU.add))
            ordered()
            assert n[0] == CONSTS, n[0]

            def small_inputs(l):
                for name in VEC:
                    rows_of = {"m_conv": CONV_W * KC, "gla_gk_bias": HEADS}.get(name, KC)
                    src = t[name][l]
                    src = src.rearrange("j (c p) -> (j c) p", p=P) if name == "m_conv" else src.rearrange("(c p) -> c p", p=P)
                    pool.dma_start(vrow[VEC[name]:VEC[name] + rows_of, :], src).then_inc(vec_in, 16)
                pool.dma_start(wsmall[:, :, 0:RANK], t["w_in"][l, :, OFF["g_lr"]:OFF["g_lr"] + RANK].rearrange(
                    "(k p) n -> p k n", p=P)).then_inc(vec_in, 16)
                pool.dma_start(wsmall[:, :, RANK:], t["w_in"][l, :, OFF["m_i"]:OFF["m_i"] + 2 * HEADS].rearrange(
                    "(k p) n -> p k n", p=P)).then_inc(vec_in, 16)
                pool.dma_start(gkup[:, :], t["gla_gk_up"][l]).then_inc(vec_in, 16)
                for c in range(2):
                    pool.dma_start(gbias[:, c:c + 1], t["m_gate_bias"][l, c * HEADS:(c + 1) * HEADS].rearrange(
                        "(h o) -> h o", o=1)).then_inc(vec_in, 16)

            small_inputs(0)
            pool.dma_start(rw[:, :, :], t["moe_router"][0].rearrange("(k p) e -> p k e", p=P)).then_inc(router_in, 16)
            with pool.Fori(0, DEPTH) as l:
                pool.sem_inc(L["pool_in_layer"], 1)
                pool.wait_ge(pe_group, GROUPS[("decay", 1)] + 1)
                pool.wait_ge(L["row_dm"], 1)
                with pool.If(l == 0):
                    small_inputs(1)
                pool.wait_ge(layer_done, ENGINES - 1)
                for s_ in layer_sems:
                    pool.sem_clear(s_)
                pool.sem_clear(layer_done)
                pool.sem_inc(layer_go, 1)
                pool.wait_ge(layer_seen, ENGINES - 1)
                pool.sem_clear(layer_go)
                pool.sem_clear(layer_seen)

        @block.tensor
        def _(pe):
            pe.wait_ge(const_ready, CONSTS)

            def turn_mem():
                pe.wait_ge(mem_n, 2)
                for j in range(4):
                    for k in range(2):
                        for a in range(TT):
                            ins = pe.transpose(bank[j][:, (k * TT + a) * P:(k * TT + a + 1) * P],
                                               gg[:, a, (2 * j + k) * P:(2 * j + k + 1) * P], ident[:, :])
                    ins.then_inc(mem_tp, 1)
                pe.wait_ge(mem_ready, 4)

            turn_mem()

            with pe.Fori(0, DEPTH) as l:
                def begin(*name):
                    g = GROUPS[name]
                    if g >= GROUP_BANKS:
                        pe.wait_ge(moved[g % GROUP_BANKS], g // GROUP_BANKS)
                    return bank[g % GROUP_BANKS]

                def end(ins):
                    ins.then_inc(pe_group, 1)

                def turn(name, src, j):
                    n, b = turn_no(name, j)
                    if n >= 6:
                        pe.wait_ge(L["turn_lo"], n - 5)
                    for k in range(2):
                        for a in range(TT):
                            ins = pe.transpose(b[:, (k * TT + a) * P:(k * TT + a + 1) * P],
                                               src[:, a, (2 * j + k) * P:(2 * j + k + 1) * P], ident[:, :])
                    ins.then_inc(L["turn_ps"], 1)

                def product(ps, moving, stationary, start, stop):
                    pe.matmul(ps, stationary[0], moving[0], start=start, stop=False)
                    pe.matmul(ps, stationary[0], moving[1], start=False, stop=False)
                    return pe.matmul(ps, stationary[1], moving[0], start=False, stop=stop)

                def both(pair, *index):
                    return [f[index] for f in pair]

                ALL = slice(None)

                H, B = (Hhi, Hlo), (Bhi, Blo)

                def weights(k, p, kind, w=512):
                    return [split_piece(f, k, p, kind, w) for f in (whi, wlo)]

                def rows_out(k, src, turn_name=None, before=None, after=None):
                    name, j = BLOCKS[k]
                    for p in range(PIECES):
                        if before is not None:
                            before(p)
                        if turn_name is not None:
                            wait_turned(pe, turn_name, p)
                        pe.wait_ge(lo_done, PIECES * k + p + 1)
                        w = weights(k, p, "rows")
                        for a in range(TT):
                            ps = begin(name, j, a) if p == 0 else bank[GROUPS[(name, j, a)] % GROUP_BANKS]
                            for c in range(2):
                                ins = product(ps[:, :], both(w, ALL, c, ALL),
                                              both(src, ALL, 2 * p + c, slice(a * P, (a + 1) * P)),
                                              start=(p == 0 and c == 0), stop=(p == PIECES - 1 and c == 1))
                            if p == PIECES - 1:
                                end(ins)
                        if p < PIECES - 1:
                            ins.then_inc(pe_piece, 1)
                        if after is not None:
                            after(p)

                def channels_out(k, src, turn_name=None):
                    name, j = BLOCKS[k]
                    for p in range(PIECES):
                        pe.wait_ge(lo_done, PIECES * k + p + 1)
                        w = weights(k, p, "columns")
                        ps = begin(name, j, p // 2) if p % 2 == 0 else bank[GROUPS[(name, j, p // 2)] % GROUP_BANKS]
                        for c in range(KC):
                            if turn_name is not None and p == 0 and c % 2 == 0:
                                wait_turned(pe, turn_name, c // 2)
                            ins = product(ps[:, (p % 2) * S:(p % 2 + 1) * S], both(src, ALL, c, ALL), both(w, ALL, c, ALL),
                                          start=(c == 0), stop=(c == KC - 1))
                        if p % 2:
                            end(ins)
                        else:
                            ins.then_inc(pe_piece, 1)

                pe.wait_ge(vec_in, VEC_DMAS * 16 * (l + 1))
                end(pe.transpose(begin("vec", 0)[:, 0:NVEC], vrow[:, :], ident[0:NVEC, 0:NVEC]))
                pe.wait_ge(L["xn_ready"], 1)
                pe.wait_ge(L["xn_second"], 1)
                for j in range(4):
                    turn("mix_t", xn, j)
                pe.wait_ge(L["small_lo"], 1)
                small = (wsmall_hi, wsmall_lo)
                ps = begin("small", 0)
                for k in range(KC):
                    if k % 2 == 0:
                        wait_turned(pe, "mix_t", k // 2)
                    product(ps[0:RANK, 0:S], both(H, ALL, k, ALL), both(small, ALL, k, slice(0, RANK)),
                            start=(k == 0), stop=(k == KC - 1))
                for k in range(KC):
                    ins = product(ps[0:HEADS, S:2 * S], both(H, ALL, k, ALL), both(small, ALL, k, slice(RANK, RANK + HEADS)),
                                  start=(k == 0), stop=(k == KC - 1))
                end(ins)
                ps = begin("small", 1)
                for k in range(KC):
                    ins = product(ps[0:HEADS, 0:S], both(H, ALL, k, ALL),
                                  both(small, ALL, k, slice(RANK + HEADS, RANK + 2 * HEADS)),
                                  start=(k == 0), stop=(k == KC - 1))
                end(ins)
                channels_out(0, H)
                channels_out(1, H)
                wait_moved(pe, "small", 0)
                for a in range(2):
                    ps = begin("decay", a)
                    for c in range(2):
                        ins = pe.matmul(ps[:, c * S:(c + 1) * S], gkup[:, (2 * a + c) * P:(2 * a + c + 1) * P], lrT[:, :],
                                        start=True, stop=True)
                    end(ins)
                channels_out(2, H)
                channels_out(3, H)
                for k in range(4, 8):
                    rows_out(k, H)
                pe.wait_ge(L["rows_ready"], 1)
                ps = begin("gate_cols", 0)
                for a in range(TT):
                    ins = pe.transpose(ps[:, a * P:(a + 1) * P], rows[:, a * P:(a + 1) * P], ident[:, :])
                end(ins)

                def head_scores(n):
                    h = n % HEADS
                    if n == 0:
                        pe.wait_ge(L["gla_in"], 1)
                    if n == HEADS:
                        pe.wait_ge(L["qk_ready"], 1)
                    if n > 0:
                        pe.wait_ge(L["h_masked"], n)
                    q_, k_, turned_ = ((gqT[:, h, :], gkT[:, h, :], gkeT[:, h, :]) if n < HEADS else
                                       (qk[:, h, :], qk[:, HEADS + h, :], qk[:, HEADS + h, :]))
                    for a in range(TT):
                        pe.matmul(bank[2][:, a * P:(a + 1) * P], k_[:, a * P:(a + 1) * P], q_[:, a * P:(a + 1) * P],
                                  start=True, stop=True)
                    for a in range(TT):
                        ins = pe.transpose(bank[2][:, (TT + a) * P:(TT + a + 1) * P], turned_[:, a * P:(a + 1) * P],
                                           ident[:, :])
                    ins.then_inc(L["h_scores"], 1)

                def head_rows(n):
                    h = n % HEADS
                    if n >= HEADS:
                        pe.wait_ge(L["h_state"], 3 * n - 1)
                        if n > HEADS:
                            pe.wait_ge(L["h_qs"], h)
                        pe.matmul(bank[3][:, 0:S + NCH], pick[:, h, :], mrow[:, :], start=True, stop=True)
                        pe.matmul(bank[4][:, 0:S], pick[:, h, :], grow[:, 5, :], start=True, stop=True)\
                            .then_inc(L["h_bcast"], 1)

                def head_values(n, r, a):
                    h = n % HEADS
                    return gv[r, a, h * DV:(h + 1) * DV] if n < HEADS else mv[r, a, h, :]

                def head_increments(n, chunks):
                    width = DV if n < HEADS else DV + 1
                    if n == 0:
                        for j in range(2):
                            for a in range(TT):
                                wait_moved(pe, "g_v", j, a)
                    if n == HEADS:
                        for j in range(2):
                            for a in range(TT):
                                wait_moved(pe, "m_v", j, a)
                    pe.wait_ge(L["h_keys_sb"], n + 1)
                    if n > 0:
                        pe.wait_ge(L["h_state"], 3 * n)
                    if n >= HEADS:
                        pe.wait_ge(L["h_qs"], n - HEADS + 1)
                    for c in chunks:
                        r = slice((c % 2) * CH, (c % 2 + 1) * CH)
                        if c == 2:
                            pe.wait_ge(L["h_state"], 3 * n + 1)
                        pe.matmul(bank[(5, 3)[c % 2]][:, 0:width], kn[r, c // 2, :], head_values(n, r, c // 2),
                                  start=True, stop=True).then_inc(L["h_dstate"], 1)

                def head_outputs(n):
                    h = n % HEADS
                    width = DV if n < HEADS else DV + 1
                    weight = sT[:, n % 2, :] if n < HEADS else wT[:, n % 2, :]
                    query = gqT[:, h, :] if n < HEADS else qs[:, n % 2, :]
                    pe.wait_ge(L["h_masked"], n + 1)
                    if n > 0:
                        pe.wait_ge(L["h_outsb"], TT * n)
                    for a in range(TT):
                        for c in (2 * a, 2 * a + 1):
                            r = slice((c % 2) * CH, (c % 2 + 1) * CH)
                            ins = pe.matmul(bank[6 + a][r, 0:width], weight[r, c * CH:(c + 1) * CH], head_values(n, r, a),
                                            start=True, stop=(c == 0))
                            if c > 0:
                                pe.wait_ge(L["h_state"], 3 * n + c)
                                ins = pe.matmul(bank[6 + a][r, 0:width], query[:, c * CH:(c + 1) * CH], st[:, c - 1, 0:width],
                                                start=False, stop=True)
                        ins.then_inc(L["h_out"], 1)

                def gap(i):
                    if 0 <= i - 2 < 2 * HEADS:
                        head_outputs(i - 2)
                    if 0 <= i - 1 < 2 * HEADS:
                        head_increments(i - 1, range(NCH - 2))
                    if i < 2 * HEADS:
                        head_scores(i)
                    if 0 <= i - 1 < 2 * HEADS:
                        head_increments(i - 1, (NCH - 2,))
                    if i < 2 * HEADS:
                        head_rows(i)

                for k in GAP_BLOCKS:
                    rows_out(k, H, after=lambda p: gap(2 * (k - GAP_BLOCKS[0]) + p // 2) if p % 2 else None)

                pe.wait_ge(L["h_outsb"], TT * 2 * HEADS)
                pe.wait_ge(L["h_masked"], 2 * HEADS)
                pe.wait_ge(L["h_state"], 3 * 2 * HEADS)
                pe.wait_ge(L["h_qs"], HEADS)
                pe.wait_ge(L["gated_g"], TT * HEADS)
                for j in range(4):
                    turn("gla_t", xn, j)
                pe.wait_ge(L["gated_m"], TT * HEADS)
                for j in range(4):
                    turn("m_t", om, j)
                for k in (16, 17):
                    rows_out(k, B, turn_name="gla_t")
                for k in (18, 19):
                    rows_out(k, H, turn_name="m_t")
                for j in range(4):
                    if j % 2 == 0:
                        for a in range(TT):
                            wait_moved(pe, "m_proj", j // 2, a)
                    turn("merged_t", ag, j)
                for k in (20, 21):
                    rows_out(k, B, turn_name="merged_t")

                pe.wait_ge(L["mem_t"], KC)
                channels_out(22, H)
                channels_out(23, H)
                rows_out(24, H)
                rows_out(25, H)
                pe.wait_ge(L["xn_ready"], 2)
                pe.wait_ge(L["xn_second"], 2)
                for j in range(4):
                    turn("x_t", xn, j)

                def scores(h):
                    for a in range(2):
                        wait_moved(pe, "x_wq", h // 2, a)
                    if h >= 2:
                        pe.wait_ge(L["x_exp"], TT * (h - 1))
                    for a in range(TT):
                        for c in range(2):
                            ins = pe.matmul(bank[4 + h % 2][:, a * M:(a + 1) * M], xqT[:, 2 * h + c, a * P:(a + 1) * P],
                                            kT[:, 2 * h + c, :], start=(c == 0), stop=(c == 1))
                    ins.then_inc(L["x_score"], 1)

                def turn_prob(h):
                    pe.wait_ge(L["x_prob"], h + 1)
                    if h > 0:
                        pe.wait_ge(L["x_pt_sb"], h)
                    for m in range(2):
                        for a in range(TT):
                            ins = pe.transpose(bank[6][:, (m * TT + a) * P:(m * TT + a + 1) * P],
                                               prob[:, h % 2, a, m * P:(m + 1) * P], ident[:, :])
                    ins.then_inc(L["x_pt"], 1)

                def attend(h):
                    pe.wait_ge(L["x_pt_sb"], h + 1)
                    if h > 0:
                        pe.wait_ge(L["x_o_sb"], h)
                    for c in range(2):
                        for m in range(2):
                            ins = pe.matmul(bank[7][:, c * S:(c + 1) * S],
                                            gv[:, m, h * DV + c * P:h * DV + (c + 1) * P], probT[:, m, :],
                                            start=(m == 0), stop=(m == 1))
                    ins.then_inc(L["x_o"], 1)

                channels_out(26, B, turn_name="x_t")
                scores(0)
                scores(1)
                channels_out(27, B)
                turn_prob(0)
                scores(2)
                attend(0)
                turn_prob(1)
                scores(3)
                attend(1)

                def after_piece(p):
                    if p == 1:
                        attend(2)
                    if p == 2:
                        attend(3)
                    if p < 2:
                        turn_prob(p + 2)

                rows_out(28, H, before=lambda p: pe.wait_ge(L["x_o_sb"], p + 1), after=after_piece)
                rows_out(29, H)

                pe.wait_ge(L["xn_ready"], 3)
                pe.wait_ge(L["xn_second"], 3)
                pe.wait_ge(L["x_exp"], TT * HEADS)
                pe.wait_ge(L["x_pt_sb"], HEADS)
                pe.wait_ge(L["x_o_sb"], HEADS)
                for j in range(4):
                    turn("ffn_t", xn, j)
                for j in range(4):
                    wait_turned(pe, "ffn_t", j)
                for a in range(TT):
                    wait_moved(pe, "x_wo", 1, a)
                GATE, UP, Y = (0, 5), (1, 6), ((3, 4), (2, 7))

                def ff_wait(f, p, q):
                    n = PIECES * (MIX_BLOCKS + f) + p + 1
                    pe.wait_ge(lo_done, n if q is None else q + n)

                def ff_columns(f, src, banks, tiles, w, done, q=None, after=None):
                    for p in range(PIECES):
                        ff_wait(f, p, q)
                        wt = weights(MIX_BLOCKS + f, p, "rows", w)
                        for a in range(tiles):
                            for c in range(2):
                                ins = product(bank[banks[a]][:, 0:w], both(wt, ALL, c, ALL),
                                              both(src, ALL, 2 * p + c, slice(a * P, (a + 1) * P)),
                                              start=(p == 0 and c == 0), stop=(p == PIECES - 1 and c == 1))
                        ins.then_inc(pe_piece if p < PIECES - 1 else done, 1)
                        if after is not None:
                            after(p)

                def at_piece(n, work):
                    return lambda p: work() if p == n else None

                def ff_turn(tiles, w, n):
                    pe.wait_ge(L["hid_ready"], n + 1)
                    for a in range(tiles):
                        for k in range((w + P - 1) // P):
                            m = min(P, w - k * P)
                            ins = pe.transpose(bank[UP[a]][0:m, k * P:(k + 1) * P], hid[:, a, k * P:k * P + m], ident[:, :])
                    ins.then_inc(L["hid_tr"], 1)

                def ff_down(f, tiles, w, n, first, last, q=None, half=0, after=None):
                    pe.wait_ge(L["hidT_ready"], n + 1)
                    chunks = (w + P - 1) // P
                    for p in range(chunks):
                        ff_wait(f, p, q)
                        wt = weights(MIX_BLOCKS + f, p, "down")
                        m = min(P, w - p * P)
                        for a in range(tiles):
                            for c in range(2):
                                ins = product(bank[Y[a][c]][:, :], both(wt, slice(0, m), 0, slice(c * 512, (c + 1) * 512)),
                                              both(hidT, slice(0, m), a + half, slice(p * P, (p + 1) * P)),
                                              start=(first and p == 0), stop=(last and p == chunks - 1))
                        ins.then_inc(pe_piece if p < chunks - 1 else L["y_ps"], 1)
                        if after is not None:
                            after(p)

                with pe.If(l == 0):
                    def w_of(i):
                        return HB if i < DENSE_STEPS - 1 else DENSE_TAIL

                    ff_columns(0, B, GATE, TT, HB, L["gate_ps"])
                    ff_columns(1, B, UP, TT, HB, L["up_ps"])
                    for i in range(1, DENSE_STEPS):
                        pe.wait_ge(L["silu_done"], i)
                        ff_columns(3 * i - 1, B, GATE, TT, w_of(i), L["gate_ps"], after=at_piece(0, lambda: ff_turn(TT, HB, i - 1)))
                        ff_down(3 * i, TT, HB, i - 1, first=(i == 1), last=False)
                        ff_columns(3 * i + 1, B, UP, TT, w_of(i), L["up_ps"])
                    i = DENSE_STEPS
                    ff_turn(TT, DENSE_TAIL, i - 1)
                    ff_down(3 * i - 1, TT, DENSE_TAIL, i - 1, first=False, last=True)
                    pe.wait_ge(L["y_done"], 1)
                with pe.Else():
                    pe.wait_ge(L["small_lo"], 2)
                    for k in range(KC):
                        ins = product(bank[4][0:NE, 0:S], both(B, ALL, k, ALL), both((rw_hi, rw_lo), ALL, k, ALL),
                                      start=(k == 0), stop=(k == KC - 1))
                    ins.then_inc(L["logit_ps"], 1)
                    pe.wait_ge(L["logitT_sb"], 1)
                    for a in range(TT):
                        ins = pe.transpose(bank[3][:, a * NE:(a + 1) * NE], logitT[:, a * P:(a + 1) * P], ident[0:NE, 0:NE])
                    ins.then_inc(L["logit_ps"], 1)
                    pe.wait_ge(L["count_in"], 1)
                    pe.matmul(bank[5][:, 0:NE], tri[:, :], chosen[:, 0, 0:NE], start=True, stop=True)
                    pe.matmul(bank[5][:, NE:2 * NE], tri[:, :], chosen[:, 1, 0:NE], start=True, stop=False)
                    pe.matmul(bank[5][:, NE:2 * NE], ones[:, :], chosen[:, 0, 0:NE], start=False, stop=True)
                    pe.matmul(bank[5][:, 2 * NE:3 * NE], ones[:, :], chosen[:, 0, 0:NE], start=True, stop=False)
                    pe.matmul(bank[5][:, 2 * NE:3 * NE], ones[:, :], chosen[:, 1, 0:NE], start=False, stop=True)\
                        .then_inc(L["count_ps"], 1)
                    pe.wait_ge(L["npass_ready"], 1)
                    npass = pe.value_load(npass_i[0:1, 0:1], min_val=1, max_val=TT)

                    def gather(n, part):
                        if part == 0:
                            pe.wait_ge(L["onehot_ready"], n + 1)
                        for k in (2 * part, 2 * part + 1):
                            for a in range(TT):
                                ins = pe.matmul(bank[5 + k // 4][:, (k % 4) * P:(k % 4 + 1) * P],
                                                xn[:, a, k * P:(k + 1) * P], onehot[:, a, :], start=(a == 0), stop=(a == 1))
                        if part == 3:
                            ins.then_inc(L["gather_ps"], 1)

                    def scatter(n, part):
                        a, c = part // 2, part % 2
                        if part == 0:
                            pe.wait_ge(L["gated_sb"], n + 1)
                        if c == 0:
                            pe.wait_ge(L["y_left"], n + 1)
                        else:
                            pe.wait_ge(L["y_right"], n + 1)
                        pe.matmul(bank[(5, 6, 7, 2)[part]][:, :], gatedT[:, a * P:(a + 1) * P],
                                  yacc[:, c * 512:(c + 1) * 512], start=True, stop=True).then_inc(L["scatter_ps"], 1)

                    def expert(q, g, tokens):
                        at = q * (PIECES * MOE_BLOCKS)

                        def turn_gates():
                            pe.wait_ge(L["scattered"], q + 1)
                            for a in range(TT):
                                ins = pe.transpose(bank[7][:, a * P:(a + 1) * P], gated[:, a, :], ident[:, :])
                            ins.then_inc(L["gated_ps"], 1)

                        pe.wait_ge(L["gather_sb"], g + 1)
                        def between(p):
                            if p == 0:
                                scatter(q, 3)
                            if p == 2:
                                turn_gates()

                        ff_columns(0, tokens, GATE, 1, HB, L["gate_ps"], at, lambda p: scatter(q, p - 1) if p > 0 else None)
                        ff_columns(1, tokens, UP, 1, HB, L["up_ps"], at, between)

                        def step(i, at, first):
                            n = q * MOE_STEPS + i
                            pe.wait_ge(L["silu_done"], n)
                            ff_columns(2, tokens, GATE, 1, HB, L["gate_ps"], at, at_piece(1, lambda: ff_turn(1, HB, n - 1)))
                            ff_down(3, 1, HB, n - 1, first, False, at)
                            ff_columns(4, tokens, UP, 1, HB, L["up_ps"], at)

                        step(1, at, True)
                        with pe.Fori(2, MOE_STEPS - 1) as i:
                            step(i, at + (i - 1) * (3 * PIECES), False)
                        n = q * MOE_STEPS + MOE_STEPS - 1
                        f = MOE_BLOCKS - 4
                        pe.wait_ge(L["silu_done"], n)
                        ff_columns(f, tokens, GATE, 1, HB, L["gate_ps"], at, at_piece(1, lambda: ff_turn(1, HB, n - 1)))
                        pe.wait_ge(L["hidT_ready"], n)
                        ff_columns(f + 1, tokens, UP, 1, HB, L["up_ps"], at, lambda p: gather(g + 1, p))
                        ff_down(f + 2, 1, HB, n - 1, False, False, at, after=at_piece(1, lambda: ff_turn(1, HB, n)))
                        ff_down(f + 3, 1, HB, n, False, True, at, half=1)

                    with pe.Fori(0, npass) as ps_:
                        for part in range(4):
                            gather(ps_ * (NE + 1), part)
                        with pe.Fori(0, NE // 2) as pair:
                            for r in range(2):
                                e = 2 * pair + r
                                expert(ps_ * NE + e, ps_ * (NE + 1) + e, hg[r])
                        pe.wait_ge(L["gather_sb"], (ps_ + 1) * (NE + 1))
                    for part in range(4):
                        scatter(npass * NE, part)
                pe.nop()
                layer_end(pe, l)

        @block.scalar
        def _(act):
            step = Steps(act, act_own)

            def chain(ins, sem=None, value=None):
                step.did(ins, sem, value)
                step.wait()

            act.wait_ge(mem_in, 16)
            for a in range(TT):
                act.activation(gv[:, a, :], xn[:, a, :], ACT.Square, accum_out=ssum2[:, a:a + 1]).then_inc(mem_sq, 1)
            act.wait_ge(mem_var, 1)
            act.activation(rstd2[:, :], ssum2[:, :], ACT.Sqrt).then_inc(mem_root, 1)
            act.wait_ge(mem_root, 1)
            act.wait_ge(x_in, 16)
            act.wait_ge(const_ready, CONSTS)

            with act.Fori(0, DEPTH) as l:
                step.n, step.last = 0, None

                def sums(n, j):
                    for a in range(TT):
                        c = slice(j * 512, (j + 1) * 512)
                        chain(act.activation(junk[:, c], x[:, a, c], ACT.Square, accum_out=ssq[:, j, a:a + 1]),
                              L["sq_done"], 2 * TT * n + TT * j + a + 1)

                def root(n):
                    act.wait_ge(L["var_done"], n + 1)
                    chain(act.activation(rstd2[:, :], ssum2[:, :], ACT.Sqrt), L["root_done"], n + 1)

                def second_tile(n):
                    act.wait_ge(L["inverse_done"], n + 1)
                    chain(act.activation(xn[:, 1, :], x[:, 1, :], ACT.Copy, scale=rstd2[:, 1:2]), L["xn_second"], n + 1)

                def turn_hi(name, dst, gain_name):
                    for j in range(4):
                        n, ps = turn_no(name, j)
                        act.wait_ge(L["turn_ps"], n + 1)
                        for k in range(2):
                            c = 2 * j + k
                            scale = vcol[:, VEC[gain_name] + c:VEC[gain_name] + c + 1] if gain_name else 1.0
                            ins = act.activation(dst[:, c, :], ps[:, k * S:(k + 1) * S], ACT.Copy, scale=scale)
                            chain(ins, L["turn_hi"], n + 1) if k else chain(ins)

                def split(k, p, kind, w=512, rows=P):
                    act.activation(split_piece(whi, k, p, kind, w)[0:rows], raw_piece(k, p, kind, w)[0:rows], ACT.Copy)\
                        .then_inc(hi_done, 1)

                def split_ahead(k, p):
                    wait_used(act, k, p)
                    k, p = ahead(k, p)
                    wait_full(act, l, k, p)
                    split(k, p, kind_of(k))

                def blocks(numbers, read, between=None):
                    for k in numbers:
                        name, j = BLOCKS[k]
                        for p in range(PIECES):
                            if read is not None and ends_group(k, p) is not None:
                                for a in ((p // 2,) if is_columns(k) else range(TT)):
                                    read(name, j, a)
                            split_ahead(k, p)
                            if between is not None:
                                between(k, p)

                def read_out(name, dst, func, **kw):
                    wait_group(act, *name)
                    ps, mv_, v = group(*name)
                    chain(act.activation(dst, ps[:, :], func, **kw), mv_, v)

                for j in range(2):
                    sums(0, j)
                root(0)
                second_tile(0)
                act.wait_ge(vec_in, VEC_DMAS * 16 * (l + 1))
                act.activation(wsmall_hi[:, :, :], wsmall[:, :, :], ACT.Copy).then_inc(L["small_hi"], 1)
                for p in range(SPLIT):
                    wait_full(act, l, 0, p)
                    split(0, p, kind_of(0))
                wait_moved(act, "vec", 0)
                turn_hi("mix_t", Hhi, "norm_mix")
                ps, mv_, v = group("small", 0)
                wait_group(act, "small", 0)
                chain(act.activation(grow[:, 0, :], ps[0:HEADS, S:2 * S], ACT.Copy))
                chain(act.activation(lrT[:, :], ps[0:RANK, 0:S], ACT.Copy), mv_, v)
                def read_front(name, j, a):
                    ps, mv_, v = group(name, j, a)
                    wait_group(act, name, j, a)
                    rows_ = "p (c s) -> p c s"
                    if name in ("g_q", "g_k"):
                        dst = (gqT if name == "g_q" else gkT)[:, 2 * a:2 * a + 2, :]
                        src = ps[:, :].rearrange(rows_, c=2)
                    elif name in ("m_q", "m_k"):
                        c = (0 if name == "m_q" else 4) + 2 * a
                        dst = cin[:, c:c + 2, CONV_W - 1:]
                        src = ps[:, :].rearrange(rows_, c=2)
                    elif name == "g_v":
                        dst, src = gv[:, a, j * 512:(j + 1) * 512], ps[:, :]
                    else:
                        dst, src = mv[:, a, 2 * j:2 * j + 2, 0:DV], ps[:, :].rearrange("p (h v) -> p h v", h=2)
                    chain(act.activation(dst, src, ACT.Copy), mv_, v)

                def front(k, p):
                    if (k, p) == (1, 3):
                        act.wait_ge(L["decay_z"], 1)
                        chain(act.activation(e1[:, :, :], e1[:, :, :], ACT.Exp, scale=-1.0))
                        chain(act.activation(e1[:, :, :], e1[:, :, :], ACT.Ln, bias=1.0), L["decay_e"], 1)
                    if (k, p) == (2, 0):
                        act.wait_ge(L["gate_z"], 1)
                        chain(act.activation(grow[:, 2, :], grow[:, 2, :], ACT.Exp, scale=-1.0))
                        chain(act.activation(grow[:, 2, :], grow[:, 2, :], ACT.Ln, bias=1.0), L["row_ln"], 1)
                    if (k, p) == (2, 3):
                        act.wait_ge(L["cum_ready"], 1)
                        chain(act.activation(e1[:, :, :], gkeT[:, :, :], ACT.Exp))
                        chain(act.activation(cum[:, :, :], gkeT[:, :, :], ACT.Exp, scale=-1.0), L["e_ready"], 1)
                    if (k, p) == (5, 3):
                        act.wait_ge(L["row_dm"], 1)
                        chain(act.activation(grow[:, 5, :], grow[:, 4, :], ACT.Exp, scale=-1.0, bias=lnscale[0:HEADS, :]))
                        chain(act.activation(mrow[:, S:], grow[:, 4, CH - 1:S:CH], ACT.Exp, scale=-1.0))
                        chain(act.activation(rows[64:64 + HEADS, :], rows[64:64 + HEADS, :], ACT.Exp))
                        chain(act.activation(rows[96:96 + HEADS, :], rows[96:96 + HEADS, :], ACT.Exp, scale=-1.0),
                              L["rows_ready"], 1)
                    if (k, p) == (7, 1):
                        act.wait_ge(L["conv_out"], 1)
                        chain(act.activation(qk[:, :, :], qk[:, :, :], ACT.Silu), L["qk_ready"], 1)

                blocks(range(8), read_front, front)
                wait_moved(act, "gate_cols", 0)

                def head_outputs(n):
                    h = n % HEADS
                    for a in range(TT):
                        s_ = slice(a * HEADS + h, a * HEADS + h + 1)
                        if n < HEADS:
                            act.wait_ge(L["h_out"], TT * n + a + 1)
                            o = xn[:, a, h * DV:(h + 1) * DV]
                            chain(act.activation(o, bank[6 + a][:, 0:DV], ACT.Copy))
                        else:
                            act.wait_ge(L["h_den"], TT * h + a + 1)
                            o = om[:, a, h * DV:(h + 1) * DV]
                            chain(act.activation(o, bank[6 + a][:, 0:DV], ACT.Copy, scale=den[:, a:a + 1]))
                        chain(act.activation(junk[:, 0:DV], o, ACT.Square, accum_out=ssum[:, n // HEADS, s_]),
                              L["h_outsb"], TT * n + a + 1)

                def head_scores(n):
                    h = n % HEADS
                    act.wait_ge(L["h_scores"], n + 1)
                    if n > 0:
                        act.wait_ge(L["h_dstate"], 3 * n)
                    for a in range(TT):
                        scale = cols[:, a, 64 + h:65 + h] if n >= HEADS else 1.0
                        ins = act.activation(kn[:, a, :], bank[2][:, (TT + a) * P:(TT + a + 1) * P], ACT.Copy, scale=scale)
                        chain(ins, L["h_keys_sb"], n + 1) if a else chain(ins)
                    if n >= HEADS:
                        act.wait_ge(L["h_dexp_in"], h + 1)
                        chain(act.activation(dexp[:, :], dexp[:, :], ACT.Exp, scale=-1.0), L["h_dexp"], h + 1)

                def head_root(r):
                    act.wait_ge(L["norm_var"], r + 1)
                    chain(act.activation(rstd[:, r, :], ssum[:, r, :], ACT.Sqrt), L["norm_root"], r + 1)

                def read_gate(name, j, a):
                    dst, func = {"g_g": (gg, ACT.Silu), "m_o": (mo, ACT.Sigmoid), "a_gla": (ag, ACT.Sigmoid),
                                 "a_m": (am, ACT.Sigmoid)}[name]
                    read_out((name, j, a), dst[:, a, j * 512:(j + 1) * 512], func)

                def gap(k, p):
                    i = 2 * (k - GAP_BLOCKS[0]) + p // 2
                    if p % 2 == 0:
                        return
                    if 0 <= i - 2 < 2 * HEADS:
                        head_outputs(i - 2)
                    if i < 2 * HEADS:
                        head_scores(i)
                    if i - 2 in (HEADS - 1, 2 * HEADS - 1):
                        head_root((i - 2) // HEADS)

                blocks(GAP_BLOCKS, read_gate, gap)
                turn_hi("gla_t", Bhi, "gla_norm")
                turn_hi("m_t", Hhi, "m_norm")
                blocks(range(16, 20), None)
                turn_hi("merged_t", Bhi, None)

                def memory(k, p):
                    if k > 20:
                        return
                    for c in (2 * p, 2 * p + 1):
                        at = VEC["norm_mem"] + c
                        chain(act.activation(Hhi[:, c, :], memhT[:, c, :], ACT.Copy, scale=vcol[:, at:at + 1]),
                              L["mem_hi"], c + 1)

                blocks(range(20, 22), None, memory)
                def wait_added(name, j):
                    for a in range(TT):
                        wait_moved(act, name, j, a)

                def read_memory(name, j, a):
                    c = 4 * j + 2 * a
                    if name == "x_wk":
                        read_out((name, j, a), kT[:, c:c + 2, :].rearrange("p c s -> p (c s)"), ACT.Copy)
                    else:
                        read_out((name, j, a), gv[:, a, j * 512:(j + 1) * 512], ACT.Copy)

                wait_added("w_out", 0)
                sums(1, 0)
                wait_added("w_out", 1)
                sums(1, 1)

                def norm_between(k, p):
                    if (k, p) == (22, 0):
                        root(1)
                    if (k, p) == (22, 1):
                        second_tile(1)
                    if (k, p) == (24, 0):
                        act.wait_ge(router_in, 16)
                        chain(act.activation(rw_hi[:, :, :], rw[:, :, :], ACT.Copy), L["small_hi"], 2)

                blocks(range(22, 26), read_memory, norm_between)
                turn_hi("x_t", Bhi, "norm_xattn")

                def queries(name, j, a):
                    c = 4 * j + 2 * a
                    read_out((name, j, a), xqT[:, c:c + 2, :].rearrange("p c s -> p (c s)"), ACT.Copy)

                def exps(h):
                    act.wait_ge(L["x_negmax"], h + 1)
                    if h >= 2:
                        act.wait_ge(L["x_pt"], h - 1)
                    for a in range(TT):
                        chain(act.activation(prob[:, h % 2, a, :], bank[4 + h % 2][:, a * M:(a + 1) * M], ACT.Exp,
                                             scale=X_SCALE, bias=nmx[:, h % 2, a:a + 1], accum_out=rsum[:, h % 2, a:a + 1]),
                              L["x_exp"], TT * h + a + 1)

                def turned_prob(h):
                    act.wait_ge(L["x_pt"], h + 1)
                    if h > 0:
                        act.wait_ge(L["x_o"], h)
                    chain(act.activation(probT[:, :, :].rearrange("p m s -> p (m s)"), bank[6][:, :], ACT.Copy),
                          L["x_pt_sb"], h + 1)

                def attended(h):
                    act.wait_ge(L["x_o"], h + 1)
                    chain(act.activation(Hhi[:, 2 * h:2 * h + 2, :].rearrange("p c s -> p (c s)"), bank[7][:, :], ACT.Copy),
                          L["x_o_hi"], h + 1)

                blocks((26,), queries)
                exps(0)
                exps(1)
                blocks((27,), queries)
                turned_prob(0)
                exps(2)
                attended(0)
                turned_prob(1)
                exps(3)
                attended(1)

                def last_heads(k, p):
                    if p == 1:
                        attended(2)
                    if p == 2:
                        attended(3)
                    if p < 2:
                        turned_prob(p + 2)

                blocks((28,), None, last_heads)

                def first_half(k, p):
                    if p == 1:
                        wait_added("x_wo", 0)
                        sums(2, 0)

                blocks((29,), None, first_half)
                wait_added("x_wo", 1)
                sums(2, 1)
                root(2)
                second_tile(2)
                turn_hi("ffn_t", Bhi, "norm_ffn")

                def ff_silu(tiles, w, n):
                    act.wait_ge(L["gate_ps"], n + 1)
                    for a in range(tiles):
                        ins = act.activation(sg[:, a, 0:w], bank[(0, 5)[a]][:, 0:w], ACT.Silu)
                    ins.then_inc(L["silu_done"], 1)

                def ff_hidT(tiles, w, n, half=0):
                    act.wait_ge(L["hid_tr"], n + 1)
                    whole = w // P * P
                    for a in range(tiles):
                        ins = act.activation(hidT[0][:, a + half, 0:whole], bank[(1, 6)[a]][:, 0:whole], ACT.Copy)
                        if w > whole:
                            ins = act.activation(hidT[0][0:w - whole, a, whole:whole + P],
                                                 bank[(1, 6)[a]][0:w - whole, whole:whole + P], ACT.Copy)
                    ins.then_inc(L["hidT_hi"], 1)

                with act.If(l == 0):
                    for f in range(DENSE_BLOCKS):
                        what, i = step_of(f, DENSE_STEPS)
                        w = dense_width(i)
                        for p in range(dense_pieces(f)):
                            wait_piece(act, f, p, DENSE_STEPS)
                            if dense_ahead(f, p) is not None:
                                f_, p_, kind, w_, rows_, arrived = dense_ahead(f, p)
                                wait_full(act, 0, MIX_BLOCKS + f_, arrived)
                                split(MIX_BLOCKS + f_, p_, kind, w_, rows_)
                            if what == "gate" and p == 0 and i > 0:
                                ff_hidT(TT, HB, i - 1)
                        if what == "gate":
                            ff_silu(TT, w, i)
                        if what == "up" and i == DENSE_STEPS - 1:
                            ff_hidT(TT, w, i)
                    act.wait_ge(L["y_done"], 1)
                with act.Else():
                    act.dma_start(gain, t["norm_ffn"][1].rearrange("(o d) -> o d", o=1).broadcast_to([P, D]))\
                        .then_inc(L["gain_in"], 16)
                    act.wait_ge(L["top_e_in"], 1)
                    act.activation(tw[:, :, 0:1], tw[:, :, 0:1], ACT.Exp).then_inc(L["top_e"], 1)
                    act.wait_ge(L["npass_ready"], 1)
                    npass = act.value_load(npass_i[0:1, 0:1], min_val=1, max_val=TT)

                    act.sem_inc(L["y_left"], 1)

                    def gathered(n, tokens, k):
                        act.wait_ge(L["gather_ps"], n + 1)
                        act.activation(tokens[0][:, 4 * k:4 * k + 4, :], bank[5 + k][:, :].rearrange("p (k c) -> p k c", k=4),
                                       ACT.Copy).then_inc(L["gather_hi"], 1)

                    def expert(q, g, next_tokens):
                        def pieces(f, steps=0, after=None):
                            for p in range(PIECES):
                                wait_piece(act, f, p, MOE_STEPS, q * MOE_STEPS, steps)
                                f_, p_ = ahead(f, p)
                                wait_full(act, 1, MIX_BLOCKS + f_, p_, q * MOE_STEPS + steps)
                                split(MIX_BLOCKS + f_, p_, moe_kind(f_))
                                if after is not None:
                                    after(p)

                        def at_piece(n, work):
                            return lambda p: work() if p == n else None

                        def gates_turned():
                            act.wait_ge(L["gated_ps"], q + 1)
                            act.activation(gatedT, bank[7][:, 0:S], ACT.Copy).then_inc(L["gated_sb"], 1)

                        pieces(0)
                        ff_silu(1, HB, q * MOE_STEPS)
                        pieces(1, after=at_piece(2, gates_turned))

                        def step(i, steps):
                            n = q * MOE_STEPS + i
                            pieces(2, steps, at_piece(1, lambda: ff_hidT(1, HB, n - 1)))
                            ff_silu(1, HB, n)
                            pieces(3, steps)
                            pieces(4, steps)

                        step(1, 0)
                        with act.Fori(2, MOE_STEPS - 1) as i:
                            step(i, i - 1)
                        n = q * MOE_STEPS + MOE_STEPS - 1
                        f = MOE_BLOCKS - 4
                        pieces(f, after=at_piece(1, lambda: ff_hidT(1, HB, n - 1)))
                        ff_silu(1, HB, n)
                        pieces(f + 1)
                        pieces(f + 2, after=lambda p: (gathered(g + 1, next_tokens, p // 2) if p % 2 == 0 else
                                                       ff_hidT(1, HB, n, half=1) if p == 1 else None))
                        pieces(f + 3)
                        act.wait_ge(L["y_ps"], (q + 1) * MOE_STEPS)
                        act.activation(yacc[:, 0:512], bank[3][:, :], ACT.Copy).then_inc(L["y_left"], 1)
                        act.activation(yacc[:, 512:1024], bank[4][:, :], ACT.Copy).then_inc(L["y_right"], 1)

                    with act.Fori(0, npass) as ps_:
                        for k in range(2):
                            gathered(ps_ * (NE + 1), hg[0], k)
                        with act.Fori(0, NE // 2) as pair:
                            for r in range(2):
                                e = 2 * pair + r
                                expert(ps_ * NE + e, ps_ * (NE + 1) + e, hg[1 - r])
                act.nop()
                layer_end(act, l)
            for a in range(TT):
                act.activation(gv[:, a, :], x[:, a, :], ACT.Square, accum_out=ssum2[:, a:a + 1]).then_inc(fin_sq, 1)
            act.wait_ge(fin_var, 1)
            act.activation(rstd2[:, :], ssum2[:, :], ACT.Sqrt).then_inc(fin_root, 1)
            act.dma_start(junk[:, :], t["norm_final"].rearrange("(o d) -> o d", o=1).broadcast_to([P, D])).then_inc(last_in, 16)

        @block.vector
        def _(dve):
            step = Steps(dve, dve_own)

            def op(ins, sem=None, value=None):
                step.did(ins, sem, value)
                step.wait()

            dve.wait_ge(mem_sq, 2)
            dve.tensor_scalar(ssum2[:, :], ssum2[:, :], 1.0 / D, EPS, ALU.mult, ALU.add).then_inc(mem_var, 1)
            dve.wait_ge(mem_root, 1)
            dve.reciprocal(rstd2[:, :], rstd2[:, :]).then_inc(mem_var, 1)
            dve.wait_ge(mem_var, 2)
            for a in range(TT):
                dve.tensor_scalar(gg[:, a, :], xn[:, a, :], rstd2[:, a:a + 1], None, ALU.mult).then_inc(mem_n, 1)
            dve.wait_ge(const_ready, CONSTS)
            for j in range(4):
                dve.wait_ge(mem_tp, j + 1)
                dve.tensor_copy(memhT[:, 2 * j:2 * j + 2, :].rearrange("p k s -> p (k s)"), bank[j][:, :]).then_inc(mem_ready, 1)
            dve.wait_ge(mem_ready, 4)
            dve.wait_ge(x_in, 16)

            with dve.Fori(0, DEPTH) as l:
                step.n, step.last = 0, None

                def norm_var(n):
                    dve.wait_ge(L["sq_done"], 2 * TT * (n + 1))
                    op(dve.tensor_tensor(ssum2[:, :], ssq[:, 0, :], ssq[:, 1, :], ALU.add))
                    op(dve.tensor_scalar(ssum2[:, :], ssum2[:, :], 1.0 / D, EPS, ALU.mult, ALU.add), L["var_done"], n + 1)

                def first_tile(n):
                    dve.wait_ge(L["root_done"], n + 1)
                    op(dve.reciprocal(rstd2[:, :], rstd2[:, :]), L["inverse_done"], n + 1)
                    op(dve.tensor_scalar(xn[:, 0, :], x[:, 0, :], rstd2[:, 0:1], None, ALU.mult), L["xn_ready"], n + 1)

                def norm(n):
                    norm_var(n)
                    first_tile(n)

                def turn_lo(name, pair, gain_name):
                    for j in range(4):
                        n, ps = turn_no(name, j)
                        dve.wait_ge(L["turn_hi"], n + 1)
                        for k in range(2):
                            c = 2 * j + k
                            if gain_name:
                                ins = dve.scalar_tensor_tensor(pair[1][:, c, :], ps[:, k * S:(k + 1) * S],
                                                               vcol[:, VEC[gain_name] + c:VEC[gain_name] + c + 1],
                                                               pair[0][:, c, :].bitcast(F32), ALU.mult, ALU.subtract)
                            else:
                                ins = dve.tensor_tensor(pair[1][:, c, :], ps[:, k * S:(k + 1) * S],
                                                        pair[0][:, c, :].bitcast(F32), ALU.subtract)
                            op(ins, L["turn_lo"], n + 1) if k else op(ins)

                def split(k, p, kind, w=512, rows=P):
                    dve.tensor_tensor(split_piece(wlo, k, p, kind, w)[0:rows], raw_piece(k, p, kind, w)[0:rows],
                                      split_piece(whi, k, p, kind, w)[0:rows].bitcast(F32), ALU.subtract).then_inc(lo_done, 1)

                def split_ahead(k, p):
                    k, p = ahead(k, p)
                    dve.wait_ge(hi_done, PIECES * k + p + 1)
                    split(k, p, kind_of(k))

                def blocks(numbers, read=None, between=None):
                    for k in numbers:
                        name, j = BLOCKS[k]
                        for p in range(PIECES):
                            if read is not None and ends_group(k, p) is not None:
                                for a in ((p // 2,) if is_columns(k) else range(TT)):
                                    read(name, j, a)
                            split_ahead(k, p)
                            if between is not None:
                                between(k, p)

                H, B = (Hhi, Hlo), (Bhi, Blo)
                wait_group(dve, "vec", 0)
                op(dve.tensor_copy(vcol[:, :], bank[GROUPS[("vec", 0)] % GROUP_BANKS][:, 0:NVEC]), moved[0], 1)
                norm(0)
                dve.wait_ge(L["small_hi"], 1)
                dve.tensor_tensor(wsmall_lo[:, :, :], wsmall[:, :, :], wsmall_hi[:, :, :].bitcast(F32), ALU.subtract)\
                    .then_inc(L["small_lo"], 1)
                turn_lo("mix_t", H, "norm_mix")
                for p in range(SPLIT):
                    dve.wait_ge(hi_done, p + 1)
                    split(0, p, kind_of(0))
                ps, mv_, v = group("small", 1)
                wait_group(dve, "small", 1)
                op(dve.tensor_scalar(grow[:, 1, :], ps[0:HEADS, 0:S], gbias[:, 1:2], None, ALU.add), mv_, v)
                op(dve.scalar_tensor_tensor(grow[:, 2, :], grow[:, 1, :], -1.0, grow[:, 1, :], ALU.mult, ALU.max), L["gate_z"], 1)

                def decay_input():
                    for a in range(2):
                        ps, mv_, v = group("decay", a)
                        wait_group(dve, "decay", a)
                        for c in range(2):
                            h = 2 * a + c
                            ins = dve.tensor_scalar(cum[:, h, :], ps[:, c * S:(c + 1) * S],
                                                    vcol[:, VEC["gla_gk_bias"] + h:VEC["gla_gk_bias"] + h + 1], None, ALU.add)
                            op(ins, mv_, v) if c else op(ins)
                    op(dve.scalar_tensor_tensor(e1[:, :, :].rearrange(flat), cum[:, :, :].rearrange(flat), -1.0,
                                                cum[:, :, :].rearrange(flat), ALU.mult, ALU.max), L["decay_z"], 1)

                def row_chunk(c):
                    s_ = slice(c * CH, (c + 1) * CH)
                    e_ = slice((c + 1) * CH - 1, (c + 1) * CH)
                    op(dve.tensor_tensor_scan(mrow[:, s_], zrow[:, :], grow[:, 1, s_], mst[:, c:c + 1], ALU.add, ALU.max))
                    op(dve.tensor_scalar(grow[:, 4, s_], mrow[:, s_], mst[:, c:c + 1], None, ALU.subtract))
                    op(dve.tensor_scalar(rows[64:64 + HEADS, s_], grow[:, 1, s_], mrow[:, e_], None, ALU.subtract))
                    op(dve.tensor_tensor(mst[:, c + 1:c + 2], grow[:, 3, e_], mrow[:, e_], ALU.add))

                def convolve(c):
                    if c % 2 == 0:
                        wait_moved(dve, "m_q" if c < 4 else "m_k", 0, c % 4 // 2)

                    def tap(j):
                        at = VEC["m_conv"] + j * KC + c
                        return vcol[:, at:at + 1]

                    op(dve.tensor_scalar(qk[:, c, :], cin[:, c, 0:S], tap(0), None, ALU.mult))
                    for j in range(1, CONV_W):
                        ins = dve.scalar_tensor_tensor(qk[:, c, :], cin[:, c, j:j + S], tap(j), qk[:, c, :],
                                                       ALU.mult, ALU.add)
                        op(ins, L["conv_out"], 1) if c == KC - 1 and j == CONV_W - 1 else op(ins)

                flat = "p h s -> p (h s)"

                def front(k, p):
                    at = PIECES * k + p
                    if (k, p) == (1, 3):
                        decay_input()
                    if (k, p) == (2, 0):
                        dve.wait_ge(L["decay_e"], 1)
                        op(dve.scalar_tensor_tensor(cum[:, :, :].rearrange(flat), cum[:, :, :].rearrange(flat), 0.0,
                                                    e1[:, :, :].rearrange(flat), ALU.min, ALU.subtract))
                    if (k, p) == (2, 1):
                        op(dve.tensor_scalar(cum[:, :, :], cum[:, :, :], 1.0 / GATE_NORM, LOG_DECAY_MIN, ALU.mult, ALU.max))
                    if (k, p) == (2, 2):
                        for h in range(HEADS):
                            ins = dve.tensor_tensor_scan(gkeT[:, h, :], restart[:, :], cum[:, h, :], 0.0, ALU.mult, ALU.add)
                            op(ins, L["cum_ready"], 1) if h == HEADS - 1 else op(ins)
                    if (k, p) == (2, 3):
                        dve.wait_ge(L["row_ln"], 1)
                        op(dve.scalar_tensor_tensor(grow[:, 1, :], grow[:, 1, :], 0.0, grow[:, 2, :], ALU.min, ALU.subtract))
                        op(dve.tensor_tensor_scan(grow[:, 3, :], restart[0:HEADS, :], grow[:, 1, :], 0.0, ALU.mult, ALU.add))
                        wait_moved(dve, "small", 0)
                        op(dve.scalar_tensor_tensor(grow[:, 1, :], grow[:, 0, :], gbias[:, 0:1], grow[:, 3, :],
                                                    ALU.add, ALU.subtract))
                        op(dve.tensor_copy(rows[0:HEADS, :], grow[:, 1, :]))
                    if k == 3:
                        row_chunk(p)
                    if (k, p) == (3, 3):
                        op(dve.tensor_tensor(rows[96:96 + HEADS, :], grow[:, 3, :], mrow[:, 0:S], ALU.add), L["row_dm"], 1)
                    if (k, p) == (4, 0):
                        dve.wait_ge(L["e_ready"], 1)
                        for a in range(2):
                            wait_moved(dve, "g_q", 0, a)
                            wait_moved(dve, "g_k", 0, a)
                        op(dve.scalar_tensor_tensor(gqT[:, :, :].rearrange(flat), gqT[:, :, :].rearrange(flat), QK_SCALE,
                                                    e1[:, :, :].rearrange(flat), ALU.mult, ALU.mult))
                    if (k, p) == (4, 1):
                        op(dve.tensor_tensor(gkT[:, :, :], gkT[:, :, :], cum[:, :, :], ALU.mult))
                    if (k, p) == (4, 2):
                        ends = e1[:, :, CH - 1:S:CH].unsqueeze(3).broadcast_to([P, HEADS, NCH, CH])
                        for h in range(HEADS):
                            ins = dve.tensor_tensor(gkeT[:, h, :].rearrange("p (c s) -> p c s", s=CH),
                                                    gkT[:, h, :].rearrange("p (c s) -> p c s", s=CH), ends[:, h], ALU.mult)
                            op(ins, L["gla_in"], 1) if h == HEADS - 1 else op(ins)
                    first = PIECES * 4 + 3
                    if first <= at < first + KC:
                        convolve(at - first)

                blocks(range(8), between=front)
                ps, mv_, v = group("gate_cols", 0)
                wait_group(dve, "gate_cols", 0)
                op(dve.tensor_copy(cols[:, :, :].rearrange("p a c -> p (a c)"), ps[:, 0:TT * P]), mv_, v)

                def head_outputs(n):
                    h = n - HEADS
                    for a in range(TT):
                        dve.wait_ge(L["h_out"], TT * n + a + 1)
                        if h > 0:
                            dve.wait_ge(L["h_outsb"], TT * (n - 1) + a + 1)
                        op(dve.scalar_tensor_tensor(den[:, a:a + 1], bank[6 + a][:, DV:DV + 1], -1.0,
                                                    cols[:, a, 96 + h:97 + h], ALU.mult, ALU.max))
                        op(dve.tensor_tensor(den[:, a:a + 1], den[:, a:a + 1], bank[6 + a][:, DV:DV + 1], ALU.max))
                        op(dve.reciprocal(den[:, a:a + 1], den[:, a:a + 1]), L["h_den"], TT * h + a + 1)

                def head_states(n):
                    h = n % HEADS
                    width = DV if n < HEADS else DV + 1
                    if n > 0:
                        dve.wait_ge(L["h_out"], TT * n)
                    for c in range(NCH - 1):
                        dve.wait_ge(L["h_dstate"], 3 * n + c + 1)
                        decay = e1[:, h, (c + 1) * CH - 1:(c + 1) * CH] if n < HEADS else sdec[:, h, c:c + 1]
                        inc = bank[(5, 3)[c % 2]][:, 0:width]
                        if c == 0:
                            ins = dve.tensor_copy(st[:, 0, 0:width], inc)
                        else:
                            ins = dve.scalar_tensor_tensor(st[:, c, 0:width], st[:, c - 1, 0:width], decay, inc,
                                                           ALU.mult, ALU.add)
                        op(ins, L["h_state"], 3 * n + c + 1)

                def head_scores(n):
                    h = n % HEADS
                    if n > 1:
                        dve.wait_ge(L["h_out"], TT * (n - 1))
                    if n < HEADS:
                        dve.wait_ge(L["h_scores"], n + 1)
                        dve.wait_ge(L["h_keys_sb"], n + 1)
                        op(dve.copy_predicated(sT[:, n % 2, :], causal[:, :].bitcast(U32), bank[2][:, 0:TT * P]),
                           L["h_masked"], n + 1)
                        return
                    dve.wait_ge(L["h_bcast"], h + 1)
                    for a in range(TT):
                        ins = dve.scalar_tensor_tensor(dexp[:, a * P:(a + 1) * P], bank[3][:, a * P:(a + 1) * P],
                                                       cols[:, a, h:h + 1], hide[:, a * P:(a + 1) * P], ALU.subtract, ALU.max)
                        op(ins, L["h_dexp_in"], h + 1) if a else op(ins)
                    op(dve.tensor_copy(sdec[:, h, :], bank[3][:, S:S + NCH]))
                    if h == 0:
                        dve.wait_ge(L["qk_ready"], 1)
                    op(dve.tensor_tensor(qs[:, n % 2, :], qk[:, h, :], bank[4][:, 0:S], ALU.mult), L["h_qs"], h + 1)
                    dve.wait_ge(L["h_dexp"], h + 1)
                    dve.wait_ge(L["h_keys_sb"], n + 1)
                    op(dve.scalar_tensor_tensor(wT[:, n % 2, :], bank[2][:, 0:TT * P], QK_SCALE, dexp[:, :], ALU.mult, ALU.mult),
                       L["h_masked"], n + 1)

                def head_norm(r, part):
                    o, gate, gate_name, done = ((xn, gg, "g_g", "gated_g"), (om, mo, "m_o", "gated_m"))[r]
                    if part == 0:
                        dve.wait_ge(L["h_outsb"], TT * HEADS * (r + 1))
                        op(dve.tensor_scalar(ssum[:, r, :], ssum[:, r, :], 1.0 / DV, EPS, ALU.mult, ALU.add),
                           L["norm_var"], r + 1)
                        return
                    if part == 1:
                        for j in range(2):
                            for a in range(TT):
                                wait_moved(dve, gate_name, j, a)
                        dve.wait_ge(L["norm_root"], r + 1)
                        op(dve.reciprocal(rstd[:, r, :], rstd[:, r, :]))
                    a = part - 1
                    for h in range(HEADS):
                        i = a * HEADS + h
                        op(dve.scalar_tensor_tensor(o[:, a, h * DV:(h + 1) * DV], o[:, a, h * DV:(h + 1) * DV],
                                                    rstd[:, r, i:i + 1], gate[:, a, h * DV:(h + 1) * DV], ALU.mult, ALU.mult),
                           L[done], i + 1)

                def gap(k, p):
                    i = 2 * (k - GAP_BLOCKS[0]) + p // 2
                    if p % 2 == 0:
                        return
                    if HEADS <= i - 2 < 2 * HEADS:
                        head_outputs(i - 2)
                    if 0 <= i - 1 < 2 * HEADS:
                        head_states(i - 1)
                    if i < 2 * HEADS:
                        head_scores(i)
                    for r in range(2):
                        if 0 <= i - 2 - (HEADS * (r + 1) - 1) <= TT:
                            head_norm(r, i - 2 - (HEADS * (r + 1) - 1))

                blocks(GAP_BLOCKS, between=gap)

                turn_lo("gla_t", B, "gla_norm")
                turn_lo("m_t", H, "m_norm")

                def read_branch(name, j, a):
                    c = slice(j * 512, (j + 1) * 512)
                    ps, mv_, v = group(name, j, a)
                    wait_group(dve, name, j, a)
                    if name == "gla_proj":
                        op(dve.tensor_tensor(ag[:, a, c], ag[:, a, c], ps[:, :], ALU.mult), mv_, v)
                    else:
                        op(dve.tensor_tensor(am[:, a, c], am[:, a, c], ps[:, :], ALU.mult))
                        op(dve.tensor_tensor(ag[:, a, c], ag[:, a, c], am[:, a, c], ALU.add), mv_, v)

                blocks(range(16, 20), read_branch)
                turn_lo("merged_t", B, None)

                def add_to_x(name, j, a):
                    c = slice(j * 512, (j + 1) * 512)
                    ps, mv_, v = group(name, j, a)
                    wait_group(dve, name, j, a)
                    op(dve.tensor_tensor(x[:, a, c], x[:, a, c], ps[:, :], ALU.add), mv_, v)

                def memory(k, p):
                    if k > 20:
                        return
                    for c in (2 * p, 2 * p + 1):
                        at = VEC["norm_mem"] + c
                        dve.wait_ge(L["mem_hi"], c + 1)
                        op(dve.scalar_tensor_tensor(Hlo[:, c, :], memhT[:, c, :], vcol[:, at:at + 1],
                                                    Hhi[:, c, :].bitcast(F32), ALU.mult, ALU.subtract), L["mem_t"], c + 1)

                blocks(range(20, 22), add_to_x, memory)

                def norm_between(k, p):
                    if (k, p) == (22, 0):
                        norm_var(1)
                    if (k, p) == (22, 1):
                        first_tile(1)
                    if (k, p) == (24, 0):
                        dve.wait_ge(L["small_hi"], 2)
                        op(dve.tensor_tensor(rw_lo[:, :, :], rw[:, :, :], rw_hi[:, :, :].bitcast(F32), ALU.subtract),
                           L["small_lo"], 2)

                blocks(range(22, 26), between=norm_between)
                turn_lo("x_t", B, "norm_xattn")

                def negated_max(h):
                    dve.wait_ge(L["x_score"], h + 1)
                    op(dve.tensor_reduce(mx[:, :], bank[4 + h % 2][:, :].rearrange("p (a m) -> p a m", a=TT), axis=AX.X, op=ALU.max))
                    op(dve.tensor_scalar(nmx[:, h % 2, :], mx[:, :], -X_SCALE, None, ALU.mult), L["x_negmax"], h + 1)

                def normalise(h):
                    dve.wait_ge(L["x_exp"], TT * (h + 1))
                    op(dve.reciprocal(rinv[:, :], rsum[:, h % 2, :]))
                    for a in range(TT):
                        ins = dve.tensor_scalar(prob[:, h % 2, a, :], prob[:, h % 2, a, :], rinv[:, a:a + 1], None, ALU.mult)
                        op(ins, L["x_prob"], h + 1) if a else op(ins)

                def attended(h):
                    dve.wait_ge(L["x_o"], h + 1)
                    dve.wait_ge(L["x_o_hi"], h + 1)
                    c = slice(2 * h, 2 * h + 2)
                    op(dve.tensor_tensor(Hlo[:, c, :].rearrange("p c s -> p (c s)"), bank[7][:, :],
                                         Hhi[:, c, :].rearrange("p c s -> p (c s)").bitcast(F32), ALU.subtract),
                       L["x_o_sb"], h + 1)

                def between_heads(k, p):
                    if (k, p) == (26, 3):
                        negated_max(0)
                        negated_max(1)
                    if k == 27 and p < 2:
                        normalise(p)

                blocks((26, 27), between=between_heads)
                negated_max(2)
                attended(0)
                negated_max(3)
                attended(1)
                normalise(2)
                normalise(3)
                blocks((28, 29), add_to_x, lambda k, p: attended(p + 1) if k == 28 and p in (1, 2) else None)
                norm(2)
                turn_lo("ffn_t", B, "norm_ffn")

                def ff_hid(tiles, w, n):
                    dve.wait_ge(L["silu_done"], n + 1)
                    dve.wait_ge(L["up_ps"], n + 1)
                    for a in range(tiles):
                        ins = dve.tensor_tensor(hid[:, a, 0:w], sg[:, a, 0:w], bank[(1, 6)[a]][:, 0:w], ALU.mult)
                    ins.then_inc(L["hid_ready"], 1)

                def ff_hidT(tiles, w, n, half=0):
                    dve.wait_ge(L["hidT_hi"], n + 1)
                    whole = w // P * P
                    for a in range(tiles):
                        ins = dve.tensor_tensor(hidT[1][:, a + half, 0:whole], bank[(1, 6)[a]][:, 0:whole],
                                                hidT[0][:, a + half, 0:whole].bitcast(F32), ALU.subtract)
                        if w > whole:
                            r = slice(0, w - whole)
                            ins = dve.tensor_tensor(hidT[1][r, a, whole:whole + P], bank[(1, 6)[a]][r, whole:whole + P],
                                                    hidT[0][r, a, whole:whole + P].bitcast(F32), ALU.subtract)
                    ins.then_inc(L["hidT_ready"], 1)

                with dve.If(l == 0):
                    for f in range(DENSE_BLOCKS):
                        what, i = step_of(f, DENSE_STEPS)
                        for p in range(dense_pieces(f)):
                            if what == "up" and p == PIECES - 1:
                                ff_hid(TT, dense_width(i), i)
                            if dense_ahead(f, p) is not None:
                                f_, p_, kind, w_, rows_, _ = dense_ahead(f, p)
                                wait_lo(dve, f_, p_)
                                split(MIX_BLOCKS + f_, p_, kind, w_, rows_)
                            if what == "gate" and p == 0 and i > 0:
                                ff_hidT(TT, HB, i - 1)
                        if what == "up" and i == DENSE_STEPS - 1:
                            ff_hidT(TT, dense_width(i), i)
                    dve.wait_ge(L["y_ps"], DENSE_STEPS)
                    for a in range(TT):
                        for c in range(2):
                            s_ = slice(c * 512, (c + 1) * 512)
                            ins = dve.tensor_tensor(x[:, a, s_], x[:, a, s_], bank[((3, 4), (2, 7))[a][c]][:, :], ALU.add)
                    ins.then_inc(L["y_done"], 1)
                    dve.wait_ge(L["y_done"], 1)
                with dve.Else():
                    for v in (place, chosen, gates):
                        op(dve.memset(v[:, :, NE:NE + 1], 0.0))
                    op(dve.memset(yacc, 0.0))
                    op(dve.memset(gatedT, 0.0))
                    dve.wait_ge(L["gain_in"], 16)
                    dve.wait_ge(L["turn_ps"], 4 * len(TURNS))
                    dve.wait_ge(L["xn_second"], 3)
                    op(dve.tensor_tensor(xn[:, 0, :], xn[:, 0, :], gain, ALU.mult))
                    dve.wait_ge(L["logit_ps"], 1)
                    op(dve.tensor_copy(logitT[:, :], bank[4][0:NE, 0:S]), L["logitT_sb"], 1)
                    dve.wait_ge(L["logit_ps"], 2)
                    op(dve.tensor_copy(logit[:, :, :].rearrange("p a e -> p (a e)"), bank[3][:, 0:TT * NE]))
                    for a in range(TT):
                        op(dve.max(top[:, a, :], logit[:, a, :]))
                    op(dve.tensor_tensor(tw[:, :, 0:1], top[:, :, 1:2], top[:, :, 0:1], ALU.subtract), L["top_e_in"], 1)
                    for a in range(TT):
                        op(dve.max_index(topi[:, a, :], top[:, a, :], logit[:, a, :]))
                    op(dve.tensor_copy(topf[:, :, :], topi[:, :, :]))
                    for a in range(TT):
                        for r in range(2):
                            op(dve.tensor_scalar(oh[:, a, r, :], expert_no[:, :], topf[:, a, r:r + 1], None, ALU.is_equal))
                    op(dve.tensor_tensor(chosen[:, :, 0:NE], oh[:, :, 0, :], oh[:, :, 1, :], ALU.add), L["count_in"], 1)
                    op(dve.tensor_tensor(xn[:, 1, :], xn[:, 1, :], gain, ALU.mult))
                    dve.wait_ge(L["top_e"], 1)
                    op(dve.tensor_scalar(tw[:, :, 1:2], tw[:, :, 0:1], 1.0, None, ALU.add))
                    op(dve.reciprocal(tw[:, :, 2:3], tw[:, :, 1:2]))
                    op(dve.tensor_tensor(tw[:, :, 3:4], tw[:, :, 0:1], tw[:, :, 2:3], ALU.mult))
                    for a in range(TT):
                        op(dve.tensor_scalar(oh[:, a, 0, :], oh[:, a, 0, :], tw[:, a, 2:3], None, ALU.mult))
                        op(dve.scalar_tensor_tensor(gates[:, a, 0:NE], oh[:, a, 1, :], tw[:, a, 3:4], oh[:, a, 0, :],
                                                    ALU.mult, ALU.add))
                    dve.wait_ge(L["count_ps"], 1)
                    op(dve.tensor_copy(place[:, :, 0:NE], bank[5][:, 0:TT * NE].rearrange("p (a e) -> p a e", a=TT)))
                    op(dve.tensor_reduce(most, bank[5][:, TT * NE:(TT + 1) * NE], axis=AX.X, op=ALU.max))
                    op(dve.tensor_scalar(npass_i[:, :], most, float(P), 1.0, ALU.is_gt, ALU.add), L["npass_ready"], 1)
                    npass = dve.value_load(npass_i[0:1, 0:1], min_val=1, max_val=TT)
                    dve.sem_inc(L["y_right"], 1)
                    dve.sem_inc(L["gated_sb"], 1)

                    def prepare(e, n, part):
                        if part > 0:
                            dve.wait_ge(dve_q, n * Q_STEPS + part * TT)
                        for a in range(TT):
                            if part == 0:
                                col = bass.ds(e, 1)
                                dve.tensor_copy(place_p[:, a, 0:1], place[:, a, col])
                                dve.tensor_copy(place_p[:, a, 1:2], chosen[:, a, col])
                                ins = dve.tensor_copy(place_p[:, a, 2:3], gates[:, a, col])
                            elif part == 1:
                                ins = dve.tensor_scalar(onehot[:, a, :], slot_no[:, :], place_p[:, a, 0:1],
                                                        place_p[:, a, 1:2], ALU.is_equal, ALU.mult)
                            else:
                                ins = dve.tensor_scalar(gated[:, a, :], onehot[:, a, :], place_p[:, a, 2:3], None, ALU.mult)
                            ins.then_inc(dve_q, 1)
                        if part == 2:
                            dve.wait_ge(dve_q, n * Q_STEPS + 3 * TT)
                            dve.sem_inc(L["onehot_ready"], 1)

                    def gathered(n, tokens, k):
                        dve.wait_ge(L["gather_hi"], n * 2 + (k + 1))
                        c = slice(4 * k, 4 * k + 4)
                        ins = dve.tensor_tensor(tokens[1][:, c, :], bank[5 + k][:, :].rearrange("p (k c) -> p k c", k=4),
                                                tokens[0][:, c, :].bitcast(F32), ALU.subtract)
                        if k == 1:
                            ins.then_inc(L["gather_sb"], 1)

                    def scattered(n, part):
                        dve.wait_ge(L["scatter_ps"], n * 4 + (part + 1))
                        a, s_ = part // 2, slice(part % 2 * 512, (part % 2 + 1) * 512)
                        ins = dve.tensor_tensor(x[:, a, s_], x[:, a, s_], bank[(5, 6, 7, 2)[part]][:, :], ALU.add)
                        if part == 3:
                            ins.then_inc(L["scattered"], 1)

                    def expert(q, g, e, next_tokens):
                        def pieces(f, steps=0, before=None, after=None):
                            for p in range(PIECES):
                                if p == PIECES - 1 and before is not None:
                                    before()
                                f_, p_ = ahead(f, p)
                                wait_lo(dve, f_, p_, (q * MOE_STEPS + steps) * (3 * PIECES))
                                split(MIX_BLOCKS + f_, p_, moe_kind(f_))
                                if after is not None:
                                    after(p)

                        def at_piece(n, work):
                            return lambda p: work() if p == n else None

                        def step(i, steps, between=None):
                            n = q * MOE_STEPS + i
                            pieces(2, steps, after=at_piece(1, lambda: ff_hidT(1, HB, n - 1)))
                            pieces(3, steps, after=between)
                            pieces(4, steps, before=lambda: ff_hid(1, HB, n))

                        pieces(0, after=lambda p: scattered(q, p - 1) if p > 0 else None)
                        pieces(1, before=lambda: ff_hid(1, HB, q * MOE_STEPS), after=at_piece(0, lambda: scattered(q, 3)))
                        def prepare_next(p):
                            if p == 0:
                                dve.wait_ge(L["gather_ps"], g + 1)
                                dve.wait_ge(L["gated_ps"], q + 1)
                            if p < 3:
                                prepare(e + 1, g + 1, p)

                        step(1, 0, prepare_next)
                        with dve.Fori(2, MOE_STEPS - 1) as i:
                            step(i, i - 1)
                        n = q * MOE_STEPS + MOE_STEPS - 1
                        f = MOE_BLOCKS - 4
                        dve.wait_ge(L["scattered"], q + 1)
                        pieces(f, after=at_piece(1, lambda: ff_hidT(1, HB, n - 1)))
                        pieces(f + 1, before=lambda: ff_hid(1, HB, n))
                        pieces(f + 2, after=lambda p: (gathered(g + 1, next_tokens, p // 2) if p % 2 == 0 else
                                                       ff_hidT(1, HB, n, half=1) if p == 1 else None))
                        pieces(f + 3)

                    with dve.Fori(0, npass) as ps_:
                        for part in range(3):
                            prepare(0, ps_ * (NE + 1), part)
                        for k in range(2):
                            gathered(ps_ * (NE + 1), hg[0], k)
                        with dve.Fori(0, NE // 2) as pair:
                            for r in range(2):
                                e = 2 * pair + r
                                expert(ps_ * NE + e, ps_ * (NE + 1) + e, e, hg[1 - r])
                        dve.wait_ge(L["gather_ps"], (ps_ + 1) * (NE + 1))
                        dve.tensor_scalar(place[:, :, :], place[:, :, :], -float(P), None, ALU.add).then_inc(dve_p, 1)
                        dve.wait_ge(dve_p, ps_ + 1)
                    for part in range(4):
                        scattered(npass * NE, part)
                dve.nop()
                layer_end(dve, l)
            dve.wait_ge(fin_sq, 2)
            dve.tensor_scalar(ssum2[:, :], ssum2[:, :], 1.0 / D, EPS, ALU.mult, ALU.add).then_inc(fin_var, 1)
            dve.wait_ge(fin_root, 1)
            dve.reciprocal(rstd2[:, :], rstd2[:, :]).then_inc(fin_var, 1)
            dve.wait_ge(fin_var, 2)
            dve.wait_ge(last_in, 16)
            for a in range(TT):
                dve.scalar_tensor_tensor(xn[:, a, :], x[:, a, :], rstd2[:, a:a + 1], junk[:, :], ALU.mult, ALU.mult)\
                    .then_inc(fin_out, 1)


_INS = ["x", "mem", "norm_mix", "w_in", "gla_gk_up", "gla_gk_bias", "gla_norm", "m_conv", "m_gate_bias", "m_norm",
        "gla_proj", "m_proj", "w_out", "norm_xattn", "norm_mem", "x_wq", "x_wkv", "x_wo", "norm_ffn",
        "ffn_w13", "ffn_w2", "moe_router", "moe_w13", "moe_w2", "norm_final"]


def kernel(**inputs):
    import numpy as _np
    import concourse.bacc as _bacc
    from concourse import mybir as _mybir
    from concourse.bass_utils import run_bass_kernel_spmd as _run

    nc = _bacc.Bacc("TRN2", target_bir_lowering=False, num_devices=1)
    arrays, tensors = {}, {}
    for name in _INS:
        a = _np.ascontiguousarray(inputs[name])
        arrays[f"in_{name}_dram"] = a
        tensors[name] = nc.dram_tensor(f"in_{name}_dram", a.shape, _mybir.dt.from_np(a.dtype), kind="ExternalInput").ap()
    out = nc.dram_tensor("out_0_dram", (1, S, D), F32, kind="ExternalOutput").ap()
    hybrid_decoder_kernel(nc, tensors, out)
    r = _run(nc, [arrays], core_ids=[0])
    return r.results[0]["out_0_dram"]
```
